# Optimizing a Trainium2 kernel written in Bass

```python
import math, functools
import jax, jax.numpy as jnp
from jax import lax
import numpy as np

D_MODEL = 1024
BATCH = 1
SEQ = 128
DEPTH = 1
DEC_BATCH = 1
DEC_SEQ = 512
PAST_LEN = 128

GRID_W = 64
H_ATT = 8
HEAD_DIM = 64
D_ATT = H_ATT * HEAD_DIM
D_HYENA = 512
D_MIX = D_ATT + D_HYENA
D_IN = 3 * D_ATT + 3 * D_HYENA
NA_ROWS = 8
NA_COLS = 16
Q_BLOCK = 128
SHORT_CONV = 3
FILTER_BANDS = 16
EMB_DIM = 1 + 2 * FILTER_BANDS
FILTER_FF = 64
DECAY_TARGET = 1e-2
FAST_DECAY_PCT = 0.3
SLOW_DECAY_PCT = 1.5
MIN_DECAY = math.log(DECAY_TARGET) / SLOW_DECAY_PCT
MAX_DECAY = math.log(DECAY_TARGET) / FAST_DECAY_PCT
N_GROUPS = 4
EXPERTS_PER_GROUP = 4
N_EXPERTS = N_GROUPS * EXPERTS_PER_GROUP
TOP_K = 2
D_EXPERT = 512
N_MOD = 6
EPS = 1e-6
NEG_INF = -1e30

kernel_name = "hybrid_na_hyena_hmoe_diffusion_step"

f32 = jnp.float32

def rms_norm(x, g):
    xf = x.astype(f32)
    y = xf * lax.rsqrt(jnp.mean(xf * xf, axis=-1, keepdims=True) + EPS)
    return (y * g.astype(f32)).astype(x.dtype)

def ada_mod(cond, w, b):
    m = jax.nn.silu(cond) @ w + b
    m = m.reshape(cond.shape[0], N_MOD, 1, D_MODEL)
    return tuple(m[:, i] for i in range(N_MOD))

def split_projection(proj):
    B, L, _ = proj.shape
    q, k, v, hy = jnp.split(proj, [D_ATT, 2 * D_ATT, 3 * D_ATT], axis=-1)
    shp = (B, L, H_ATT, HEAD_DIM)
    return q.reshape(shp), k.reshape(shp), v.reshape(shp), hy

def context_attention(q, k, v):
    B, S, H, Dh = q.shape
    nb = S // Q_BLOCK
    qb = (q * (Dh ** -0.5)).reshape(B, nb, Q_BLOCK, H, Dh).transpose(1, 0, 2, 3, 4)

    def block(qi):
        s = jnp.einsum('bqhd,bkhd->bhqk', qi, k).astype(f32)
        p = jax.nn.softmax(s, axis=-1).astype(v.dtype)
        return jnp.einsum('bhqk,bkhd->bqhd', p, v)

    o = lax.map(block, qb)
    return o.transpose(1, 0, 2, 3, 4).reshape(B, S, H * Dh)

def neighbourhood_attention(q, k, v, k_ctx, v_ctx, rpb):
    B, L, H, Dh = q.shape
    rows = L // GRID_W
    kh = min(NA_ROWS, rows)
    r = np.arange(rows)
    rs = np.clip(r - kh // 2, 0, rows - kh)
    row_idx = rs[:, None] + np.arange(kh)[None, :]
    col = np.arange(GRID_W)
    cs = np.clip(col - NA_COLS // 2, 0, GRID_W - NA_COLS)
    col_mask = (col[None, :] >= cs[:, None]) & (col[None, :] < cs[:, None] + NA_COLS)
    dr = row_idx - r[:, None] + NA_ROWS - 1
    dc = np.clip(col[None, :] - col[:, None] + NA_COLS - 1, 0, 2 * NA_COLS - 2)

    qg = (q * (Dh ** -0.5)).reshape(B, rows, GRID_W, H, Dh)
    kg = k.reshape(B, rows, GRID_W, H, Dh)[:, row_idx]
    vg = v.reshape(B, rows, GRID_W, H, Dh)[:, row_idx]
    s_lat = jnp.einsum('brqhd,brkwhd->bhrqkw', qg, kg).astype(f32)
    bias = rpb[:, dr[:, None, :, None], dc[None, :, None, :]].astype(f32)
    s_lat = jnp.where(col_mask[:, None, :], s_lat + bias[None], NEG_INF)
    s_ctx = jnp.einsum('brqhd,bchd->bhrqc', qg, k_ctx).astype(f32)
    nk = kh * GRID_W
    s = jnp.concatenate([s_lat.reshape(B, H, rows, GRID_W, nk), s_ctx], axis=-1)
    p = jax.nn.softmax(s, axis=-1).astype(v.dtype)
    p_lat = p[..., :nk].reshape(B, H, rows, GRID_W, kh, GRID_W)
    p_ctx = p[..., nk:]
    o = (jnp.einsum('bhrqkw,brkwhd->brqhd', p_lat, vg)
         + jnp.einsum('bhrqc,bchd->brqhd', p_ctx, v_ctx))
    return o.reshape(B, L, H * Dh)

def short_conv(u, w, b):
    L = u.shape[1]
    pad = SHORT_CONV // 2
    up = jnp.pad(u, ((0, 0), (pad, pad), (0, 0)))
    y = b
    for j in range(SHORT_CONV):
        y = y + up[:, j:j + L] * w[j]
    return y

def hyena_filters(L, w1, b1, w2, b2, w3, freq):
    t = jnp.linspace(0.0, 1.0, L, dtype=f32)[:, None]
    w = 2.0 * math.pi * jnp.arange(L, dtype=f32)[:, None] / L
    fb = jnp.linspace(1e-4, FILTER_BANDS - 1, FILTER_BANDS, dtype=f32)[None, :]
    z = jnp.concatenate([t, jnp.cos(fb * w), -jnp.sin(fb * w)], axis=-1)
    fr = freq.astype(f32)
    h = jnp.sin(fr * (z @ w1.astype(f32) + b1.astype(f32)))
    h = jnp.sin(fr * (h @ w2.astype(f32) + b2.astype(f32)))
    h = h @ w3.astype(f32)
    deltas = jnp.abs(jnp.linspace(MIN_DECAY, MAX_DECAY, D_HYENA, dtype=f32))
    decay = jnp.exp(-t * deltas[None, :])
    return h[:, :D_HYENA] * decay, h[:, D_HYENA:] * decay

def bidirectional_long_conv(u, h_fwd, h_bwd):
    L = u.shape[1]
    n = 2 * L
    two_sided = jnp.concatenate([h_fwd, jnp.zeros((1, D_HYENA), f32), h_bwd[1:][::-1]], axis=0)
    U = jnp.fft.rfft(u, n=n, axis=1)
    K = jnp.fft.rfft(two_sided, n=n, axis=0)
    return jnp.fft.irfft(U * K[None], n=n, axis=1)[:, :L]

def hyena_mixer(hy, lp):
    L = hy.shape[1]
    uc = short_conv(hy, lp['conv_w'], lp['conv_b'])
    x0, x1, v = jnp.split(uc, 3, axis=-1)
    z = (v * x1).astype(f32)
    h_fwd, h_bwd = hyena_filters(L, lp['filt_w1'], lp['filt_b1'], lp['filt_w2'],
                                 lp['filt_b2'], lp['filt_w3'], lp['filt_freq'])
    y = bidirectional_long_conv(z, h_fwd, h_bwd) + z * lp['hyena_skip'].astype(f32)
    return (y * x0.astype(f32)).astype(hy.dtype)

def hier_moe(h, lp):
    B, L, D = h.shape
    xt = h.reshape(B * L, D)
    g_prob = jax.nn.softmax((xt @ lp['router_grp_w']).astype(f32) + lp['router_grp_b'].astype(f32), axis=-1)
    g_idx = jnp.argmax(g_prob, axis=-1)
    g_w = jnp.take_along_axis(g_prob, g_idx[:, None], axis=-1)
    e_logit = ((xt @ lp['router_exp_w']).astype(f32) + lp['router_exp_b'].astype(f32))
    e_logit = e_logit.reshape(-1, N_GROUPS, EXPERTS_PER_GROUP)
    e_logit = jnp.take_along_axis(e_logit, g_idx[:, None, None], axis=1)[:, 0]
    e_prob = jax.nn.softmax(e_logit, axis=-1)
    top_w, top_i = lax.top_k(e_prob, TOP_K)
    top_w = top_w / jnp.sum(top_w, axis=-1, keepdims=True)
    expert_id = g_idx[:, None] * EXPERTS_PER_GROUP + top_i
    combine = jnp.sum(jax.nn.one_hot(expert_id, N_EXPERTS, dtype=f32) * (g_w * top_w)[..., None], axis=1)
    hid = jax.nn.silu(jnp.einsum('td,edf->tef', xt, lp['w_gate'])) * jnp.einsum('td,edf->tef', xt, lp['w_up'])
    hid = hid * combine[..., None].astype(hid.dtype)
    out = jnp.einsum('tef,efd->td', hid, lp['w_down'])
    return out.reshape(B, L, D)

def trunk_layer(x, cond, lp, attend):
    sh1, sc1, gt1, sh2, sc2, gt2 = ada_mod(cond, lp['w_ada'], lp['b_ada'])
    h = rms_norm(x, lp['norm1_g']) * (1.0 + sc1) + sh1
    q, k, v, hy = split_projection(h @ lp['w_in'])
    att = attend(q, k, v)
    hyo = hyena_mixer(hy, lp)
    merged = jnp.concatenate([rms_norm(att, lp['gnorm_att']), rms_norm(hyo, lp['gnorm_hyena'])], axis=-1)
    x = x + gt1 * (merged @ lp['w_out'])
    h2 = rms_norm(x, lp['norm2_g']) * (1.0 + sc2) + sh2
    x = x + gt2 * hier_moe(h2, lp)
    return x, k, v

def setup_inputs(seed: int = 0) -> dict:
    key = jax.random.key(seed)
    ks = jax.random.split(key, 40)
    nrm = lambda k, shape, s: jax.random.normal(k, shape, f32) * s
    return {
        'x_prompt': nrm(ks[0], (BATCH, SEQ, D_MODEL), 1.0),
        'x_sample': nrm(ks[1], (DEC_BATCH, DEC_SEQ, D_MODEL), 1.0),
        'cache_k': nrm(ks[2], (DEC_BATCH, DEPTH, PAST_LEN, H_ATT, HEAD_DIM), 1.0),
        'cache_v': nrm(ks[3], (DEC_BATCH, DEPTH, PAST_LEN, H_ATT, HEAD_DIM), 1.0),
        'c': nrm(ks[4], (DEC_BATCH, D_MODEL), 1.0),
        'c_ctx': nrm(ks[5], (D_MODEL,), 1.0),
        'w_ada': nrm(ks[6], (DEPTH, D_MODEL, N_MOD * D_MODEL), 0.5 * D_MODEL ** -0.5),
        'b_ada': nrm(ks[7], (DEPTH, N_MOD * D_MODEL), 0.05),
        'norm1_g': 1.0 + nrm(ks[8], (DEPTH, D_MODEL), 0.02),
        'w_in': nrm(ks[9], (DEPTH, D_MODEL, D_IN), D_MODEL ** -0.5),
        'rpb': nrm(ks[10], (DEPTH, H_ATT, 2 * NA_ROWS - 1, 2 * NA_COLS - 1), 0.5),
        'conv_w': nrm(ks[11], (DEPTH, SHORT_CONV, 3 * D_HYENA), SHORT_CONV ** -0.5),
        'conv_b': nrm(ks[12], (DEPTH, 3 * D_HYENA), 0.02),
        'filt_w1': nrm(ks[13], (DEPTH, EMB_DIM, FILTER_FF), EMB_DIM ** -0.5),
        'filt_b1': nrm(ks[14], (DEPTH, FILTER_FF), 0.02),
        'filt_w2': nrm(ks[15], (DEPTH, FILTER_FF, FILTER_FF), FILTER_FF ** -0.5),
        'filt_b2': nrm(ks[16], (DEPTH, FILTER_FF), 0.02),
        'filt_w3': nrm(ks[17], (DEPTH, FILTER_FF, 2 * D_HYENA), FILTER_FF ** -0.5),
        'filt_freq': 1.0 + nrm(ks[18], (DEPTH, FILTER_FF), 0.1),
        'hyena_skip': nrm(ks[19], (DEPTH, D_HYENA), 1.0),
        'gnorm_att': 1.0 + nrm(ks[20], (DEPTH, D_ATT), 0.02),
        'gnorm_hyena': 1.0 + nrm(ks[21], (DEPTH, D_HYENA), 0.02),
        'w_out': nrm(ks[22], (DEPTH, D_MIX, D_MODEL), D_MIX ** -0.5),
        'norm2_g': 1.0 + nrm(ks[23], (DEPTH, D_MODEL), 0.02),
        'router_grp_w': nrm(ks[24], (DEPTH, D_MODEL, N_GROUPS), D_MODEL ** -0.5),
        'router_grp_b': nrm(ks[25], (DEPTH, N_GROUPS), 0.01),
        'router_exp_w': nrm(ks[26], (DEPTH, D_MODEL, N_EXPERTS), D_MODEL ** -0.5),
        'router_exp_b': nrm(ks[27], (DEPTH, N_EXPERTS), 0.01),
        'w_gate': nrm(ks[28], (DEPTH, N_EXPERTS, D_MODEL, D_EXPERT), D_MODEL ** -0.5),
        'w_up': nrm(ks[29], (DEPTH, N_EXPERTS, D_MODEL, D_EXPERT), D_MODEL ** -0.5),
        'w_down': nrm(ks[30], (DEPTH, N_EXPERTS, D_EXPERT, D_MODEL), D_EXPERT ** -0.5),
        'final_g': 1.0 + nrm(ks[31], (D_MODEL,), 0.02),
    }

def reference(x_prompt, x_sample, cache_k, cache_v, c, c_ctx,
              w_ada, b_ada, norm1_g, w_in, rpb, conv_w, conv_b,
              filt_w1, filt_b1, filt_w2, filt_b2, filt_w3, filt_freq, hyena_skip,
              gnorm_att, gnorm_hyena, w_out, norm2_g,
              router_grp_w, router_grp_b, router_exp_w, router_exp_b,
              w_gate, w_up, w_down, final_g):
    xp = x_prompt
    xs = x_sample
    k_states = []
    v_states = []
    for l in range(DEPTH):
        lp = {
            'w_ada': w_ada[l], 'b_ada': b_ada[l], 'norm1_g': norm1_g[l], 'w_in': w_in[l],
            'conv_w': conv_w[l], 'conv_b': conv_b[l],
            'filt_w1': filt_w1[l], 'filt_b1': filt_b1[l], 'filt_w2': filt_w2[l],
            'filt_b2': filt_b2[l], 'filt_w3': filt_w3[l], 'filt_freq': filt_freq[l],
            'hyena_skip': hyena_skip[l], 'gnorm_att': gnorm_att[l], 'gnorm_hyena': gnorm_hyena[l],
            'w_out': w_out[l], 'norm2_g': norm2_g[l],
            'router_grp_w': router_grp_w[l], 'router_grp_b': router_grp_b[l],
            'router_exp_w': router_exp_w[l], 'router_exp_b': router_exp_b[l],
            'w_gate': w_gate[l], 'w_up': w_up[l], 'w_down': w_down[l],
        }
        xp, k_ctx_new, v_ctx_new = trunk_layer(xp, c_ctx[None, :], lp, context_attention)
        k_states.append(k_ctx_new)
        v_states.append(v_ctx_new)
        attend_lat = functools.partial(neighbourhood_attention, k_ctx=cache_k[:, l],
                                       v_ctx=cache_v[:, l], rpb=rpb[l])
        xs, _, _ = trunk_layer(xs, c, lp, attend_lat)
    y_prompt = rms_norm(xp, final_g)
    y_sample = rms_norm(xs, final_g)
    new_k = jnp.stack(k_states, axis=1)
    new_v = jnp.stack(v_states, axis=1)
    return (y_prompt, y_sample, new_k, new_v)


_drawn_inputs = setup_inputs


def setup_inputs(seed=0):
    import zlib

    import numpy as np

    out = dict(_drawn_inputs(seed))
    spreads = {}
    factors = {'norm1_g': 3.099,
     'conv_b': 5.926,
     'filt_b1': 5.33,
     'filt_b2': 3.489,
     'gnorm_att': 8.0,
     'gnorm_hyena': 8.0,
     'norm2_g': 4.809,
     'router_grp_b': 8.0,
     'router_exp_b': 8.0,
     'final_g': 22.686,
     'cache_k': 8.0,
     'cache_v': 8.0,
     'rpb': 8.0}
    for name, (base, spread) in spreads.items():
        noise = np.random.default_rng([zlib.crc32(name.encode()), seed]).standard_normal(out[name].shape)
        drawn = base * np.exp(spread * noise) if base else spread * noise
        out[name] = __import__('jax').numpy.asarray(drawn.astype(out[name].dtype))
    for name, factor in factors.items():
        out[name] = (out[name] * factor).astype(out[name].dtype)
    return out
```

```python
import math
from contextlib import ExitStack

import numpy as np

import concourse.bass as bass
from concourse import mybir

F32 = mybir.dt.float32
F16 = mybir.dt.float16
I32 = mybir.dt.int32
U32 = mybir.dt.uint32
ALU = mybir.AluOpType
ACT = mybir.ActivationFunctionType
AX = mybir.AxisListType.X

P = 128
D = 1024
KT = D // P
LAT, CTX = 512, 128
TOK = LAT + CTX
NT = TOK // P
CT = NT - 1
H, DH = 8, 64
CH = 512
CB = CH // P
GRID_W, NA_ROWS, NA_COLS = 64, 8, 16
ROWS = LAT // GRID_W
FF, EMB = 64, 33
NG, EPG = 4, 4
NE = NG * EPG
FE = 512
EPS = 1e-6
TWO_PI = 2.0 * math.pi
ROUND = 1.5 * 2.0 ** 23
PI_A = float(np.float32(6.28125))
PI_B = float(np.float32(np.float32(1.9353071795e-3) * 1.0))
PI_B = float(np.floor(PI_B * 2 ** 22) / 2 ** 22)
PI_C = float(np.float32(TWO_PI - PI_A - PI_B))
CAP = 128

WQ, WK, WV, WX0, WX1, WVH = range(6)
HY = [WVH, WX1, WX0]
NA_FIRST = 4
N_ADA = 12


def key_tiles(b):
    return [t for t in (b - 1, b, b + 1) if 0 <= t < CT] if b < CT else []


def psum_jobs():
    jobs = []
    turn = [0]

    def add(name, eng, bank=None):
        if bank is None:
            bank = turn[0] % 6
            turn[0] += 1
        jobs.append((name, bank, eng))

    for i in range(2):
        add(("mlp1", i), "dve")
    for i in range(2):
        add(("mlp2", i), "dve")
    for t in range(NT):
        for d in range(2):
            add(("filt", t, d), "dve")
    add(("ckT",), "act")
    for kt in range(NT):
        for ri in range(2):
            add(("kf", kt, ri), "act")
    for j in range(NA_FIRST):
        add(("ada", j), "dve")
    add(("mcol",), "dve")
    for k in range(KT):
        add(("xT", k), "dve")
    for g in range(2):
        add(("xTp", g), "dve")
    for c in range(3):
        for cb in range(CB):
            add(("hy", c, cb), "act")
        add(("hyp", c), "act")
    for t in range(NT):
        add(("zT", t), "act")
    for kt in range(NT):
        for ri in range(2):
            add(("uf", kt, ri), "dve")
    for j in range(NA_FIRST, N_ADA):
        add(("ada", j), "dve")
    for cb in range(CB):
        add(("inv", cb), "dve")
    add(("invp",), "dve")
    add(("hst",), "dve")
    for c in "qk":
        for cb in range(CB):
            add((c, cb), "act")
        add((c + "p",), "act")
    for t in range(NT):
        add(("V", t), "act")
    add(("nk",), "act")
    units = [(b, h) for b in range(NT) for h in range(H)]
    for u in range(-2, len(units) + 1):
        if u + 2 < len(units):
            add(("s", u + 2), "dve", (u + 2) % 3)
        if 0 <= u < len(units):
            add(("pt", u), "act", 3 + u % 3)
        if u >= 1 and (u - 1) % H == H - 1:
            add(("o", (u - 1) // H), "dve", 6)
        if u - 1 >= H and (u - 1) % H == 3:
            add(("aT", (u - 1) // H - 1), "dve", 7)
    add(("aT", NT - 1), "dve", 7)
    turn[0] = 0
    for b in range(NT):
        for n in range(2):
            add(("wa", b, n), "dve")
            add(("wh", b, n), "dve")
    for b in range(NT):
        for g in range(2):
            add(("h2T", b, g), "act")
        add(("rt", b), "dve", 6)
    add(("rank",), "dve", 7)
    add(("total",), "dve", 6)
    return jobs


JOBS = psum_jobs()
JOB = {name: i for i, (name, _, _) in enumerate(JOBS)}
ORD = {}
for _name, _bank, _eng in JOBS:
    ORD[_name] = 1 + sum(1 for n in ORD if JOBS[JOB[n]][2] == _eng)

CHUNKS = ([("dft",)] + [("ada", j) for j in range(NA_FIRST)] + [("win", c) for c in HY] + [("dft",)]
          + [("ada", j) for j in range(NA_FIRST, N_ADA)] + [("idft",)]
          + [("win", c) for c in (WQ, WK, WV)] + [("wout", n) for n in range(2)])
NRING = 4
NCH = len(CHUNKS)
ESLOTS = 6
HYROW = range(3)


def last_jobs():
    seen, out = 0, []
    for c in CHUNKS:
        if c[0] == "dft":
            out.append(("kf", CT - 1, 1) if seen == 0 else ("uf", CT - 1, 1))
            seen += 1
        elif c[0] == "ada":
            out.append(c)
        elif c[0] == "idft":
            out.append(("inv", CB - 1))
        elif c[0] == "wout":
            out.append(("wh", NT - 1, c[1]))
        elif c[1] in HY:
            out.append(("hyp", HY.index(c[1])))
        else:
            out.append({WQ: ("qp",), WK: ("kp",), WV: ("V", NT - 1)}[c[1]])
    return out


LAST_JOB = last_jobs()
FIRST_USE = {}
for _i, _c in enumerate(CHUNKS):
    FIRST_USE.setdefault(_c, []).append(_i)


def program(nc, a, outs):
    ctx = ExitStack()
    with ctx:
        def sb(name, shape, dt=F32):
            return ctx.enter_context(nc.sbuf_tensor(name, shape, dt))

        def sem(name):
            return ctx.enter_context(nc.semaphore(name))

        bank = [ctx.enter_context(nc.psum_tensor(f"bank{i}", [P, 512], F32)) for i in range(8)]
        KB = 256
        big = sb("big", [P, 198 * KB])

        def at(kb, *shape):
            n = int(np.prod(shape))
            v = big[:, int(kb * KB):int(kb * KB) + n]
            if len(shape) == 1:
                return v
            names = "abcd"[:len(shape)]
            return v.rearrange(f"p ({' '.join(names)}) -> p {' '.join(names)}",
                               **{x: s for x, s in zip(names[1:], shape[1:])})

        slot_kb = [0, 16, 32, 48, 164, 180]
        slot = [at(kb, 4096) for kb in slot_kb]
        x = at(64, NT, D)
        hT = at(84, KT, TOK)
        s_flt, d_flt = at(104, NT, CH), at(114, NT, CH)
        dec = at(124, NT, CH)
        zf = at(134, TOK)
        mw3 = at(136.5, 2 * CH)
        mh = [at(140.5, TOK), at(143, TOK)]
        KR, KI = at(147, NT, CH), at(157, NT, CH)
        mtmp = [at(167, TOK), at(169.5, TOK)]
        fbuf = at(172, 2, CH)
        xn = at(178, NT, D)
        UW = 644
        ustrip = at(104, CB, UW)
        z = at(114.25, CB, UW)
        x0 = at(124.5, CB, UW)
        ctmp = at(134.75, 2, UW)
        zt = at(178, NT, CH)
        YR, YI = at(188, NT, CH), at(167, NT, CH)
        ytmp = at(140, 2, CH)
        hyoT = at(104, CB, TOK)
        sq = at(178, CB, TOK)
        t1 = at(140, 2, TOK)
        QT, KTt = at(114.25, CB, TOK), at(124.5, CB, TOK)
        V = at(134.75, NT, CH)
        nkb = at(188, CH)
        base = at(145, H, NA_ROWS, 3 * NA_COLS)
        Tm = at(157, 3, 512)
        pr = at(164, 2, 512)
        PT = at(168, 2, 4, P)
        sc = at(172, 2, 512)
        att = at(176, NT, CH)
        attT = at(186, CB, TOK)
        gt1 = at(84, 2, D)
        G2 = at(92, 2, D)
        SH2 = at(114.25, 2, D)
        wtmp = at(122.25, 2, 2, 512)
        h2 = at(130.5, 2, D)
        h2T = at(138.5, 2, KT, P)
        xg = at(84, 2, D)
        xgT = at(92, 2, KT, P)
        hid = at(100, 2, FE)
        hidT = at(104, 2, FE // P, P)
        sil = at(108, FE)
        yout = at(110, 2, D)
        gt2 = at(118, 2, D)
        fg = at(126, D)
        ya = at(130, 2, D)
        yb = at(138, 2, D)
        sqd = at(147, D)
        sqs = at(100, CH)

        ident = sb("ident", [P, P])
        b_buf = [at(134, 2, 512)[0:2], at(104, 2, 512)[0:2]]
        mrow = [at(138, 2, 512)[0:2], at(108, 2, 512)[0:2]]
        ckT = sb("ckT", [P, CB, P])
        craw = at(188, CH)
        cv = at(196, CH)
        cond = sb("cond", [P, KT, 2])
        scond = sb("scond", [P, KT, 2])
        csig = sb("csig", [P, KT, 2])
        mcol = sb("mcol", [P, 2, KT, 2])
        g1c = sb("g1c", [P, KT])
        cwb = sb("cwb", [P, 3, CB, 4])
        chn = sb("chn", [P, 3, CB])
        mlp_c = sb("mlp_c", [FF, 3])
        mlp_f = sb("mlp_f", [FF, 2])
        w12 = sb("w12", [FF, 2, FF])
        bmask = sb("bmask", [P, NT])
        maskb = sb("maskb", [P, 3, 3 * NA_COLS])
        dftp = sb("dftp", [P, 4, P])
        ones = sb("ones", [P, P])
        tri = sb("tri", [P, P])
        iota = sb("iota", [P, P], F16)
        tid = sb("tid", [P, NT], F16)
        rw = sb("rw", [P, KT, NG + NE])
        rb = sb("rb", [P, NG + NE])
        ss = sb("ss", [P, 8, NT])
        rmx = sb("rmx", [P, 4])
        nmx = sb("nmx", [P, 4])
        rsum = sb("rsum", [P, 2, H])
        rinv = sb("rinv", [P, 2, H])
        lg = sb("lg", [P, NT, NG + NE])
        R = at(151, 16, NT, NE)
        rankm = sb("rankm", [P, NT, NE])
        posf = sb("posf", [P, 2, NT])
        posi = sb("posi", [P, 2, NT], I32)
        wts = sb("wts", [P, 2, NT])
        over = sb("over", [1, 1], I32)
        rsh = sb("rsh", [P, 2, NT])
        sel = at(156, 2, NT, P // 2).bitcast(F16)
        idx = sb("idx", [P, 2], I32)

        m_dram = nc.dram_tensor("m_scratch", [2, 6 * D], F32).ap()
        h2_dram = nc.dram_tensor("h2_scratch", [TOK, D], F32).ap()
        y_dram = nc.dram_tensor("y_scratch", [NT * NE * P, D], F32).ap()

        pe_full = sem("pe_bank_full")
        drained = {"act": sem("act_bank_drained"), "dve": sem("dve_bank_drained")}
        chunk_in = [sem(f"chunk_in{i}") for i in range(NRING)]
        in_mlp, in_dec, in_cond, in_small, in_x, in_base, in_ctx = (
            sem(n) for n in ("in_mlp", "in_dec", "in_cond", "in_small", "in_x", "in_base", "in_ctx"))
        in_dft = sem("in_dft")
        b_in = [sem("b_ada_in0"), sem("b_ada_in1")]
        m_out = [sem("m_row_out0"), sem("m_row_out1")]
        gt1_in, g2_in, sh2_in, tail_in = sem("gt1_in"), sem("g2_in"), sem("sh2_in"), sem("tail_in")
        act_chain, dve_chain, pool_chain = sem("act_chain"), sem("dve_chain"), sem("pool_chain")
        consts_ok = sem("consts_ok")
        cond_ok = sem("cond_ok")
        sin_arg, sin_ok = sem("sin_arg"), sem("sin_ok")
        filt_ok = sem("filt_ok")
        x_sq, x_rt, x_rs, xn_ok = sem("x_sq"), sem("x_rt"), sem("x_rs"), sem("xn_ok")
        conv_ok, z_ok = sem("conv_ok"), sem("z_ok")
        tap_ok, tap_used = sem("conv_tap_ok"), sem("conv_tap_used")
        y_ok = sem("y_ok")
        hyo_ok, hsq_ok, hg_ok = sem("hyo_ok"), sem("hsq_ok"), sem("hyena_gained")
        hrt = sem("h_root")
        kv_out = sem("kv_out")
        tm_ok, tm_used = sem("bias_ok"), sem("bias_used")
        mx_ok, p_ok = sem("mx_ok"), sem("p_ok")
        att_sq, att_rt = sem("att_sq"), sem("att_root")
        pv_ok = sem("pv_ok")
        wt_ok, wt2_ok = sem("wt_ok"), sem("x1_ok")
        n_sq, n_rt, h2_ok = sem("n_sq"), sem("n_rt"), sem("h2_ok")
        h2_out = [sem("h2_out0"), sem("h2_out1")]
        route_e, route_a, route_ok = sem("route_exp_arg"), sem("route_exp_ok"), sem("route_ok")
        mask_ok = sem("mask_ok")
        ew_in = [sem(f"expert_w_in{i}") for i in range(ESLOTS)]
        epsb = sb("epsb", [P, 1])
        mrow_used = sem("mod_row_turned")
        assigned, shifted = sem("assigned"), sem("ranks_shifted")
        gather_go = sem("gather_go")
        sel_ok, idx_full, idx_ok = sem("sel_ok"), sem("idx_full"), sem("idx_ok")
        xg_in = [sem("xg_in0"), sem("xg_in1")]
        xgT_full, xgT_ok = sem("xgT_full"), sem("xgT_ok")
        gu_full, sil_ok, hid_ok = sem("gate_up_full"), sem("silu_ok"), sem("hid_ok")
        hidT_full, hidT_ok = sem("hidT_full"), sem("hidT_ok")
        y_full, y_cp = sem("y_full"), sem("y_copied")
        y_out = [sem("y_out0"), sem("y_out1")]
        yab_in = [sem("results_in0"), sem("results_in1")]
        stores_ok = sem("stores_ok")
        strip_ok, sq_ok = sem("strip_ok"), sem("sq_ok")
        y_cpA, y_cpD = sem("y_copied_act"), sem("y_copied_dve")
        f_cmb, f_sq, f_rt, f_ok, f_out = sem("f_cmb"), sem("f_sq"), sem("f_rt"), sem("f_ok"), sem("f_out")

        def full(eng, *name):
            eng.wait_ge(pe_full, JOB[name] + 1)
            return bank[JOBS[JOB[name]][1]]

        def have(eng, *name):
            eng.wait_ge(drained[JOBS[JOB[name]][2]], ORD[name])

        def drain(ins, *name):
            return ins.then_inc(drained[JOBS[JOB[name]][2]], 1)

        def wait_past(eng, sema, count):
            if not isinstance(count, int) or count > 0:
                eng.wait_ge(sema, count)

        def wait_pv(eng, u):
            if u % H == H - 1:
                full(eng, "o", u // H)
            else:
                eng.wait_ge(pv_ok, u // H * (H - 1) + u % H + 1)

        def turned_h2(act, b):
            for g in range(2):
                bk = full(act, "h2T", b, g)
                if b >= 2:
                    full(act, "rt", b - 2)
                drain(act.copy(h2T[:, b % 2, 4 * g:4 * g + 4, :].rearrange("p a b -> p (a b)"), bk[:, :]), "h2T", b, g)

        def chunk_src(c):
            if c[0] == "dft":
                return a["dft"][0]
            if c[0] == "idft":
                return a["dft"][1]
            w = {"ada": a["w_ada"], "win": a["w_in"], "wout": a["w_out"]}[c[0]]
            return w[:, c[1] * 512:(c[1] + 1) * 512].rearrange("(k p) n -> p k n", p=P)

        def chunk_view(i):
            return slot[i % NRING].rearrange("p (k n) -> p k n", n=512)

        pairs = NE // 2

        block = ctx.enter_context(nc.Block())

        @block.sync
        def _(sp):
            sp.dma_start(zf[0:EMB, :], a["zf"]).then_inc(in_mlp, 16)
            sp.dma_start(w12[0:EMB, 0, :], a["w1"]).then_inc(in_mlp, 16)
            sp.dma_start(w12[:, 1, :], a["w2"]).then_inc(in_mlp, 16)
            sp.dma_start(mlp_c[:, :], a["mlp_c"]).then_inc(in_mlp, 16)
            sp.dma_start(mw3[0:FF, :], a["w3"]).then_inc(in_mlp, 16)
            sp.dma_start(dec, a["dec"].rearrange("(t p) n -> p t n", p=P)).then_inc(in_dec, 16)
            sp.dma_start(bmask[:, :], a["bmask"]).then_inc(in_dec, 16)

            def load_chunk(i):
                if i >= NRING:
                    full(sp, *LAST_JOB[i - NRING])
                src = chunk_src(CHUNKS[i])
                if len(src.shape) == 2:
                    src = src.rearrange("p (k n) -> p k n", n=512)
                sp.dma_start(chunk_view(i), src).then_inc(chunk_in[i % NRING], 16)

            load_chunk(0)
            sp.dma_start(dftp[:, :, :], a["dftp"]).then_inc(in_dft, 16)
            sp.dma_start(x, a["x"].rearrange("(t p) n -> p t n", p=P)).then_inc(in_x, 16)
            for i in range(1, NCH):
                load_chunk(i)
            wg, wu, wd = a["w_gate"], a["w_up"], a["w_down"]

            def load_expert(e, s):
                for j, w in enumerate((wg, wu, wd)):
                    src = w[bass.ds(e, 1), :, :] if not isinstance(e, int) else w[e:e + 1, :, :]
                    n = 512 if j < 2 else 1024
                    src = src.rearrange("a (k p) n -> p (a k) n", p=P)
                    sp.dma_start(slot[3 * s + j].rearrange("p (k n) -> p k n", n=n), src)\
                      .then_inc(ew_in[3 * s + j], 16)
            full(sp, *LAST_JOB[-1])
            load_expert(0, 0)
            load_expert(1, 1)
            with sp.Fori(1, pairs) as i:
                for s in range(2):
                    sp.wait_ge(y_full, i * 4 + 2 * (s - 1))
                    load_expert(i * 2 + s, s)
            sp.wait_ge(route_ok, 1)
            v = sp.value_load(over[0:1, 0:1])
            with sp.If(v > 0):
                with sp.Fori(1, NT) as t:
                    with sp.Fori(0, pairs) as i:
                        for s in range(2):
                            sp.wait_ge(y_full, (t * pairs + i) * 4 + 2 * (s - 1))
                            load_expert(i * 2 + s, s)
            for t in range(NT):
                sp.wait_ge(f_ok, t + 1)
                sp.dma_start(outs["y"][t * P:(t + 1) * P, :], x[:, t, :]).then_inc(f_out, 16)
            sp.wait_ge(f_out, 16 * NT)
            sp.wait_ge(kv_out, 32)

        @block.gpsimd
        def _(pool):
            n_chain = [0]

            def link(ins):
                n_chain[0] += 1
                ins.then_inc(pool_chain, 1)
                pool.wait_ge(pool_chain, n_chain[0])

            link(pool.memset(ident[:, :], 0.0))
            link(pool.affine_select(out=ident[:, :], in_=ident[:, :], compare_op=ALU.not_equal, fill=1.0,
                                    base=0, pattern=[[-1, P]], channel_multiplier=1))
            link(pool.memset(ones[:, :], 1.0))
            link(pool.affine_select(out=tri[:, :], in_=ones[:, :], compare_op=ALU.is_gt, fill=0.0,
                                    base=0, pattern=[[1, P]], channel_multiplier=-1))
            pool.memset(over[:, :], 0).then_inc(consts_ok, 1)
            pool.dma_start(rw[:, :, :], a["rw"].rearrange("(k p) n -> p k n", p=P)).then_inc(in_small, 16)
            pool.dma_start(rb[:, :], a["rb"].partition_broadcast(P)).then_inc(in_small, 16)
            pool.dma_start(iota[:, :], a["iota"]).then_inc(in_small, 16)
            pool.dma_start(tid[:, :], a["tid"]).then_inc(in_small, 16)
            pool.dma_start(maskb[:, :, :], a["maskb"]).then_inc(in_small, 16)
            have(pool, "invp")
            have(pool, "hst")
            for r in range(ROWS):
                pool.dma_start(base[r * NA_COLS:(r + 1) * NA_COLS].rearrange("p h r c -> p h (r c)"),
                               a["rpb"][:, :, (NA_ROWS - 1 - r) * 3 * NA_COLS:(2 * NA_ROWS - 1 - r) * 3 * NA_COLS])\
                    .then_inc(in_base, 16)
            link(pool.memset(Tm, 0.0))
            pool.wait_ge(in_small, 5 * 16)
            pool.wait_ge(in_base, 16 * ROWS)
            for u in range(CT * H):
                b, h = u // H, u % H
                if u >= 3:
                    have(pool, "s", u - 3)
                kts = key_tiles(b)
                kind = 0 if b == 0 else 2 if b == CT - 1 else 1
                for j, t in enumerate(kts):
                    dt = t - b + 1
                    out = Tm[:, u % 3, P * (1 + j):P * (2 + j)].rearrange("p (r c) -> p r c", c=NA_COLS)
                    in0 = base[:, h, :, dt * NA_COLS:(dt + 1) * NA_COLS]
                    in1 = maskb[:, kind, dt * NA_COLS:(dt + 1) * NA_COLS].unsqueeze(1)\
                        .broadcast_to([P, NA_ROWS, NA_COLS])
                    last = pool.tensor_tensor(out, in0, in1, ALU.add)
                last.then_inc(tm_ok, 1)
            for q in m_out:
                pool.wait_ge(q, 8 * (N_ADA - NA_FIRST))
            have(pool, "V", NT - 1)
            for c in range(2):
                pool.dma_start(gt1[:, c, :], m_dram[c:c + 1, 2 * D:3 * D].rearrange("a n -> (a n)").partition_broadcast(P)).then_inc(gt1_in, 16)
            for c in range(2):
                pool.dma_start(G2[:, c, :], m_dram[c:c + 1, 4 * D:5 * D].rearrange("a n -> (a n)").partition_broadcast(P)).then_inc(g2_in, 16)
            have(pool, "aT", NT - 1)
            for c in range(2):
                pool.dma_start(SH2[:, c, :], m_dram[c:c + 1, 3 * D:4 * D].rearrange("a n -> (a n)").partition_broadcast(P)).then_inc(sh2_in, 16)
            pool.dma_start(h2[:, 0, :], a["g2"].partition_broadcast(P)).then_inc(g2_in, 16)
            pool.wait_ge(g2_in, 48)
            for c in range(2):
                link(pool.tensor_scalar(G2[:, c, :], G2[:, c, :], 1.0, None, ALU.add))
            for c in range(2):
                ins = pool.tensor_tensor(G2[:, c, :], G2[:, c, :], h2[:, 0, :], ALU.mult)
                ins.then_inc(mask_ok, 1)
            pool.wait_ge(gt1_in, 32)
            for b in range(NT):
                for n in range(2):
                    i = 2 * b + n
                    have(pool, "wh", b, n)
                    w = wtmp[:, i % 2, 0, :]
                    link(pool.tensor_tensor(w, w, gt1[:, b // CT, n * 512:(n + 1) * 512], ALU.mult))
                    pool.tensor_tensor(x[:, b, n * 512:(n + 1) * 512], x[:, b, n * 512:(n + 1) * 512], w,
                                       ALU.add).then_inc(wt2_ok, 1)
            for b in range(NT):
                pool.wait_ge(h2_ok, b + 1)
                pool.dma_start(h2_dram[b * P:(b + 1) * P, :], h2[:, b % 2, :]).then_inc(h2_out[b % 2], 16)
            pool.wait_ge(h2_out[0], 16 * 3)
            pool.wait_ge(h2_out[1], 16 * 2)
            pool.wait_ge(route_ok, 1)
            for c in range(2):
                pool.dma_start(gt2[:, c, :], m_dram[c:c + 1, 5 * D:6 * D].rearrange("a n -> (a n)").partition_broadcast(P)).then_inc(tail_in, 16)
            pool.dma_start(fg, a["fg"].partition_broadcast(P)).then_inc(tail_in, 16)

            def gather(i, first):
                for s in range(2):
                    pool.wait_ge(idx_ok, i * 2 + (s + 1))
                    if not first:
                        pool.wait_ge(xgT_full, i * 4 + 2 * (s - 1))
                    pool.sem_inc(gather_go, 1)
                    pool.indirect_dma_start(out=xg[:, s, :], out_offset=None, in_=h2_dram,
                                            in_offset=bass.IndirectOffsetOnAxis(ap=idx[:, s:s + 1].bitcast(U32), axis=0))\
                        .then_inc(xg_in[s], 16)
            gather(0, True)
            with pool.Fori(1, pairs) as i:
                gather(i, False)
            v = pool.value_load(over[0:1, 0:1])
            with pool.If(v > 0):
                with pool.Fori(pairs, NT * pairs) as i:
                    gather(i, False)
            pool.wait_ge(stores_ok, 1)

            def results(table):
                for t in range(NT):
                    if t >= 2:
                        pool.wait_ge(f_cmb, t - 1)
                    for k, buf in enumerate((ya, yb)):
                        pool.indirect_dma_start(out=buf[:, t % 2, :], out_offset=None, in_=table,
                                                in_offset=bass.IndirectOffsetOnAxis(ap=posi[:, k, t:t + 1].bitcast(U32), axis=0))\
                            .then_inc(yab_in[t % 2], 16)
            with pool.If(v > 0):
                results(y_dram)
            with pool.Else():
                results(y_dram[0:NE * P, :])

        @block.scalar
        def _(act):
            n_chain = [0]

            def link(ins):
                n_chain[0] += 1
                ins.then_inc(act_chain, 1)
                act.wait_ge(act_chain, n_chain[0])

            act.dma_start(cond[:, :, :], a["cond"]).then_inc(in_cond, 16)
            act.dma_start(craw, a["ck"]).then_inc(in_ctx, 16)
            act.dma_start(g1c[:, :], a["g1c"]).then_inc(in_cond, 16)
            act.dma_start(cwb[:, :, :, :], a["cwb"]).then_inc(in_cond, 16)
            act.dma_start(chn[:, :, :], a["chn"]).then_inc(in_cond, 16)
            act.wait_ge(in_cond, 64)
            act.activation(scond[:, :, :], cond[:, :, :], ACT.Silu).then_inc(cond_ok, 1)
            for layer in range(2):
                act.wait_ge(sin_arg, layer + 1)
                act.activation(mh[layer][0:FF, :], mtmp[0][0:FF, :], ACT.Sin).then_inc(sin_ok, 1)
            def load_bias(j):
                r = 0 if j < NA_FIRST else 1
                act.dma_start(b_buf[r][:, j % 2, :], a["b2"][:, j * 512:(j + 1) * 512]).then_inc(b_in[j % 2], 16)
            have(act, "filt", NT - 1, 1)
            load_bias(0)
            load_bias(1)
            full(act, "ckT")
            drain(act.copy(ckT[:, :, :].rearrange("p a b -> p (a b)"), bank[JOBS[JOB[("ckT",)]][1]][:, :]), "ckT")
            for kt in range(NT):
                for ri, K in enumerate((KR, KI)):
                    b = full(act, "kf", kt, ri)
                    drain(act.copy(K[:, kt, :], b[:, :]), "kf", kt, ri)
            have(act, "ada", 0)
            load_bias(2)
            have(act, "ada", 1)
            load_bias(3)
            act.wait_ge(in_x, 16)
            have(act, "ckT")
            for t in range(NT):
                ins = act.activation(xn[:, t, :], x[:, t, :], ACT.Square, scale=1.0 / 32.0,
                                     accum_out=ss[:, 0, t:t + 1])
                link(ins)
            act.activation(ss[:, 1, :], ss[:, 0, :], ACT.Sqrt, bias=epsb[:, :]).then_inc(x_rt, 1)
            act.wait_ge(x_rs, 1)
            for t in range(NT):
                act.activation(xn[:, t, :], x[:, t, :], ACT.Copy, scale=ss[:, 2, t:t + 1]).then_inc(xn_ok, 1)
            n_tap = 0
            for c in range(3):
                for cb in range(CB):
                    b = full(act, "hy", c, cb)
                    if c == 0 and cb == 0:
                        act.wait_ge(strip_ok, 1)
                    if c > 0:
                        act.wait_ge(conv_ok, (c - 1) * CB + cb + 1)
                    dst = ustrip[:, cb, 1:1 + LAT].rearrange("p (r b c) -> p b r c", r=ROWS, c=NA_COLS)
                    drain(act.copy(dst, b[:, :].rearrange("p (b r c) -> p b r c", r=ROWS, c=NA_COLS)), "hy", c, cb)
                b = full(act, "hyp", c)
                drain(act.copy(ustrip[:, :, LAT + 2:LAT + 2 + CTX],
                               b[:, :].rearrange("p (a n) -> p a n", n=CTX)), "hyp", c)
                have(act, "hyp", c)
                for cb in range(CB):
                    dst = (z[:, cb], ctmp[:, cb % 2], x0[:, cb])[c][:, 0:UW - 3]
                    if c == 1 and cb >= 2:
                        act.wait_ge(z_ok, cb - 1)
                    act.activation(dst, ustrip[:, cb, 1:UW - 2], ACT.Identity, scale=cwb[:, HYROW[c], cb, 1:2],
                                   bias=cwb[:, HYROW[c], cb, 3:4]).then_inc(tap_ok, 1)
            for t in range(NT):
                b = full(act, "zT", t)
                drain(act.copy(zt[:, t, :], b[:, :]), "zT", t)
            act.wait_ge(conv_ok, 3 * CB)
            load_bias(4)
            load_bias(5)
            for j in range(NA_FIRST, N_ADA):
                have(act, "ada", j)
                act.dma_start(m_dram[:, j * 512:(j + 1) * 512], mrow[1][:, j % 2, :]).then_inc(m_out[j % 2], 16)
                if j + 2 < N_ADA:
                    load_bias(j + 2)
            for cb in range(CB):
                act.wait_ge(hyo_ok, CB)
                act.activation(sq[:, cb, :], hyoT[:, cb, :], ACT.Square).then_inc(hsq_ok, 1)
            act.wait_ge(hsq_ok, CB)
            for cb in range(CB):
                act.activation(hyoT[:, cb, :], hyoT[:, cb, :], ACT.Copy, scale=chn[:, 1, cb:cb + 1]).then_inc(hg_ok, 1)
            have(act, "invp")
            act.dma_start(cv, a["cv"]).then_inc(in_ctx, 16)
            for ch, dst, scale in (("q", QT, DH ** -0.5), ("k", KTt, 1.0)):
                for cb in range(CB):
                    b = full(act, ch, cb)
                    drain(act.activation(dst[:, cb, 0:LAT], b[:, :], ACT.Copy, scale=scale), ch, cb)
                b = full(act, ch + "p")
                drain(act.activation(dst[:, :, LAT:TOK], b[:, :].rearrange("p (a n) -> p a n", n=CTX), ACT.Copy,
                                     scale=scale), ch + "p")
            for t in range(NT):
                b = full(act, "V", t)
                drain(act.copy(V[:, t, :], b[:, :]), "V", t)
            b = full(act, "nk")
            drain(act.copy(nkb, b[:, :]), "nk")
            have(act, "nk")
            act.dma_start(outs["v"], V[:, CT, :]).then_inc(kv_out, 16)
            act.dma_start(outs["k"], nkb).then_inc(kv_out, 16)

            def exps(u):
                b, h = u // H, u % H
                n = P * (1 + len(key_tiles(b)))
                act.wait_ge(mx_ok, u + 1)
                if u >= 2:
                    full(act, "pt", u - 2)
                if h == 0 and b >= 2:
                    have(act, "o", b - 2)
                act.activation(pr[:, u % 2, 0:n], sc[:, u % 2, 0:n], ACT.Exp, bias=nmx[:, u % 4:u % 4 + 1],
                               accum_out=rsum[:, b % 2, h:h + 1]).then_inc(p_ok, 1)

            def probs_turned(u):
                nk = 1 + len(key_tiles(u // H))
                b = full(act, "pt", u)
                if u >= 2:
                    wait_pv(act, u - 2)
                drain(act.copy(PT[:, u % 2, 0:nk, :].rearrange("p a b -> p (a b)"), b[:, 0:nk * P]), "pt", u)

            def att_squares(b):
                have(act, "o", b)
                link(act.activation(sqs, att[:, b, :], ACT.Square, accum_out=ss[:, 3, b:b + 1]))

            exps(0)
            for u in range(NT * H):
                if u + 1 < NT * H:
                    exps(u + 1)
                probs_turned(u)
                if u % H == 4 and u > H:
                    att_squares(u // H - 1)
            att_squares(NT - 1)
            act.activation(ss[:, 4, :], ss[:, 3, :], ACT.Sqrt, scale=1.0 / CH, bias=epsb[:, :]).then_inc(att_rt, 1)
            act.wait_ge(hrt, 1)
            act.activation(ss[:, 6, :], ss[:, 5, :], ACT.Sqrt, scale=1.0 / CH, bias=epsb[:, :]).then_inc(att_rt, 1)
            for b in range(NT):
                act.wait_ge(wt2_ok, 2 * b + 2)
                link(act.activation(sqd, x[:, b, :], ACT.Square, scale=1.0 / 32.0, accum_out=ss[:, 0, b:b + 1]))
                act.activation(ss[:, 1, b:b + 1], ss[:, 0, b:b + 1], ACT.Sqrt, bias=epsb[:, :]).then_inc(n_rt, 1)
                if b > 0:
                    turned_h2(act, b - 1)
            turned_h2(act, NT - 1)
            act.wait_ge(route_e, 1)
            act.activation(R[:, 1, :, 0:NG], R[:, 0, :, 0:NG], ACT.Exp).then_inc(route_a, 1)
            act.wait_ge(route_e, 2)
            act.activation(R[:, 9, :, 0:1], R[:, 8, :, 0:1], ACT.Exp).then_inc(route_a, 1)

            def expert(p, i, s):
                n = (i + p * pairs) * 2 + s
                act.wait_ge(gu_full, n * 2 + 1)
                wait_past(act, hid_ok, n)
                act.activation(sil, bank[2][:, :], ACT.Silu).then_inc(sil_ok, 1)
                act.wait_ge(hidT_full, n + 1)
                act.copy(hidT[:, s].rearrange("p a b -> p (a b)"), bank[4][:, :]).then_inc(hidT_ok, 1)
                act.wait_ge(y_full, n * 2 + 1)
                wait_past(act, y_out[s], (i + p * pairs) * 16)
                act.copy(yout[:, s, 0:512], bank[5][:, :]).then_inc(y_cpA, 1)
                act.wait_ge(y_cpA, n + 1)
                act.wait_ge(y_cpD, n + 1)
                row = n * P
                act.dma_start(y_dram[bass.ds(row, P), :], yout[:, s, :]).then_inc(y_out[s], 16)

            def one_pass(p):
                for s in range(2):
                    expert(p, 0, s)
                with act.Fori(1, pairs) as i:
                    for s in range(2):
                        expert(p, i, s)
                for s in range(2):
                    act.wait_ge(y_out[s], (p + 1) * (pairs * 16))
            one_pass(0)
            act.wait_ge(route_ok, 1)
            v = act.value_load(over[0:1, 0:1])
            with act.If(v > 0):
                with act.Fori(1, NT) as p:
                    one_pass(p)
            act.copy(ss[:, 7, :], ss[:, 6, :]).then_inc(stores_ok, 1)
            for t in range(NT):
                act.wait_ge(f_cmb, t + 1)
                link(act.activation(sqd, x[:, t, :], ACT.Square, scale=1.0 / 32.0, accum_out=ss[:, 0, t:t + 1]))
                act.activation(ss[:, 1, t:t + 1], ss[:, 0, t:t + 1], ACT.Sqrt, bias=epsb[:, :]).then_inc(f_rt, 1)

        @block.vector
        def _(dve):
            n_chain = [0]

            def link(ins):
                n_chain[0] += 1
                ins.then_inc(dve_chain, 1)
                dve.wait_ge(dve_chain, n_chain[0])

            dve.memset(epsb[:, :], EPS).then_inc(consts_ok, 1)
            dve.wait_ge(in_mlp, 80)
            for layer in range(2):
                v, k = mtmp[0][0:FF, :], mtmp[1][0:FF, :]
                if layer:
                    dve.wait_ge(sin_ok, 1)
                for i, (lo, hi) in enumerate(((0, LAT), (LAT, TOK))):
                    b = full(dve, f"mlp{layer + 1}", i)
                    drain(dve.tensor_scalar(v[:, lo:hi], b[0:FF, 0:hi - lo], mlp_c[:, layer:layer + 1], mlp_c[:, 2:3],
                                            ALU.add, ALU.mult), f"mlp{layer + 1}", i)
                have(dve, f"mlp{layer + 1}", 1)
                link(dve.tensor_scalar(k, v, 1.0 / TWO_PI, ROUND, ALU.mult, ALU.add))
                link(dve.tensor_scalar(k, k, ROUND, None, ALU.subtract))
                for part in (PI_A, PI_B, PI_C):
                    link(dve.scalar_tensor_tensor(out=v, in0=k, scalar=-part, in1=v, op0=ALU.mult, op1=ALU.add))
                dve.tensor_scalar(v, v, 3.1415925, -3.1415925, ALU.min, ALU.max).then_inc(sin_arg, 1)
            dve.wait_ge(in_dec, 32)
            for t in range(NT):
                b = full(dve, "filt", t, 0)
                drain(dve.tensor_tensor(fbuf[:, 0, :], b[:, :], dec[:, t, :], ALU.mult), "filt", t, 0)
                b = full(dve, "filt", t, 1)
                drain(dve.scalar_tensor_tensor(out=fbuf[:, 1, :], in0=b[:, :], scalar=bmask[:, t:t + 1],
                                               in1=dec[:, t, :], op0=ALU.mult, op1=ALU.mult), "filt", t, 1)
                have(dve, "filt", t, 1)
                dve.tensor_tensor(s_flt[:, t, :], fbuf[:, 0, :], fbuf[:, 1, :], ALU.add).then_inc(filt_ok, 1)
                dve.tensor_tensor(d_flt[:, t, :], fbuf[:, 0, :], fbuf[:, 1, :], ALU.subtract).then_inc(filt_ok, 1)
                dve.wait_ge(filt_ok, 2 * t + 2)

            def ada(j):
                r = 0 if j < NA_FIRST else 1
                dve.wait_ge(b_in[j % 2], 16 * (j // 2 + 1))
                if j >= NA_FIRST + 2:
                    dve.wait_ge(m_out[j % 2], 16 * ((j - NA_FIRST) // 2))
                b = full(dve, "ada", j)
                drain(dve.tensor_tensor(mrow[r][:, j % 2, :], b[0:2, :], b_buf[r][:, j % 2, :], ALU.add), "ada", j)

            for j in range(NA_FIRST):
                if j >= 2:
                    dve.wait_ge(mrow_used, j - 1)
                ada(j)
            dve.wait_ge(in_cond, 64)
            b = full(dve, "mcol")
            mc = b[:, 0:4 * KT].rearrange("p (v k c) -> p v k c", v=2, c=2)
            link(dve.tensor_copy(mcol[:, 1], mc[:, 0]))
            drain(dve.scalar_tensor_tensor(out=mcol[:, 0], in0=mc[:, 1], scalar=1.0,
                                           in1=g1c[:, :].unsqueeze(2).broadcast_to([P, KT, 2]),
                                           op0=ALU.add, op1=ALU.mult), "mcol")
            have(dve, "mcol")
            dve.wait_ge(x_rt, 1)
            dve.reciprocal(ss[:, 2, :], ss[:, 1, :]).then_inc(x_rs, 1)
            have(dve, "kf", NT - 1, 1)
            for k in range(KT):
                b = full(dve, "xT", k)
                drain(dve.tensor_scalar(hT[:, k, 0:LAT], b[:, :], mcol[:, 0, k, 0:1], mcol[:, 1, k, 0:1],
                                        ALU.mult, ALU.add), "xT", k)
            for g in range(2):
                b = full(dve, "xTp", g)
                for j in range(4):
                    k = 4 * g + j
                    ins = dve.tensor_scalar(hT[:, k, LAT:TOK], b[:, j * P:(j + 1) * P], mcol[:, 0, k, 1:2],
                                            mcol[:, 1, k, 1:2], ALU.mult, ALU.add)
                drain(ins, "xTp", g)
            dve.memset(ustrip, 0.0).then_inc(strip_ok, 1)
            n = 0
            for c in range(3):
                for cb in range(CB):
                    n += 1
                    dst = (z[:, cb], ctmp[:, cb % 2], x0[:, cb])[c][:, 0:UW - 3]
                    w = cwb[:, HYROW[c], cb, :]
                    dve.wait_ge(tap_ok, n)
                    link(dve.scalar_tensor_tensor(out=dst, in0=ustrip[:, cb, 0:UW - 3], scalar=w[:, 0:1], in1=dst,
                                                  op0=ALU.mult, op1=ALU.add))
                    dve.scalar_tensor_tensor(out=dst, in0=ustrip[:, cb, 2:UW - 1], scalar=w[:, 2:3], in1=dst,
                                             op0=ALU.mult, op1=ALU.add).then_inc(conv_ok, 1)
                    dve.wait_ge(conv_ok, n)
                    if c == 1:
                        dve.tensor_tensor(z[:, cb, 0:UW - 3], z[:, cb, 0:UW - 3], dst, ALU.mult).then_inc(z_ok, 1)
            for kt in range(NT):
                re, im = full(dve, "uf", kt, 0), None
                yr, yi = YR[:, kt, :], YI[:, kt, :]
                if kt == 0:
                    have(dve, "kf", NT - 1, 1)
                link(dve.tensor_tensor(yr, re[:, :], KR[:, kt, :], ALU.mult))
                drain(dve.tensor_tensor(yi, re[:, :], KI[:, kt, :], ALU.mult), "uf", kt, 0)
                im = full(dve, "uf", kt, 1)
                link(dve.tensor_tensor(ytmp[:, 0, :], im[:, :], KI[:, kt, :], ALU.mult))
                drain(dve.tensor_tensor(ytmp[:, 1, :], im[:, :], KR[:, kt, :], ALU.mult), "uf", kt, 1)
                have(dve, "uf", kt, 1)
                link(dve.tensor_tensor(yr, yr, ytmp[:, 0, :], ALU.subtract))
                dve.tensor_tensor(yi, yi, ytmp[:, 1, :], ALU.add).then_inc(y_ok, 1)
                dve.wait_ge(y_ok, kt + 1)
            for j in range(NA_FIRST, N_ADA):
                ada(j)
            for q in m_out:
                dve.wait_ge(q, 8 * (N_ADA - NA_FIRST))
            perm = "p (b r c) -> p r b c"
            for cb in range(CB):
                b = full(dve, "inv", cb)
                drain(dve.scalar_tensor_tensor(out=t1[:, cb % 2, 0:LAT], in0=z[:, cb, 0:LAT], scalar=chn[:, 0, cb:cb + 1],
                                               in1=b[:, :], op0=ALU.mult, op1=ALU.add), "inv", cb)
                have(dve, "inv", cb)
                nat = "p (r b c) -> p r b c"
                link(dve.tensor_tensor(hyoT[:, cb, 0:LAT].rearrange(perm, r=ROWS, c=NA_COLS),
                                       t1[:, cb % 2, 0:LAT].rearrange(nat, r=ROWS, c=NA_COLS),
                                       x0[:, cb, 0:LAT].rearrange(nat, r=ROWS, c=NA_COLS), ALU.mult))
            b = full(dve, "invp")
            for cb in range(CB):
                ins = dve.scalar_tensor_tensor(out=t1[:, cb % 2, cb // 2 * P:cb // 2 * P + P], in0=z[:, cb, LAT + 1:LAT + 1 + CTX],
                                               scalar=chn[:, 0, cb:cb + 1], in1=b[:, cb * P:(cb + 1) * P],
                                               op0=ALU.mult, op1=ALU.add)
            drain(ins, "invp")
            have(dve, "invp")
            for cb in range(CB):
                dve.tensor_tensor(hyoT[:, cb, LAT:TOK], t1[:, cb % 2, cb // 2 * P:cb // 2 * P + P],
                                  x0[:, cb, LAT + 1:LAT + 1 + CTX], ALU.mult).then_inc(hyo_ok, 1)
            b = full(dve, "hst")
            drain(dve.tensor_copy(ss[:, 5, :], b[:, 0:NT]), "hst")
            have(dve, "hst")
            dve.tensor_copy(rsh[:, 1, :], ss[:, 5, :]).then_inc(hrt, 1)

            def scores(u):
                b = full(dve, "s", u)
                n = P * (1 + len(key_tiles(u // H)))
                if u >= 2:
                    dve.wait_ge(p_ok, u - 1)
                if u < CT * H:
                    dve.wait_ge(tm_ok, u + 1)
                else:
                    dve.wait_ge(tm_ok, CT * H)
                drain(dve.tensor_tensor_reduce(sc[:, u % 2, 0:n], b[:, 0:n], Tm[:, u % 3, 0:n], 1.0, -3.0e38,
                                               ALU.add, ALU.max, rmx[:, u % 4:u % 4 + 1]), "s", u)
                have(dve, "s", u)
                dve.tensor_scalar(nmx[:, u % 4:u % 4 + 1], rmx[:, u % 4:u % 4 + 1], -1.0, None, ALU.mult)\
                   .then_inc(mx_ok, 1)

            def out_tile(b):
                dve.wait_ge(p_ok, H * b + H)
                link(dve.reciprocal(rinv[:, b % 2, :], rsum[:, b % 2, :]))
                bk = full(dve, "o", b)
                drain(dve.tensor_tensor(att[:, b, :].rearrange("p (h d) -> p h d", d=DH),
                                        bk[:, :].rearrange("p (h d) -> p h d", d=DH),
                                        rinv[:, b % 2, :].unsqueeze(2).broadcast_to([P, H, DH]), ALU.mult), "o", b)

            def turned(b):
                bk = full(dve, "aT", b)
                if b == 0:
                    dve.wait_ge(kv_out, 32)
                drain(dve.tensor_tensor(attT[:, :, b * P:(b + 1) * P], bk[:, :].rearrange("p (a n) -> p a n", n=P),
                                        chn[:, 2, :].unsqueeze(2).broadcast_to([P, CB, P]), ALU.mult), "aT", b)

            for u in range(-2, NT * H + 1):
                if u + 2 < NT * H:
                    scores(u + 2)
                if u >= 1 and (u - 1) % H == H - 1:
                    out_tile((u - 1) // H)
                if u - 1 >= H and (u - 1) % H == 3:
                    turned((u - 1) // H - 1)
            turned(NT - 1)
            dve.wait_ge(att_rt, 1)
            link(dve.reciprocal(rsh[:, 0, :], ss[:, 4, :]))
            dve.wait_ge(att_rt, 2)
            link(dve.reciprocal(rsh[:, 1, :], ss[:, 6, :]))
            for b in range(NT):
                for n in range(2):
                    i = 2 * b + n
                    w = wtmp[:, i % 2, 0, :]
                    bk = full(dve, "wa", b, n)
                    if i >= 2:
                        dve.wait_ge(wt2_ok, i - 1)
                    drain(dve.tensor_scalar(w, bk[:, :], rsh[:, 0, b:b + 1], None, ALU.mult), "wa", b, n)
                    have(dve, "wa", b, n)
                    bk = full(dve, "wh", b, n)
                    drain(dve.scalar_tensor_tensor(out=w, in0=bk[:, :], scalar=rsh[:, 1, b:b + 1], in1=w,
                                                   op0=ALU.mult, op1=ALU.add), "wh", b, n)
            dve.wait_ge(mask_ok, 2)
            dve.wait_ge(sh2_in, 32)
            for b in range(NT):
                c = b // CT
                dve.wait_ge(n_rt, b + 1)
                link(dve.reciprocal(ss[:, 2, b:b + 1], ss[:, 1, b:b + 1]))
                if b >= 2:
                    full(dve, "h2T", b - 2, 1)
                    dve.wait_ge(h2_out[b % 2], 16 * (b // 2))
                link(dve.scalar_tensor_tensor(out=h2[:, b % 2, :], in0=x[:, b, :], scalar=ss[:, 2, b:b + 1],
                                              in1=G2[:, c, :], op0=ALU.mult, op1=ALU.mult))
                dve.tensor_tensor(h2[:, b % 2, :], h2[:, b % 2, :], SH2[:, c, :], ALU.add).then_inc(h2_ok, 1)
                if b == 0:
                    dve.wait_ge(in_small, 80)
                if b > 0:
                    bk = full(dve, "rt", b - 1)
                    drain(dve.tensor_tensor(lg[:, b - 1, :], bk[:, 0:NG + NE], rb[:, :], ALU.add), "rt", b - 1)
            bk = full(dve, "rt", NT - 1)
            drain(dve.tensor_tensor(lg[:, NT - 1, :], bk[:, 0:NG + NE], rb[:, :], ALU.add), "rt", NT - 1)
            have(dve, "rt", NT - 1)

            def r4(i):
                return R[:, i, :, 0:NG]

            def r1(i):
                return R[:, i, :, 0:1]

            def over4(v):
                return v.broadcast_to([P, NT, NG])

            def first_max(val, mx, out, tmp, low):
                link(dve.tensor_reduce(mx, val, AX, ALU.max))
                link(dve.tensor_tensor(out, val, over4(mx), ALU.is_equal))
                link(dve.scalar_tensor_tensor(out=tmp, in0=out, scalar=-float(NG),
                                              in1=iota[:, 0:NG].unsqueeze(1).broadcast_to([P, NT, NG]),
                                              op0=ALU.mult, op1=ALU.add))
                link(dve.tensor_reduce(low, tmp, AX, ALU.min))
                link(dve.tensor_tensor(out, tmp, over4(low), ALU.is_equal))

            gl = lg[:, :, 0:NG]
            first_max(gl, r1(2), r4(3), r4(4), r1(5))
            dve.tensor_tensor(r4(0), gl, over4(r1(2)), ALU.subtract).then_inc(route_e, 1)
            el = lg[:, :, NG:].rearrange("p t (g j) -> p t g j", j=EPG)
            prod = R[:, 10].rearrange("p t (g j) -> p t g j", j=EPG)
            link(dve.tensor_tensor(prod, el, r4(3).unsqueeze(3).broadcast_to([P, NT, NG, EPG]), ALU.mult))
            link(dve.tensor_reduce(r4(6), prod.rearrange("p t g j -> p t j g"), AX, ALU.add))
            first_max(r4(6), r1(2), r4(7), r4(4), r1(5))
            link(dve.scalar_tensor_tensor(out=r4(6), in0=r4(7), scalar=-1.0e30, in1=r4(6), op0=ALU.mult, op1=ALU.add))
            first_max(r4(6), r1(12), r4(11), r4(4), r1(5))
            dve.tensor_tensor(r1(8), r1(12), r1(2), ALU.subtract).then_inc(route_e, 1)
            A1, A2, A = R[:, 13], R[:, 14], R[:, 15]
            for dst, j1 in ((A1, 7), (A2, 11)):
                link(dve.tensor_tensor(dst.rearrange("p t (g j) -> p t g j", j=EPG),
                                       r4(3).unsqueeze(3).broadcast_to([P, NT, NG, EPG]),
                                       r4(j1).unsqueeze(2).broadcast_to([P, NT, NG, EPG]), ALU.mult))
            dve.tensor_tensor(A, A1, A2, ALU.add).then_inc(assigned, 1)
            dve.wait_ge(route_a, 2)
            link(dve.tensor_reduce(r1(5), r4(1), AX, ALU.add))
            link(dve.reciprocal(r1(5), r1(5)))
            link(dve.tensor_scalar(r1(2), r1(9), 1.0, None, ALU.add))
            link(dve.reciprocal(r1(2), r1(2)))
            w1 = wts[:, 0, :].unsqueeze(2)
            link(dve.tensor_tensor(w1, r1(2), r1(5), ALU.mult))
            link(dve.tensor_tensor(wts[:, 1, :].unsqueeze(2), w1, r1(9), ALU.mult))
            bk = full(dve, "rank")
            rk = R[:, 10]
            drain(dve.tensor_copy(rk, bk[:, 0:NT * NE].rearrange("p (t e) -> p t e", e=NE)), "rank")
            have(dve, "rank")
            link(dve.scalar_tensor_tensor(out=rankm[:, :, :], in0=rk, scalar=1.0, in1=A, op0=ALU.add, op1=ALU.mult))
            link(dve.tensor_scalar(rankm[:, :, :], rankm[:, :, :], -1.0, None, ALU.add))
            row, more = R[:, 9], R[:, 11]
            link(dve.scalar_tensor_tensor(out=row, in0=iota[:, 0:NE].unsqueeze(1).broadcast_to([P, NT, NE]),
                                          scalar=float(P), in1=rk, op0=ALU.mult, op1=ALU.add))
            for p in range(1, NT):
                link(dve.tensor_scalar(more, rk, float(p * CAP), float(NE * P - CAP), ALU.is_ge, ALU.mult))
                link(dve.tensor_tensor(row, row, more, ALU.add))
            for k, Ak in enumerate((A1, A2)):
                link(dve.tensor_tensor(Ak, Ak, row, ALU.mult))
                link(dve.tensor_reduce(posf[:, k, :].unsqueeze(2), Ak, AX, ALU.add))
            link(dve.tensor_copy(posi[:, :, :], posf[:, :, :]))
            bk = full(dve, "total")
            drain(dve.tensor_reduce(R[:, 12, 0, 0:1], bk[:, 0:NE], AX, ALU.max), "total")
            have(dve, "total")
            dve.wait_ge(consts_ok, 2)
            dve.tensor_scalar(over[0:1, 0:1], R[0:1, 12, 0, 0:1], float(CAP), None, ALU.is_gt).then_inc(route_ok, 1)

            def slots_of(n, e, s):
                wait_past(dve, idx_full, n - 1)
                dve.tensor_tensor(sel[:, s], iota[:, :].unsqueeze(1).broadcast_to([P, NT, P]),
                                  rankm[:, :, bass.ds(e, 1)].broadcast_to([P, NT, P]), ALU.is_equal).then_inc(sel_ok, 1)

            def numbers(n, s):
                dve.wait_ge(idx_full, n + 1)
                wait_past(dve, xg_in[s], (n - s) * 8)
                dve.tensor_copy(idx[:, s:s + 1], bank[7][:, 0:1]).then_inc(idx_ok, 1)

            def rows_turned(n, s):
                for g in range(2):
                    dve.wait_ge(xgT_full, n * 2 + (g + 1))
                    dve.tensor_copy(xgT[:, s, 4 * g:4 * g + 4, :].rearrange("p a b -> p (a b)"), bank[g][:, :])\
                       .then_inc(xgT_ok, 1)

            def expert(p, i, s, ahead2, ahead1):
                n = (i + p * pairs) * 2 + s
                if ahead2:
                    slots_of(n + 2, i * 2 + (s + 2), s)
                dve.wait_ge(gu_full, n * 2 + 2)
                dve.wait_ge(sil_ok, n + 1)
                dve.tensor_tensor(hid[:, s, :], sil, bank[3][:, :], ALU.mult).then_inc(hid_ok, 1)
                if ahead2:
                    numbers(n + 2, s)
                if ahead1:
                    rows_turned(n + 1, 1 - s)
                dve.wait_ge(y_full, n * 2 + 2)
                wait_past(dve, y_out[s], (i + p * pairs) * 16)
                dve.tensor_copy(yout[:, s, 512:1024], bank[6][:, :]).then_inc(y_cpD, 1)

            def one_pass(p):
                for s in range(2):
                    slots_of(p * NE + s, s, s)
                    numbers(p * NE + s, s)
                rows_turned(p * NE, 0)
                for s in range(2):
                    expert(p, 0, s, True, True)
                with dve.Fori(1, pairs - 1) as i:
                    for s in range(2):
                        expert(p, i, s, True, True)
                for s in range(2):
                    expert(p, pairs - 1, s, False, s == 0)
            one_pass(0)
            v = dve.value_load(over[0:1, 0:1])
            with dve.If(v > 0):
                with dve.Fori(1, NT) as p:
                    dve.tensor_scalar(rankm[:, :, :], rankm[:, :, :], -float(CAP), None, ALU.add).then_inc(shifted, 1)
                    dve.wait_ge(shifted, p)
                    one_pass(p)
            dve.wait_ge(tail_in, 48)
            for t in range(NT + 1):
                if t < NT:
                    u, c = ya[:, t % 2, :], t // CT
                    dve.wait_ge(yab_in[t % 2], 32 * (t // 2 + 1))
                    link(dve.tensor_scalar(u, u, wts[:, 0, t:t + 1], None, ALU.mult))
                    link(dve.scalar_tensor_tensor(out=u, in0=yb[:, t % 2, :], scalar=wts[:, 1, t:t + 1], in1=u,
                                                  op0=ALU.mult, op1=ALU.add))
                    link(dve.tensor_tensor(u, u, gt2[:, c, :], ALU.mult))
                    dve.tensor_tensor(x[:, t, :], x[:, t, :], u, ALU.add).then_inc(f_cmb, 1)
                if t > 0:
                    q = t - 1
                    dve.wait_ge(f_rt, t)
                    link(dve.reciprocal(ss[:, 2, q:q + 1], ss[:, 1, q:q + 1]))
                    dve.scalar_tensor_tensor(out=x[:, q, :], in0=x[:, q, :], scalar=ss[:, 2, q:q + 1], in1=fg,
                                             op0=ALU.mult, op1=ALU.mult).then_inc(f_ok, 1)

        @block.tensor
        def _(pe):
            def open_bank(*name):
                j = JOB[name]
                prev = [q for q in range(j) if JOBS[q][1] == JOBS[j][1]]
                if prev:
                    have(pe, *JOBS[prev[-1]][0])
                return bank[JOBS[j][1]]

            def close(ins):
                ins.then_inc(pe_full, 1)

            def group(out, terms, start=True):
                for i, (l, r) in enumerate(terms):
                    ins = pe.matmul(out, l, r, start=(i == 0), stop=(i == len(terms) - 1))
                return ins

            def chunk(c, again=0):
                i = FIRST_USE[c][again]
                pe.wait_ge(chunk_in[i % NRING], 16 * (i // NRING + 1))
                return slot[i % NRING]

            def turn(out, src):
                return pe.transpose(out, src, ident[:, :])

            pe.wait_ge(consts_ok, 2)
            pe.wait_ge(in_mlp, 80)
            for layer in range(2):
                src, k = (zf, EMB) if layer == 0 else (mh[0], FF)
                if layer:
                    pe.wait_ge(sin_ok, 1)
                for i, (lo, hi) in enumerate(((0, LAT), (LAT, TOK))):
                    b = open_bank(f"mlp{layer + 1}", i)
                    close(pe.matmul(b[0:FF, 0:hi - lo], w12[0:k, layer, :], src[0:k, lo:hi], start=True, stop=True))
            pe.wait_ge(sin_ok, 2)
            for t in range(NT):
                for d in range(2):
                    b = open_bank("filt", t, d)
                    close(pe.matmul(b[:, :], mh[1][0:FF, t * P:(t + 1) * P], mw3[0:FF, d * CH:(d + 1) * CH],
                                    start=True, stop=True))
            pe.wait_ge(in_ctx, 16)
            b = open_bank("ckT")
            for cb in range(CB):
                ins = turn(b[:, cb * P:(cb + 1) * P], craw[:, cb * P:(cb + 1) * P])
            close(ins)
            pe.wait_ge(filt_ok, 2 * NT)
            F = chunk(("dft",)).rearrange("p (a t k) -> p a t k", a=2, k=LAT)
            pe.wait_ge(in_dft, 16)
            for kt in range(NT):
                for ri, src in enumerate((s_flt, d_flt)):
                    b = open_bank("kf", kt, ri)
                    if kt < CT:
                        ins = group(b[:, :], [(F[:, ri, t, kt * P:(kt + 1) * P], src[:, t, :]) for t in range(CT)])
                        close(ins)
                    else:
                        ins = pe.matmul(b[:, :], dftp[:, ri, :], src[:, CT, :], start=True, stop=True)
                        close(ins)

            def col(j):
                if j == 0:
                    open_bank("mcol")
                have(pe, "ada", j)
                b = bank[JOBS[JOB[("mcol",)]][1]]
                for q in range(4):
                    o = (4 * j + q) * 2
                    ins = pe.matmul(b[:, o:o + 2], mrow[0][:, j % 2, q * P:(q + 1) * P], ident[0:2, 0:2],
                                    start=True, stop=True)
                if j < NA_FIRST - 1:
                    ins.then_inc(mrow_used, 1)
                else:
                    close(ins)

            def ada(j):
                W = chunk(("ada", j)).rearrange("p (k n) -> p k n", n=512)
                b = open_bank("ada", j)
                close(group(b[0:2, :], [(scond[:, k, :], W[:, k, :]) for k in range(KT)]))

            pe.wait_ge(cond_ok, 1)
            for j in range(NA_FIRST):
                ada(j)
                if j >= 1:
                    col(j - 1)
            col(NA_FIRST - 1)
            pe.wait_ge(xn_ok, NT)
            for k in range(KT):
                b = open_bank("xT", k)
                for t in range(CT):
                    ins = turn(b[:, t * P:(t + 1) * P], xn[:, t, k * P:(k + 1) * P])
                close(ins)
            for g in range(2):
                b = open_bank("xTp", g)
                for j in range(4):
                    k = 4 * g + j
                    ins = turn(b[:, j * P:(j + 1) * P], xn[:, CT, k * P:(k + 1) * P])
                close(ins)

            def project(job, jobp, W):
                for cb in range(CB):
                    b = open_bank(*job, cb)
                    close(group(b[:, :], [(W[:, k, cb * P:(cb + 1) * P], hT[:, k, 0:LAT]) for k in range(KT)]))
                b = open_bank(*jobp)
                for cb in range(CB):
                    ins = group(b[:, cb * P:(cb + 1) * P],
                                [(W[:, k, cb * P:(cb + 1) * P], hT[:, k, LAT:TOK]) for k in range(KT)])
                close(ins)

            have(pe, "xTp", 1)
            for c in range(3):
                project(("hy", c), ("hyp", c), chunk(("win", HY[c])).rearrange("p (k n) -> p k n", n=512))
            pe.wait_ge(z_ok, CB)
            for t in range(NT):
                b = open_bank("zT", t)
                lo = t * P if t < CT else LAT + 1
                for cb in range(CB):
                    ins = turn(b[:, cb * P:(cb + 1) * P], z[:, cb, lo:lo + P])
                close(ins)
            have(pe, "zT", NT - 1)
            F = chunk(("dft",), 1).rearrange("p (a t k) -> p a t k", a=2, k=LAT)
            for kt in range(NT):
                for ri in range(2):
                    b = open_bank("uf", kt, ri)
                    if kt < CT:
                        close(group(b[:, :], [(F[:, ri, t, kt * P:(kt + 1) * P], zt[:, t, :]) for t in range(CT)]))
                    else:
                        close(pe.matmul(b[:, :], dftp[:, ri, :], zt[:, CT, :], start=True, stop=True))
            for j in range(NA_FIRST, N_ADA):
                ada(j)
            pe.wait_ge(y_ok, NT)
            F = chunk(("idft",)).rearrange("p (a t k) -> p a t k", a=2, k=LAT)
            for cb in range(CB):
                b = open_bank("inv", cb)
                close(group(b[:, :], [(Y[:, kt, cb * P:(cb + 1) * P], F[:, ri, kt, :])
                                      for ri, Y in enumerate((YR, YI)) for kt in range(CT)]))
            b = open_bank("invp")
            for cb in range(CB):
                ins = group(b[:, cb * P:(cb + 1) * P], [(Y[:, CT, cb * P:(cb + 1) * P], dftp[:, 2 + ri, :])
                                                        for ri, Y in enumerate((YR, YI))])
            close(ins)
            b = open_bank("hst")
            pe.wait_ge(hsq_ok, CB)
            for t in range(NT):
                ins = group(b[:, t:t + 1], [(sq[:, cb, t * P:(t + 1) * P], ones[:, 0:1]) for cb in range(CB)])
            close(ins)
            for ch, w in (("q", WQ), ("k", WK)):
                project((ch,), (ch + "p",), chunk(("win", w)).rearrange("p (k n) -> p k n", n=512))
            W = chunk(("win", WV)).rearrange("p (k n) -> p k n", n=512)
            for t in range(NT):
                b = open_bank("V", t)
                close(group(b[:, :], [(hT[:, k, t * P:(t + 1) * P], W[:, k, :]) for k in range(KT)]))
            have(pe, "kp")
            b = open_bank("nk")
            for cb in range(CB):
                ins = turn(b[:, cb * P:(cb + 1) * P], KTt[:, cb, LAT:TOK])
            close(ins)
            have(pe, "V", NT - 1)
            pe.wait_ge(in_ctx, 32)

            def scores(u):
                b, h = u // H, u % H
                hp, pair = h % 2 * DH, h // 2
                bk = open_bank("s", u)
                q = QT[hp:hp + DH, pair, b * P:(b + 1) * P]
                kc = ckT[hp:hp + DH, pair, :] if b < CT else KTt[hp:hp + DH, pair, LAT:TOK]
                ins = pe.matmul(bk[:, 0:P], q, kc, start=True, stop=True)
                kts = key_tiles(b)
                if kts:
                    ins = pe.matmul(bk[:, P:P * (1 + len(kts))], q,
                                    KTt[hp:hp + DH, pair, kts[0] * P:(kts[-1] + 1) * P], start=True, stop=True)
                close(ins)

            def turn_probs(u):
                bk = open_bank("pt", u)
                pe.wait_ge(p_ok, u + 1)
                for j in range(1 + len(key_tiles(u // H))):
                    ins = turn(bk[:, j * P:(j + 1) * P], pr[:, u % 2, j * P:(j + 1) * P])
                close(ins)

            def values(u):
                b, h = u // H, u % H
                cols = slice(h * DH, (h + 1) * DH)
                if h == 0:
                    open_bank("o", b)
                have(pe, "pt", u)
                vs = [cv[:, cols]] if b < CT else [V[:, CT, cols]]
                vs += [V[:, t, cols] for t in key_tiles(b)]
                ins = group(bank[6][:, cols], [(PT[:, u % 2, j, :], v) for j, v in enumerate(vs)])
                if h == H - 1:
                    close(ins)
                else:
                    ins.then_inc(pv_ok, 1)

            def turn_att(b):
                bk = open_bank("aT", b)
                have(pe, "o", b)
                for cb in range(CB):
                    ins = turn(bk[:, cb * P:(cb + 1) * P], att[:, b, cb * P:(cb + 1) * P])
                close(ins)

            for u in range(-2, NT * H + 1):
                if u + 2 < NT * H:
                    scores(u + 2)
                if 0 <= u < NT * H:
                    turn_probs(u)
                if u >= 1:
                    values(u - 1)
                if u - 1 >= H and (u - 1) % H == 3:
                    turn_att((u - 1) // H - 1)
            turn_att(NT - 1)
            Ws = [chunk(("wout", n)).rearrange("p (k n) -> p k n", n=512) for n in range(2)]
            pe.wait_ge(hg_ok, CB)
            have(pe, "aT", NT - 1)
            for b in range(NT):
                for n in range(2):
                    for job, src, k0 in (("wa", attT, 0), ("wh", hyoT, CB)):
                        bk = open_bank(job, b, n)
                        close(group(bk[:, :], [(src[:, cb, b * P:(b + 1) * P], Ws[n][:, k0 + cb, :])
                                               for cb in range(CB)]))
            for b in range(NT):
                pe.wait_ge(h2_ok, b + 1)
                if b == 0:
                    pe.wait_ge(in_small, 80)
                for g in range(2):
                    bk = open_bank("h2T", b, g)
                    for j in range(4):
                        ins = turn(bk[:, j * P:(j + 1) * P], h2[:, b % 2, (4 * g + j) * P:(4 * g + j + 1) * P])
                    close(ins)
                have(pe, "h2T", b, 1)
                bk = open_bank("rt", b)
                close(group(bk[:, 0:NG + NE], [(h2T[:, b % 2, k, :], rw[:, k, :]) for k in range(KT)]))
            A = R[:, 15]
            pe.wait_ge(assigned, 1)
            bk = open_bank("rank")
            for t in range(NT):
                ins = group(bk[:, t * NE:(t + 1) * NE], [(ones[:, :], A[:, q, :]) for q in range(t)] + [(tri[:, :], A[:, t, :])])
            close(ins)
            bk = open_bank("total")
            close(group(bk[:, 0:NE], [(ones[:, :], A[:, t, :]) for t in range(NT)]))
            have(pe, "rank")
            have(pe, "total")

            def numbers(n, s):
                pe.wait_ge(sel_ok, n + 1)
                wait_past(pe, idx_ok, n)
                group(bank[7][:, 0:1], [(sel[:, s, t, :], tid[:, t:t + 1]) for t in range(NT)]).then_inc(idx_full, 1)

            def turn_rows(n, s):
                pe.wait_ge(xg_in[s], (n - s) * 8 + 16)
                wait_past(pe, xgT_ok, n * 2)
                for g in range(2):
                    for j in range(4):
                        ins = turn(bank[g][:, j * P:(j + 1) * P], xg[:, s, (4 * g + j) * P:(4 * g + j + 1) * P])
                    ins.then_inc(xgT_full, 1)

            def expert(p, i, s, ahead2, ahead1):
                n = (i + p * pairs) * 2 + s
                w = [slot[3 * s + j].rearrange("p (k n) -> p k n", n=512 if j < 2 else D) for j in range(3)]
                arrived = (n - s) * 8 + 16
                pe.wait_ge(xgT_ok, n * 2 + 2)
                for j, freed in ((0, sil_ok), (1, hid_ok)):
                    wait_past(pe, freed, n)
                    pe.wait_ge(ew_in[3 * s + j], arrived)
                    group(bank[2 + j][:, :], [(xgT[:, s, k, :], w[j][:, k, :]) for k in range(KT)]).then_inc(gu_full, 1)
                if ahead2:
                    numbers(n + 2, s)
                if ahead1:
                    turn_rows(n + 1, 1 - s)
                pe.wait_ge(hid_ok, n + 1)
                for f in range(FE // P):
                    ins = turn(bank[4][:, f * P:(f + 1) * P], hid[:, s, f * P:(f + 1) * P])
                ins.then_inc(hidT_full, 1)
                pe.wait_ge(hidT_ok, n + 1)
                pe.wait_ge(ew_in[3 * s + 2], arrived)
                for half, freed in ((0, y_cpA), (1, y_cpD)):
                    wait_past(pe, freed, n)
                    group(bank[5 + half][:, :], [(hidT[:, s, f, :], w[2][:, f, half * 512:(half + 1) * 512])
                                                 for f in range(FE // P)]).then_inc(y_full, 1)

            def one_pass(p):
                for s in range(2):
                    numbers(p * NE + s, s)
                turn_rows(p * NE, 0)
                for s in range(2):
                    expert(p, 0, s, True, True)
                with pe.Fori(1, pairs - 1) as i:
                    for s in range(2):
                        expert(p, i, s, True, True)
                for s in range(2):
                    expert(p, pairs - 1, s, False, s == 0)
            one_pass(0)
            pe.wait_ge(route_ok, 1)
            v = pe.value_load(over[0:1, 0:1])
            with pe.If(v > 0):
                with pe.Fori(1, NT) as p:
                    one_pass(p)


def constants():
    f = np.float32
    feats, decs = [], []
    lo, hi = math.log(1e-2) / 1.5, math.log(1e-2) / 0.3
    deltas = np.abs(np.linspace(lo, hi, CH))
    fb = np.linspace(1e-4, 15, 16)[:, None]
    for L in (LAT, CTX):
        t = np.linspace(0.0, 1.0, L)[None, :]
        w = 2.0 * np.pi * np.arange(L)[None, :] / L
        feats.append(np.concatenate([t, np.cos(fb * w), -np.sin(fb * w)], axis=0))
        decs.append(np.exp(-t.T * deltas[None, :]))
    bmask = np.ones((P, NT))
    bmask[0, 0] = bmask[0, CT] = 0.0

    def transforms(L):
        n, k = np.arange(L)[:, None], np.arange(L)[None, :]
        th = np.pi * ((2 * k + 1) * n % (4 * L)) / (2 * L) * 1.0
        th = 2 * np.pi * ((2 * k + 1) * n % (4 * L)) / (4 * L)
        return np.cos(th), -np.sin(th)

    def tiles(m):
        return m.reshape(-1, P, m.shape[1]).transpose(1, 0, 2)
    c, s = transforms(LAT)
    dft = np.stack([np.stack([tiles(c), tiles(s)], 1).reshape(P, -1),
                    np.stack([tiles(c.T / LAT), tiles(s.T / LAT)], 1).reshape(P, -1)])
    c, s = transforms(CTX)
    dftp = np.stack([c, s, c.T / CTX, s.T / CTX], 1)
    maskb = np.full((P, 3, 3 * NA_COLS), -1e30)
    for kind, b in enumerate((0, 1, LAT // P - 1)):
        for p in range(P):
            qc = b * NA_COLS + p % NA_COLS
            cs = min(max(qc - NA_COLS // 2, 0), GRID_W - NA_COLS)
            kc = (b - 1) * NA_COLS + np.arange(3 * NA_COLS)
            maskb[p, kind, (kc >= cs) & (kc < cs + NA_COLS)] = 0.0
    return {
        "zf": np.concatenate(feats, 1).astype(f), "dec": np.concatenate(decs, 0).astype(f),
        "bmask": bmask.astype(f), "dft": dft.astype(f), "dftp": dftp.astype(f), "maskb": maskb.astype(f),
        "iota": np.tile(np.arange(P, dtype=np.float16), (P, 1)),
        "tid": (np.arange(NT)[None, :] * P + np.arange(P)[:, None]).astype(np.float16),
    }


def kernel(**inp):
    import concourse.bacc as bacc
    from concourse.bass_utils import run_bass_kernel_spmd

    g = {k: np.asarray(v) for k, v in inp.items()}

    def cols(v):
        return v.reshape(-1, P).T
    latent = g["x_sample"][0].reshape(ROWS, CT, NA_COLS, D).transpose(1, 0, 2, 3).reshape(LAT, D)
    taps = np.stack([*g["conv_w"][0], g["conv_b"][0]], 0)
    padded = np.pad(g["rpb"][0], ((0, 0), (0, 0), (NA_COLS, NA_COLS)))
    shifted = np.stack([padded[:, :, NA_COLS - 1 - c:4 * NA_COLS - 1 - c] for c in range(NA_COLS)], 0)
    arrays = {
        "x": np.concatenate([latent, g["x_prompt"][0]], 0),
        "cond": np.stack([cols(g["c"][0]), cols(g["c_ctx"])], 2),
        "ck": g["cache_k"][0, 0].reshape(CTX, CH), "cv": g["cache_v"][0, 0].reshape(CTX, CH),
        "w_ada": g["w_ada"][0], "b2": np.broadcast_to(g["b_ada"], (2, 6 * D)), "w_in": g["w_in"][0],
        "w_out": g["w_out"][0], "w_gate": g["w_gate"][0], "w_up": g["w_up"][0], "w_down": g["w_down"][0],
        "g1c": cols(g["norm1_g"][0]), "g2": g["norm2_g"][0], "fg": g["final_g"],
        "cwb": np.stack([taps[:, (c - WX0) * CH:(c - WX0 + 1) * CH].reshape(4, CB, P).transpose(2, 1, 0) for c in HY], 1),
        "chn": np.stack([cols(g["hyena_skip"][0]), cols(g["gnorm_hyena"][0]), cols(g["gnorm_att"][0])], 1),
        "w1": g["filt_w1"][0], "w2": g["filt_w2"][0], "w3": g["filt_w3"][0],
        "mlp_c": np.stack([g["filt_b1"][0], g["filt_b2"][0], g["filt_freq"][0]], 1),
        "rw": np.concatenate([g["router_grp_w"][0], g["router_exp_w"][0]], 1),
        "rb": np.concatenate([g["router_grp_b"][0], g["router_exp_b"][0]], 0),
        "rpb": shifted.reshape(NA_COLS, H, -1),
        **constants(),
    }
    nc = bacc.Bacc("TRN2", target_bir_lowering=False, num_devices=1)
    a, sent = {}, {}
    for name, v in arrays.items():
        v = np.ascontiguousarray(v)
        sent["in_" + name] = v
        a[name] = nc.dram_tensor("in_" + name, v.shape, mybir.dt.from_np(v.dtype), kind="ExternalInput").ap()
    shapes = {"y": (TOK, D), "k": (CTX, CH), "v": (CTX, CH)}
    outs = {n: nc.dram_tensor("out_" + n, s, F32, kind="ExternalOutput").ap() for n, s in shapes.items()}
    program(nc, a, outs)
    r = run_bass_kernel_spmd(nc, [sent], core_ids=[0]).results[0]
    y = r["out_y"]
    ys = y[:LAT].reshape(CT, ROWS, NA_COLS, D).transpose(1, 0, 2, 3).reshape(1, LAT, D)
    kv = (1, 1, CTX, H, DH)
    return y[LAT:].reshape(1, CTX, D), ys, r["out_k"].reshape(kv), r["out_v"].reshape(kv)
```

```python
import math
from contextlib import ExitStack

import numpy as np

import concourse.bass as bass
from concourse import mybir

F32 = mybir.dt.float32
F16 = mybir.dt.float16
I32 = mybir.dt.int32
U32 = mybir.dt.uint32
ALU = mybir.AluOpType
ACT = mybir.ActivationFunctionType
AX = mybir.AxisListType.X

P = 128
D = 1024
KT = D // P
LAT, CTX = 512, 128
TOK = LAT + CTX
NT = TOK // P
CT = NT - 1
H, DH = 8, 64
CH = 512
CB = CH // P
GRID_W, NA_ROWS, NA_COLS = 64, 8, 16
ROWS = LAT // GRID_W
FF, EMB = 64, 33
NG, EPG = 4, 4
NE = NG * EPG
FE = 512
EPS = 1e-6
TWO_PI = 2.0 * math.pi
ROUND = 1.5 * 2.0 ** 23
PI_A = float(np.float32(6.28125))
PI_B = float(np.float32(np.float32(1.9353071795e-3) * 1.0))
PI_B = float(np.floor(PI_B * 2 ** 22) / 2 ** 22)
PI_C = float(np.float32(TWO_PI - PI_A - PI_B))
CAP = 128

WQ, WK, WV, WX0, WX1, WVH = range(6)
HY = [WVH, WX1, WX0]
NA_FIRST = 4
N_ADA = 12


def key_tiles(b):
    return [t for t in (b - 1, b, b + 1) if 0 <= t < CT] if b < CT else []


def psum_jobs():
    jobs = []
    turn = [0]

    def add(name, eng, bank=None):
        if bank is None:
            bank = turn[0] % 6
            turn[0] += 1
        jobs.append((name, bank, eng))

    for layer in range(2):
        for i in range(2):
            add((f"mlp{layer + 1}", i), "dve")
        if layer == 0:
            add(("ckT",), "act")
        add(("ada", layer), "dve")
    for t in range(NT):
        for d in range(2):
            add(("filt", t, d), "dve")
    for j in range(2, NA_FIRST):
        add(("ada", j), "dve")
    add(("mcol",), "dve", 6)
    for kt in range(NT):
        for ri in range(2):
            add(("kf", kt, ri), "act")
    for k in range(KT):
        add(("xT", k), "dve")
    for g in range(2):
        add(("xTp", g), "dve")
    for c in range(3):
        for cb in range(CB):
            add(("hy", c, cb), "act")
        add(("hyp", c), "act")
    for t in range(NT):
        add(("zT", t), "act")
    for kt in range(NT):
        for ri in range(2):
            add(("uf", kt, ri), "dve")
    for j in range(NA_FIRST, N_ADA):
        add(("ada", j), "dve")
    for cb in range(CB):
        add(("inv", cb), "dve")
    add(("invp",), "dve")
    add(("hst",), "dve")
    for c in "qk":
        for cb in range(CB):
            add((c, cb), "act")
        add((c + "p",), "act")
    for t in range(NT):
        add(("V", t), "act")
    add(("nk",), "act")
    units = [(b, h) for b in range(NT) for h in range(H)]
    for u in range(-2, len(units) + 1):
        if u + 2 < len(units):
            add(("s", u + 2), "dve", (u + 2) % 3)
        if 0 <= u < len(units):
            add(("pt", u), "act", 3 + u % 3)
        if u >= 1 and (u - 1) % H == H - 1:
            add(("o", (u - 1) // H), "dve", 6)
        if u - 1 >= H and (u - 1) % H == 3:
            add(("ast", (u - 1) // H - 1), "dve", 7)
    add(("ast", NT - 1), "dve", 7)
    turn[0] = 0
    for b in range(NT + 1):
        if b < NT:
            for n in range(2):
                add(("wa", b, n), "dve")
                add(("wh", b, n), "dve")
        if b > 0:
            for g in range(2):
                add(("h2T", b - 1, g), "act")
            add(("rt", b - 1), "dve", 6)
    add(("rank",), "dve", 7)
    add(("total",), "dve", 6)
    return jobs


JOBS = psum_jobs()
JOB = {name: i for i, (name, _, _) in enumerate(JOBS)}
ORD = {}
for _name, _bank, _eng in JOBS:
    ORD[_name] = 1 + sum(1 for n in ORD if JOBS[JOB[n]][2] == _eng)

CHUNKS = ([("ada", j) for j in range(NA_FIRST)] + [("dft",)] + [("win", c) for c in HY] + [("dft",)]
          + [("ada", j) for j in range(NA_FIRST, N_ADA)] + [("idft",)]
          + [("win", c) for c in (WQ, WK, WV)] + [("wout", n) for n in range(2)])
NRING = 4
NCH = len(CHUNKS)
ESLOTS = 6
HYROW = range(3)


def last_jobs():
    seen, out = 0, []
    for c in CHUNKS:
        if c[0] == "dft":
            out.append(("kf", CT - 1, 1) if seen == 0 else ("uf", CT - 1, 1))
            seen += 1
        elif c[0] == "ada":
            out.append(c)
        elif c[0] == "idft":
            out.append(("inv", CB - 1))
        elif c[0] == "wout":
            out.append(("wh", NT - 1, c[1]))
        elif c[1] in HY:
            out.append(("hyp", HY.index(c[1])))
        else:
            out.append({WQ: ("qp",), WK: ("kp",), WV: ("V", NT - 1)}[c[1]])
    return out


LAST_JOB = last_jobs()
FIRST_USE = {}
for _i, _c in enumerate(CHUNKS):
    FIRST_USE.setdefault(_c, []).append(_i)


def program(nc, a, outs):
    ctx = ExitStack()
    with ctx:
        def sb(name, shape, dt=F32):
            return ctx.enter_context(nc.sbuf_tensor(name, shape, dt))

        def sem(name):
            return ctx.enter_context(nc.semaphore(name))

        bank = [ctx.enter_context(nc.psum_tensor(f"bank{i}", [P, 512], F32)) for i in range(8)]
        KB = 256
        big = sb("big", [P, 198 * KB])

        def at(kb, *shape):
            n = int(np.prod(shape))
            v = big[:, int(kb * KB):int(kb * KB) + n]
            if len(shape) == 1:
                return v
            names = "abcd"[:len(shape)]
            return v.rearrange(f"p ({' '.join(names)}) -> p {' '.join(names)}",
                               **{x: s for x, s in zip(names[1:], shape[1:])})

        slot_kb = [0, 16, 32, 48, 164, 180]
        slot = [at(kb, 4096) for kb in slot_kb]
        x = at(64, NT, D)
        hT = at(84, KT, TOK)
        s_flt, d_flt = at(104, NT, CH), at(114, NT, CH)
        dec = at(124, NT, CH)
        zf = at(134, TOK)
        mw3 = at(136.5, 2 * CH)
        mh = [at(140.5, TOK), at(143, TOK)]
        KR, KI = at(147, NT, CH), at(157, NT, CH)
        mtmp = [at(167, TOK), at(169.5, TOK)]
        fbuf = at(172, 2, CH)
        xn = at(178, NT, D)
        UW = 644
        ustrip = at(104, CB, UW)
        z = at(114.25, CB, UW)
        x0 = at(124.5, CB, UW)
        ctmp = at(134.75, 2, UW)
        zt = at(178, NT, CH)
        YR, YI = at(188, NT, CH), at(167, NT, CH)
        ytmp = at(140, 2, CH)
        hyoT = at(104, CB, TOK)
        sq = at(178, CB, TOK)
        t1 = at(140, 2, TOK)
        QT, KTt = at(114.25, CB, TOK), at(124.5, CB, TOK)
        V = at(134.75, NT, CH)
        nkb = at(188, CH)
        base = at(145, H, NA_ROWS, 3 * NA_COLS)
        Tm = at(157, 3, 512)
        pr = at(164, 2, 512)
        PT = at(168, 2, 4, P)
        sc = at(172, 2, 512)
        oraw = at(176, 2, CB, P)
        osq = at(184, CB, P)
        osum = at(163, 2, P)
        attT = at(186, CB, TOK)
        gt1 = at(84, 2, D)
        G2 = at(92, 2, D)
        SH2 = [at(180, D), at(100, D)]
        wtmp = at(122.25, 2, 2, 512)
        h2 = at(130.5, 2, D)
        h2T = at(138.5, 2, KT, P)
        xg = at(84, 2, D)
        xgT = at(92, 2, KT, P)
        hid = at(100, 2, FE)
        hidT = at(104, 2, FE // P, P)
        sil = at(108, FE)
        yout = at(110, 2, D)
        gt2 = at(118, 2, D)
        fg = at(126, D)
        ya, yb = at(0, NT, D), at(20, NT, D)
        sqd = at(147, D)

        ident = sb("ident", [P, P])
        b_buf = [at(147, 2, 512)[0:2], at(104, 2, 512)[0:2]]
        mrow = [at(151, 2, 512)[0:2], at(108, 2, 512)[0:2]]
        g2row = at(112, 512)[0:2]
        ckT = sb("ckT", [P, CB, P])
        craw = at(176, CH)
        cv = at(196, CH)
        cond = sb("cond", [P, KT, 2])
        scond = sb("scond", [P, KT, 2])
        csig = sb("csig", [P, KT, 2])
        mcol = sb("mcol", [P, 2, KT, 2])
        g1c = sb("g1c", [P, KT])
        cwb = sb("cwb", [P, 3, CB, 4])
        chn = sb("chn", [P, 3, CB])
        mlp_c = sb("mlp_c", [FF, 3])
        mlp_f = sb("mlp_f", [FF, 2])
        w12 = sb("w12", [FF, 2, FF])
        bmask = sb("bmask", [P, NT])
        maskb = sb("maskb", [P, 3, 3 * NA_COLS])
        dftp = sb("dftp", [P, 4, P])
        ones = sb("ones", [P, P])
        tri = sb("tri", [P, P])
        iota = sb("iota", [P, P], F16)
        tid = sb("tid", [P, NT], F16)
        rw = sb("rw", [P, KT, NG + NE])
        rb = sb("rb", [P, NG + NE])
        ss = sb("ss", [P, 8, NT])
        rmx = sb("rmx", [P, 4])
        nmx = sb("nmx", [P, 4])
        rsum = sb("rsum", [P, 4])
        rinv = sb("rinv", [P, 4])
        lg = sb("lg", [P, NT, NG + NE])
        R = at(151, 16, NT, NE)
        rankm = sb("rankm", [P, NT, NE])
        posf = sb("posf", [P, 2, NT])
        posi = sb("posi", [P, 2, NT], I32)
        wts = sb("wts", [P, 2, NT])
        over = sb("over", [1, 1], I32)
        rsh = sb("rsh", [P, 2, NT])
        sel = at(156, 2, NT, P // 2).bitcast(F16)
        idx = sb("idx", [P, 2], I32)

        m_dram = nc.dram_tensor("m_scratch", [2, 6 * D], F32).ap()
        h2_dram = nc.dram_tensor("h2_scratch", [TOK, D], F32).ap()
        y_dram = nc.dram_tensor("y_scratch", [NT * NE * P, D], F32).ap()

        pe_full = sem("pe_bank_full")
        drained = {"act": sem("act_bank_drained"), "dve": sem("dve_bank_drained")}
        chunk_in = [sem(f"chunk_in{i}") for i in range(NRING)]
        in_mlp, in_dec, in_cond, in_small, in_x, in_base, in_ctx = (
            sem(n) for n in ("in_mlp", "in_dec", "in_cond", "in_small", "in_x", "in_base", "in_ctx"))
        in_dft = sem("in_dft")
        b_in = [sem("b_ada_in0"), sem("b_ada_in1")]
        m_out = [sem("m_row_out0"), sem("m_row_out1")]
        gt1_in, g2_in, sh2_in, tail_in = sem("gt1_in"), sem("g2_in"), sem("sh2_in"), sem("tail_in")
        act_chain, dve_chain, pool_chain = sem("act_chain"), sem("dve_chain"), sem("pool_chain")
        consts_ok = sem("consts_ok")
        cond_ok = sem("cond_ok")
        sin_arg, sin_ok = sem("sin_arg"), sem("sin_ok")
        filt_ok = sem("filt_ok")
        x_sq, x_rt, x_rs, xn_ok = sem("x_sq"), sem("x_rt"), sem("x_rs"), sem("xn_ok")
        conv_ok, z_ok = sem("conv_ok"), sem("z_ok")
        tap_ok, tap_used = sem("conv_tap_ok"), sem("conv_tap_used")
        y_ok = sem("y_ok")
        hyo_ok, hsq_ok, hg_ok = sem("hyo_ok"), sem("hsq_ok"), sem("hyena_gained")
        hrt = sem("h_root")
        kv_out = sem("kv_out")
        tm_ok, tm_used = sem("bias_ok"), sem("bias_used")
        mx_ok, p_ok = sem("mx_ok"), sem("p_ok")
        att_sq, att_rt = sem("att_sq"), sem("att_root")
        pv_ok = sem("pv_ok")
        wt_ok, wt2_ok = sem("wt_ok"), sem("x1_ok")
        n_sq, n_rt, h2_ok = sem("n_sq"), sem("n_rt"), sem("h2_ok")
        h2_out = [sem("h2_out0"), sem("h2_out1")]
        route_e, route_a, route_ok = sem("route_exp_arg"), sem("route_exp_ok"), sem("route_ok")
        mask_ok = sem("mask_ok")
        ew_in = [sem(f"expert_w_in{i}") for i in range(ESLOTS)]
        epsb = sb("epsb", [P, 1])
        mrow_used = sem("mod_row_turned")
        att_ok = sem("att_ok")
        assigned, shifted = sem("assigned"), sem("ranks_shifted")
        g2_done = sem("gain2_done")
        gather_go = sem("gather_go")
        sel_ok, idx_full, idx_ok = sem("sel_ok"), sem("idx_full"), sem("idx_ok")
        xg_in = [sem("xg_in0"), sem("xg_in1")]
        xgT_full, xgT_ok = sem("xgT_full"), sem("xgT_ok")
        gu_full, sil_ok, hid_ok = sem("gate_up_full"), sem("silu_ok"), sem("hid_ok")
        hidT_full, hidT_ok = sem("hidT_full"), sem("hidT_ok")
        y_full, y_cp = sem("y_full"), sem("y_copied")
        y_out = [sem("y_out0"), sem("y_out1")]
        yab_in = [sem(f"results_in{t}") for t in range(NT)]
        f_a, f_b, f_c = sem("first_weighted"), sem("results_summed"), sem("gated")
        g2row_in, pn_ok = sem("g2row_in"), sem("probs_normed")
        osq_ok, osum_ok, hsum_ok = sem("osq_ok"), sem("osum_ok"), sem("hsum_ok")
        stores_ok = sem("stores_ok")
        strip_ok, sq_ok = sem("strip_ok"), sem("sq_ok")
        y_cpA, y_cpD = sem("y_copied_act"), sem("y_copied_dve")
        f_cmb, f_sq, f_rt, f_ok, f_out = sem("f_cmb"), sem("f_sq"), sem("f_rt"), sem("f_ok"), sem("f_out")

        def full(eng, *name):
            eng.wait_ge(pe_full, JOB[name] + 1)
            return bank[JOBS[JOB[name]][1]]

        def have(eng, *name):
            eng.wait_ge(drained[JOBS[JOB[name]][2]], ORD[name])

        def drain(ins, *name):
            return ins.then_inc(drained[JOBS[JOB[name]][2]], 1)

        def wait_past(eng, sema, count):
            if not isinstance(count, int) or count > 0:
                eng.wait_ge(sema, count)

        def wait_pv(eng, u):
            if u % H == H - 1:
                full(eng, "o", u // H)
            else:
                eng.wait_ge(pv_ok, u // H * (H - 1) + u % H + 1)

        def turned_h2(act, b):
            for g in range(2):
                bk = full(act, "h2T", b, g)
                if b >= 2:
                    full(act, "rt", b - 2)
                drain(act.copy(h2T[:, b % 2, 4 * g:4 * g + 4, :].rearrange("p a b -> p (a b)"), bk[:, :]), "h2T", b, g)

        def chunk_src(c):
            if c[0] == "dft":
                return a["dft"][0]
            if c[0] == "idft":
                return a["dft"][1]
            w = {"ada": a["w_ada"], "win": a["w_in"], "wout": a["w_out"]}[c[0]]
            return w[:, c[1] * 512:(c[1] + 1) * 512].rearrange("(k p) n -> p k n", p=P)

        def chunk_view(i):
            return slot[i % NRING].rearrange("p (k n) -> p k n", n=512)

        pairs = NE // 2

        block = ctx.enter_context(nc.Block())

        @block.sync
        def _(sp):
            sp.dma_start(zf[0:EMB, :], a["zf"]).then_inc(in_mlp, 16)
            sp.dma_start(w12[0:EMB, 0, :], a["w1"]).then_inc(in_mlp, 16)
            sp.dma_start(w12[:, 1, :], a["w2"]).then_inc(in_mlp, 16)
            sp.dma_start(mlp_c[:, :], a["mlp_c"]).then_inc(in_mlp, 16)
            sp.dma_start(mw3[0:FF, :], a["w3"]).then_inc(in_mlp, 16)

            def load_chunk(i):
                if i >= NRING:
                    full(sp, *LAST_JOB[i - NRING])
                src = chunk_src(CHUNKS[i])
                if len(src.shape) == 2:
                    src = src.rearrange("p (k n) -> p k n", n=512)
                sp.dma_start(chunk_view(i), src).then_inc(chunk_in[i % NRING], 16)

            load_chunk(0)
            sp.dma_start(dec, a["dec"].rearrange("(t p) n -> p t n", p=P)).then_inc(in_dec, 16)
            sp.dma_start(bmask[:, :], a["bmask"]).then_inc(in_dec, 16)
            load_chunk(1)
            sp.dma_start(x, a["x"].rearrange("(t p) n -> p t n", p=P)).then_inc(in_x, 16)
            load_chunk(2)
            sp.dma_start(dftp[:, :, :], a["dftp"]).then_inc(in_dft, 16)
            for i in range(3, NCH):
                load_chunk(i)
            wg, wu, wd = a["w_gate"], a["w_up"], a["w_down"]

            def load_expert(e, s):
                for j, w in enumerate((wg, wu, wd)):
                    src = w[bass.ds(e, 1), :, :] if not isinstance(e, int) else w[e:e + 1, :, :]
                    n = 512 if j < 2 else 1024
                    src = src.rearrange("a (k p) n -> p (a k) n", p=P)
                    sp.dma_start(slot[3 * s + j].rearrange("p (k n) -> p k n", n=n), src)\
                      .then_inc(ew_in[3 * s + j], 16)
            full(sp, *LAST_JOB[-1])
            load_expert(0, 0)
            sp.wait_ge(h2_ok, NT)
            load_expert(1, 1)
            with sp.Fori(1, pairs) as i:
                for s in range(2):
                    sp.wait_ge(y_full, i * 4 + 2 * (s - 1))
                    load_expert(i * 2 + s, s)
            sp.wait_ge(route_ok, 1)
            v = sp.value_load(over[0:1, 0:1])
            with sp.If(v > 0):
                with sp.Fori(1, NT) as t:
                    with sp.Fori(0, pairs) as i:
                        for s in range(2):
                            sp.wait_ge(y_full, (t * pairs + i) * 4 + 2 * (s - 1))
                            load_expert(i * 2 + s, s)
            for t in range(NT):
                sp.wait_ge(f_ok, t + 1)
                sp.dma_start(outs["y"][t * P:(t + 1) * P, :], x[:, t, :]).then_inc(f_out, 16)
            sp.wait_ge(f_out, 16 * NT)
            sp.wait_ge(kv_out, 32)

        @block.gpsimd
        def _(pool):
            n_chain = [0]

            def link(ins):
                n_chain[0] += 1
                ins.then_inc(pool_chain, 1)
                pool.wait_ge(pool_chain, n_chain[0])

            link(pool.memset(ident[:, :], 0.0))
            link(pool.affine_select(out=ident[:, :], in_=ident[:, :], compare_op=ALU.not_equal, fill=1.0,
                                    base=0, pattern=[[-1, P]], channel_multiplier=1))
            link(pool.memset(ones[:, :], 1.0))
            link(pool.affine_select(out=tri[:, :], in_=ones[:, :], compare_op=ALU.is_gt, fill=0.0,
                                    base=0, pattern=[[1, P]], channel_multiplier=-1))
            pool.memset(over[:, :], 0).then_inc(consts_ok, 1)
            pool.dma_start(rw[:, :, :], a["rw"].rearrange("(k p) n -> p k n", p=P)).then_inc(in_small, 16)
            pool.dma_start(rb[:, :], a["rb"].partition_broadcast(P)).then_inc(in_small, 16)
            pool.dma_start(iota[:, :], a["iota"]).then_inc(in_small, 16)
            pool.dma_start(tid[:, :], a["tid"]).then_inc(in_small, 16)
            pool.dma_start(maskb[:, :, :], a["maskb"]).then_inc(in_small, 16)
            have(pool, "invp")
            have(pool, "hst")
            for r in range(ROWS):
                pool.dma_start(base[r * NA_COLS:(r + 1) * NA_COLS].rearrange("p h r c -> p h (r c)"),
                               a["rpb"][:, :, (NA_ROWS - 1 - r) * 3 * NA_COLS:(2 * NA_ROWS - 1 - r) * 3 * NA_COLS])\
                    .then_inc(in_base, 16)
            link(pool.memset(Tm, 0.0))
            pool.wait_ge(in_small, 5 * 16)
            pool.wait_ge(in_base, 16 * ROWS)

            def load_modulations():
                for q in m_out:
                    pool.wait_ge(q, 8 * (N_ADA - NA_FIRST))
                have(pool, "V", NT - 1)
                full(pool, "hst")
                for c in range(2):
                    for dst, v, s_in in ((gt1[:, c, :], 2, gt1_in), (G2[:, c, :], 4, g2_in), (SH2[c], 3, sh2_in)):
                        pool.dma_start(dst, m_dram[c:c + 1, v * D:(v + 1) * D].rearrange("a n -> (a n)")
                                       .partition_broadcast(P)).then_inc(s_in, 16)

            for u in range(CT * H):
                b, h = u // H, u % H
                if u >= 3:
                    have(pool, "s", u - 3)
                kts = key_tiles(b)
                kind = 0 if b == 0 else 2 if b == CT - 1 else 1
                for j, t in enumerate(kts):
                    dt = t - b + 1
                    out = Tm[:, u % 3, P * (1 + j):P * (2 + j)].rearrange("p (r c) -> p r c", c=NA_COLS)
                    in0 = base[:, h, :, dt * NA_COLS:(dt + 1) * NA_COLS]
                    in1 = maskb[:, kind, dt * NA_COLS:(dt + 1) * NA_COLS].unsqueeze(1)\
                        .broadcast_to([P, NA_ROWS, NA_COLS])
                    last = pool.tensor_tensor(out, in0, in1, ALU.add)
                last.then_inc(tm_ok, 1)
                if u == 3:
                    load_modulations()
            def store_h2(b):
                pool.wait_ge(h2_ok, b + 1)
                pool.dma_start(h2_dram[b * P:(b + 1) * P, :], h2[:, b % 2, :]).then_inc(h2_out[b % 2], 16)

            pool.wait_ge(gt1_in, 32)
            for b in range(NT):
                for n in range(2):
                    i = 2 * b + n
                    have(pool, "wh", b, n)
                    w = wtmp[:, i % 2, 0, :]
                    link(pool.tensor_tensor(w, w, gt1[:, b // CT, n * 512:(n + 1) * 512], ALU.mult))
                    pool.tensor_tensor(x[:, b, n * 512:(n + 1) * 512], x[:, b, n * 512:(n + 1) * 512], w,
                                       ALU.add).then_inc(wt2_ok, 1)
                if b > 0:
                    store_h2(b - 1)
            store_h2(NT - 1)
            pool.wait_ge(h2_out[0], 16 * 3)
            pool.wait_ge(h2_out[1], 16 * 2)
            pool.wait_ge(route_ok, 1)
            for c in range(2):
                pool.dma_start(gt2[:, c, :], m_dram[c:c + 1, 5 * D:6 * D].rearrange("a n -> (a n)").partition_broadcast(P)).then_inc(tail_in, 16)
            pool.dma_start(fg, a["fg"].partition_broadcast(P)).then_inc(tail_in, 16)

            def gather(i, first):
                for s in range(2):
                    pool.wait_ge(idx_ok, i * 2 + (s + 1))
                    if not first:
                        pool.wait_ge(xgT_full, i * 4 + 2 * (s - 1))
                    pool.sem_inc(gather_go, 1)
                    pool.indirect_dma_start(out=xg[:, s, :], out_offset=None, in_=h2_dram,
                                            in_offset=bass.IndirectOffsetOnAxis(ap=idx[:, s:s + 1].bitcast(U32), axis=0))\
                        .then_inc(xg_in[s], 16)
            gather(0, True)
            with pool.Fori(1, pairs) as i:
                gather(i, False)
            v = pool.value_load(over[0:1, 0:1])
            with pool.If(v > 0):
                with pool.Fori(pairs, NT * pairs) as i:
                    gather(i, False)
            pool.wait_ge(stores_ok, 1)

            def results(table):
                for t in range(NT):
                    for k, buf in enumerate((ya, yb)):
                        pool.indirect_dma_start(out=buf[:, t, :], out_offset=None, in_=table,
                                                in_offset=bass.IndirectOffsetOnAxis(ap=posi[:, k, t:t + 1].bitcast(U32), axis=0))\
                            .then_inc(yab_in[t], 16)
            with pool.If(v > 0):
                results(y_dram)
            with pool.Else():
                results(y_dram[0:NE * P, :])
            pool.wait_ge(tail_in, 48)
            for t in range(NT):
                pool.wait_ge(f_b, t + 1)
                pool.tensor_tensor(yb[:, t, :], yb[:, t, :], gt2[:, t // CT, :], ALU.mult).then_inc(f_c, 1)

        @block.scalar
        def _(act):
            n_chain = [0]

            def link(ins):
                n_chain[0] += 1
                ins.then_inc(act_chain, 1)
                act.wait_ge(act_chain, n_chain[0])

            act.dma_start(cond[:, :, :], a["cond"]).then_inc(in_cond, 16)
            act.dma_start(craw, a["ck"]).then_inc(in_ctx, 16)
            act.dma_start(g1c[:, :], a["g1c"]).then_inc(in_cond, 16)
            act.dma_start(cwb[:, :, :, :], a["cwb"]).then_inc(in_cond, 16)
            act.dma_start(chn[:, :, :], a["chn"]).then_inc(in_cond, 16)
            act.wait_ge(in_cond, 64)
            act.activation(scond[:, :, :], cond[:, :, :], ACT.Silu).then_inc(cond_ok, 1)

            def load_bias(j):
                r = 0 if j < NA_FIRST else 1
                act.dma_start(b_buf[r][:, j % 2, :], a["b2"][:, j * 512:(j + 1) * 512]).then_inc(b_in[j % 2], 16)
            load_bias(0)
            load_bias(1)
            for layer in range(2):
                act.wait_ge(sin_arg, layer + 1)
                act.activation(mh[layer][0:FF, :], mtmp[0][0:FF, :], ACT.Sin).then_inc(sin_ok, 1)
                if layer == 0:
                    b = full(act, "ckT")
                    drain(act.copy(ckT[:, :, :].rearrange("p a b -> p (a b)"), b[:, :]), "ckT")
                have(act, "ada", layer)
                load_bias(layer + 2)
            act.wait_ge(in_x, 16)
            for t in range(NT):
                link(act.activation(xn[:, t, :], x[:, t, :], ACT.Square, scale=1.0 / 32.0,
                                    accum_out=ss[:, 0, t:t + 1]))
            act.wait_ge(consts_ok, 2)
            act.activation(ss[:, 1, :], ss[:, 0, :], ACT.Sqrt, bias=epsb[:, :]).then_inc(x_rt, 1)
            for kt in range(NT):
                for ri, K in enumerate((KR, KI)):
                    b = full(act, "kf", kt, ri)
                    drain(act.copy(K[:, kt, :], b[:, :]), "kf", kt, ri)
                if kt == 0:
                    act.wait_ge(x_rs, 1)
                act.activation(xn[:, kt, :], x[:, kt, :], ACT.Copy, scale=ss[:, 2, kt:kt + 1]).then_inc(xn_ok, 1)
            n_tap = 0
            for c in range(3):
                for cb in range(CB):
                    b = full(act, "hy", c, cb)
                    if c == 0 and cb == 0:
                        act.wait_ge(strip_ok, 1)
                    if c > 0:
                        act.wait_ge(conv_ok, (c - 1) * CB + cb + 1)
                    dst = ustrip[:, cb, 1:1 + LAT].rearrange("p (r b c) -> p b r c", r=ROWS, c=NA_COLS)
                    drain(act.copy(dst, b[:, :].rearrange("p (b r c) -> p b r c", r=ROWS, c=NA_COLS)), "hy", c, cb)
                b = full(act, "hyp", c)
                drain(act.copy(ustrip[:, :, LAT + 2:LAT + 2 + CTX],
                               b[:, :].rearrange("p (a n) -> p a n", n=CTX)), "hyp", c)
                have(act, "hyp", c)
                for cb in range(CB):
                    dst = (z[:, cb], ctmp[:, cb % 2], x0[:, cb])[c][:, 0:UW - 3]
                    if c == 1 and cb >= 2:
                        act.wait_ge(z_ok, cb - 1)
                    act.activation(dst, ustrip[:, cb, 1:UW - 2], ACT.Identity, scale=cwb[:, HYROW[c], cb, 1:2],
                                   bias=cwb[:, HYROW[c], cb, 3:4]).then_inc(tap_ok, 1)
            for t in range(NT):
                b = full(act, "zT", t)
                drain(act.copy(zt[:, t, :], b[:, :]), "zT", t)
            act.wait_ge(conv_ok, 3 * CB)
            load_bias(4)
            load_bias(5)
            act.dma_start(g2row, a["g2r"][:, 0:512]).then_inc(g2row_in, 16)
            for j in range(NA_FIRST, N_ADA):
                have(act, "ada", j)
                if j in (8, 9):
                    act.wait_ge(g2_done, j - 7)
                act.dma_start(m_dram[:, j * 512:(j + 1) * 512], mrow[1][:, j % 2, :]).then_inc(m_out[j % 2], 16)
                if j + 2 < N_ADA:
                    load_bias(j + 2)
                if j == 8:
                    act.dma_start(g2row, a["g2r"][:, 512:1024]).then_inc(g2row_in, 16)
            for cb in range(CB):
                act.wait_ge(hyo_ok, CB)
                act.activation(sq[:, cb, :], hyoT[:, cb, :], ACT.Square).then_inc(hsq_ok, 1)
            act.wait_ge(hsq_ok, CB)
            for cb in range(CB):
                act.activation(hyoT[:, cb, :], hyoT[:, cb, :], ACT.Copy, scale=chn[:, 1, cb:cb + 1]).then_inc(hg_ok, 1)
            have(act, "invp")
            act.dma_start(cv, a["cv"]).then_inc(in_ctx, 16)
            for ch, dst, scale in (("q", QT, DH ** -0.5), ("k", KTt, 1.0)):
                for cb in range(CB):
                    b = full(act, ch, cb)
                    drain(act.activation(dst[:, cb, 0:LAT], b[:, :], ACT.Copy, scale=scale), ch, cb)
                b = full(act, ch + "p")
                drain(act.activation(dst[:, :, LAT:TOK], b[:, :].rearrange("p (a n) -> p a n", n=CTX), ACT.Copy,
                                     scale=scale), ch + "p")
            for t in range(NT):
                b = full(act, "V", t)
                drain(act.copy(V[:, t, :], b[:, :]), "V", t)
            b = full(act, "nk")
            drain(act.copy(nkb, b[:, :]), "nk")
            have(act, "nk")
            act.dma_start(outs["v"], V[:, CT, :]).then_inc(kv_out, 16)
            act.dma_start(outs["k"], nkb).then_inc(kv_out, 16)

            def exps(u):
                b, h = u // H, u % H
                n = P * (1 + len(key_tiles(b)))
                act.wait_ge(mx_ok, u + 1)
                if u >= 2:
                    full(act, "pt", u - 2)
                act.activation(pr[:, u % 2, 0:n], sc[:, u % 2, 0:n], ACT.Exp, bias=nmx[:, u % 4:u % 4 + 1],
                               accum_out=rsum[:, u % 4:u % 4 + 1]).then_inc(p_ok, 1)

            def probs_turned(u):
                nk = 1 + len(key_tiles(u // H))
                b = full(act, "pt", u)
                if u >= 2:
                    wait_pv(act, u - 2)
                drain(act.copy(PT[:, u % 2, 0:nk, :].rearrange("p a b -> p (a b)"), b[:, 0:nk * P]), "pt", u)

            def att_squares(b):
                have(act, "o", b)
                act.activation(osq, oraw[:, b % 2], ACT.Square).then_inc(osq_ok, 1)

            exps(0)
            for u in range(NT * H):
                if u + 1 < NT * H:
                    exps(u + 1)
                probs_turned(u)
                if u % H == 1 and u > H:
                    att_squares(u // H - 1)
            act.wait_ge(hrt, 1)
            act.activation(ss[:, 6, :], ss[:, 5, :], ACT.Sqrt, scale=1.0 / CH, bias=epsb[:, :]).then_inc(att_rt, 1)
            att_squares(NT - 1)
            have(act, "ast", NT - 1)
            act.activation(ss[:, 4, :], ss[:, 3, :], ACT.Sqrt, scale=1.0 / CH, bias=epsb[:, :]).then_inc(att_rt, 1)
            for b in range(NT + 1):
                if b < NT:
                    act.wait_ge(wt2_ok, 2 * b + 2)
                    link(act.activation(sqd, x[:, b, :], ACT.Square, scale=1.0 / 32.0, accum_out=ss[:, 0, b:b + 1]))
                    act.activation(ss[:, 1, b:b + 1], ss[:, 0, b:b + 1], ACT.Sqrt, bias=epsb[:, :]).then_inc(n_rt, 1)
                if b > 0:
                    turned_h2(act, b - 1)
            act.wait_ge(route_e, 1)
            act.activation(R[:, 1, :, 0:NG], R[:, 0, :, 0:NG], ACT.Exp).then_inc(route_a, 1)
            act.wait_ge(route_e, 2)
            act.activation(R[:, 9, :, 0:1], R[:, 8, :, 0:1], ACT.Exp).then_inc(route_a, 1)

            def expert(p, i, s):
                n = (i + p * pairs) * 2 + s
                act.wait_ge(gu_full, n * 2 + 1)
                wait_past(act, hid_ok, n)
                act.activation(sil, bank[2][:, :], ACT.Silu).then_inc(sil_ok, 1)
                act.wait_ge(hidT_full, n + 1)
                act.copy(hidT[:, s].rearrange("p a b -> p (a b)"), bank[4][:, :]).then_inc(hidT_ok, 1)
                act.wait_ge(y_full, n * 2 + 1)
                wait_past(act, y_out[s], (i + p * pairs) * 16)
                act.copy(yout[:, s, 0:512], bank[5][:, :]).then_inc(y_cpA, 1)
                act.wait_ge(y_cpA, n + 1)
                act.wait_ge(y_cpD, n + 1)
                row = n * P
                act.dma_start(y_dram[bass.ds(row, P), :], yout[:, s, :]).then_inc(y_out[s], 16)

            def one_pass(p):
                for s in range(2):
                    expert(p, 0, s)
                with act.Fori(1, pairs) as i:
                    for s in range(2):
                        expert(p, i, s)
                for s in range(2):
                    act.wait_ge(y_out[s], (p + 1) * (pairs * 16))
            one_pass(0)
            act.wait_ge(route_ok, 1)
            v = act.value_load(over[0:1, 0:1])
            with act.If(v > 0):
                with act.Fori(1, NT) as p:
                    one_pass(p)
            act.copy(ss[:, 7, :], ss[:, 6, :]).then_inc(stores_ok, 1)
            for t in range(NT + 1):
                if t < NT:
                    act.wait_ge(yab_in[t], 32)
                    act.activation(ya[:, t, :], ya[:, t, :], ACT.Copy, scale=wts[:, 0, t:t + 1]).then_inc(f_a, 1)
                if t > 0:
                    q = t - 1
                    act.wait_ge(f_cmb, t)
                    link(act.activation(sqd, x[:, q, :], ACT.Square, scale=1.0 / 32.0, accum_out=ss[:, 0, q:q + 1]))
                    act.activation(ss[:, 1, q:q + 1], ss[:, 0, q:q + 1], ACT.Sqrt, bias=epsb[:, :]).then_inc(f_rt, 1)

        @block.vector
        def _(dve):
            n_chain = [0]

            def link(ins):
                n_chain[0] += 1
                ins.then_inc(dve_chain, 1)
                dve.wait_ge(dve_chain, n_chain[0])

            dve.memset(epsb[:, :], EPS).then_inc(consts_ok, 1)
            dve.wait_ge(in_mlp, 80)
            def ada(j):
                r = 0 if j < NA_FIRST else 1
                dve.wait_ge(b_in[j % 2], 16 * (j // 2 + 1))
                if 2 <= j < NA_FIRST:
                    dve.wait_ge(mrow_used, j - 1)
                if j >= NA_FIRST + 2:
                    dve.wait_ge(m_out[j % 2], 16 * ((j - NA_FIRST) // 2))
                b = full(dve, "ada", j)
                m = mrow[r][:, j % 2, :]
                drain(dve.tensor_tensor(m, b[0:2, :], b_buf[r][:, j % 2, :], ALU.add), "ada", j)
                if j in (8, 9):
                    dve.wait_ge(g2row_in, 16 * (j - 7))
                    have(dve, "ada", j)
                    dve.scalar_tensor_tensor(out=m, in0=m, scalar=1.0, in1=g2row, op0=ALU.add, op1=ALU.mult)\
                       .then_inc(g2_done, 1)

            for layer in range(2):
                v, k = mtmp[0][0:FF, :], mtmp[1][0:FF, :]
                if layer:
                    dve.wait_ge(sin_ok, 1)
                for i, (lo, hi) in enumerate(((0, LAT), (LAT, TOK))):
                    b = full(dve, f"mlp{layer + 1}", i)
                    drain(dve.tensor_scalar(v[:, lo:hi], b[0:FF, 0:hi - lo], mlp_c[:, layer:layer + 1], mlp_c[:, 2:3],
                                            ALU.add, ALU.mult), f"mlp{layer + 1}", i)
                have(dve, f"mlp{layer + 1}", 1)
                link(dve.tensor_scalar(k, v, 1.0 / TWO_PI, ROUND, ALU.mult, ALU.add))
                link(dve.tensor_scalar(k, k, ROUND, None, ALU.subtract))
                for part in (PI_A, PI_B, PI_C):
                    link(dve.scalar_tensor_tensor(out=v, in0=k, scalar=-part, in1=v, op0=ALU.mult, op1=ALU.add))
                dve.tensor_scalar(v, v, 3.1415925, -3.1415925, ALU.min, ALU.max).then_inc(sin_arg, 1)
                ada(layer)
            dve.wait_ge(in_dec, 32)
            for t in range(NT):
                b = full(dve, "filt", t, 0)
                drain(dve.tensor_tensor(fbuf[:, 0, :], b[:, :], dec[:, t, :], ALU.mult), "filt", t, 0)
                b = full(dve, "filt", t, 1)
                drain(dve.scalar_tensor_tensor(out=fbuf[:, 1, :], in0=b[:, :], scalar=bmask[:, t:t + 1],
                                               in1=dec[:, t, :], op0=ALU.mult, op1=ALU.mult), "filt", t, 1)
                have(dve, "filt", t, 1)
                dve.tensor_tensor(s_flt[:, t, :], fbuf[:, 0, :], fbuf[:, 1, :], ALU.add).then_inc(filt_ok, 1)
                dve.tensor_tensor(d_flt[:, t, :], fbuf[:, 0, :], fbuf[:, 1, :], ALU.subtract).then_inc(filt_ok, 1)
                dve.wait_ge(filt_ok, 2 * t + 2)

            for j in range(2, NA_FIRST):
                ada(j)
            dve.wait_ge(in_cond, 64)
            b = full(dve, "mcol")
            mc = b[:, 0:4 * KT].rearrange("p (v k c) -> p v k c", v=2, c=2)
            link(dve.tensor_copy(mcol[:, 1], mc[:, 0]))
            drain(dve.scalar_tensor_tensor(out=mcol[:, 0], in0=mc[:, 1], scalar=1.0,
                                           in1=g1c[:, :].unsqueeze(2).broadcast_to([P, KT, 2]),
                                           op0=ALU.add, op1=ALU.mult), "mcol")
            have(dve, "mcol")
            dve.wait_ge(x_rt, 1)
            dve.reciprocal(ss[:, 2, :], ss[:, 1, :]).then_inc(x_rs, 1)
            have(dve, "kf", NT - 1, 1)
            for k in range(KT):
                b = full(dve, "xT", k)
                drain(dve.tensor_scalar(hT[:, k, 0:LAT], b[:, :], mcol[:, 0, k, 0:1], mcol[:, 1, k, 0:1],
                                        ALU.mult, ALU.add), "xT", k)
            for g in range(2):
                b = full(dve, "xTp", g)
                for j in range(4):
                    k = 4 * g + j
                    ins = dve.tensor_scalar(hT[:, k, LAT:TOK], b[:, j * P:(j + 1) * P], mcol[:, 0, k, 1:2],
                                            mcol[:, 1, k, 1:2], ALU.mult, ALU.add)
                drain(ins, "xTp", g)
            dve.memset(ustrip, 0.0).then_inc(strip_ok, 1)
            n = 0
            for c in range(3):
                for cb in range(CB):
                    n += 1
                    dst = (z[:, cb], ctmp[:, cb % 2], x0[:, cb])[c][:, 0:UW - 3]
                    w = cwb[:, HYROW[c], cb, :]
                    dve.wait_ge(tap_ok, n)
                    link(dve.scalar_tensor_tensor(out=dst, in0=ustrip[:, cb, 0:UW - 3], scalar=w[:, 0:1], in1=dst,
                                                  op0=ALU.mult, op1=ALU.add))
                    dve.scalar_tensor_tensor(out=dst, in0=ustrip[:, cb, 2:UW - 1], scalar=w[:, 2:3], in1=dst,
                                             op0=ALU.mult, op1=ALU.add).then_inc(conv_ok, 1)
                    dve.wait_ge(conv_ok, n)
                    if c == 1:
                        dve.tensor_tensor(z[:, cb, 0:UW - 3], z[:, cb, 0:UW - 3], dst, ALU.mult).then_inc(z_ok, 1)
            for kt in range(NT):
                re, im = full(dve, "uf", kt, 0), None
                yr, yi = YR[:, kt, :], YI[:, kt, :]
                if kt == 0:
                    have(dve, "kf", NT - 1, 1)
                link(dve.tensor_tensor(yr, re[:, :], KR[:, kt, :], ALU.mult))
                drain(dve.tensor_tensor(yi, re[:, :], KI[:, kt, :], ALU.mult), "uf", kt, 0)
                im = full(dve, "uf", kt, 1)
                link(dve.tensor_tensor(ytmp[:, 0, :], im[:, :], KI[:, kt, :], ALU.mult))
                drain(dve.tensor_tensor(ytmp[:, 1, :], im[:, :], KR[:, kt, :], ALU.mult), "uf", kt, 1)
                have(dve, "uf", kt, 1)
                link(dve.tensor_tensor(yr, yr, ytmp[:, 0, :], ALU.subtract))
                dve.tensor_tensor(yi, yi, ytmp[:, 1, :], ALU.add).then_inc(y_ok, 1)
                dve.wait_ge(y_ok, kt + 1)
            for j in range(NA_FIRST, N_ADA):
                ada(j)
            for q in m_out:
                dve.wait_ge(q, 8 * (N_ADA - NA_FIRST))
            perm = "p (b r c) -> p r b c"
            for cb in range(CB):
                b = full(dve, "inv", cb)
                drain(dve.scalar_tensor_tensor(out=t1[:, cb % 2, 0:LAT], in0=z[:, cb, 0:LAT], scalar=chn[:, 0, cb:cb + 1],
                                               in1=b[:, :], op0=ALU.mult, op1=ALU.add), "inv", cb)
                have(dve, "inv", cb)
                nat = "p (r b c) -> p r b c"
                link(dve.tensor_tensor(hyoT[:, cb, 0:LAT].rearrange(perm, r=ROWS, c=NA_COLS),
                                       t1[:, cb % 2, 0:LAT].rearrange(nat, r=ROWS, c=NA_COLS),
                                       x0[:, cb, 0:LAT].rearrange(nat, r=ROWS, c=NA_COLS), ALU.mult))
            b = full(dve, "invp")
            for cb in range(CB):
                ins = dve.scalar_tensor_tensor(out=t1[:, cb % 2, cb // 2 * P:cb // 2 * P + P], in0=z[:, cb, LAT + 1:LAT + 1 + CTX],
                                               scalar=chn[:, 0, cb:cb + 1], in1=b[:, cb * P:(cb + 1) * P],
                                               op0=ALU.mult, op1=ALU.add)
            drain(ins, "invp")
            have(dve, "invp")
            for cb in range(CB):
                dve.tensor_tensor(hyoT[:, cb, LAT:TOK], t1[:, cb % 2, cb // 2 * P:cb // 2 * P + P],
                                  x0[:, cb, LAT + 1:LAT + 1 + CTX], ALU.mult).then_inc(hyo_ok, 1)
            dve.wait_ge(hsq_ok, CB)
            link(dve.tensor_tensor(sq[:, 0:2, :], sq[:, 0:2, :], sq[:, 2:4, :], ALU.add))
            dve.tensor_tensor(sq[:, 0, :], sq[:, 0, :], sq[:, 1, :], ALU.add).then_inc(hsum_ok, 1)
            b = full(dve, "hst")
            drain(dve.tensor_copy(ss[:, 5, :], b[:, 0:NT]), "hst")
            have(dve, "hst")
            dve.tensor_copy(rsh[:, 1, :], ss[:, 5, :]).then_inc(hrt, 1)

            def scores(u):
                b = full(dve, "s", u)
                n = P * (1 + len(key_tiles(u // H)))
                if u >= 2:
                    dve.wait_ge(p_ok, u - 1)
                if u < CT * H:
                    dve.wait_ge(tm_ok, u + 1)
                else:
                    dve.wait_ge(tm_ok, CT * H)
                drain(dve.tensor_tensor_reduce(sc[:, u % 2, 0:n], b[:, 0:n], Tm[:, u % 3, 0:n], 1.0, -3.0e38,
                                               ALU.add, ALU.max, rmx[:, u % 4:u % 4 + 1]), "s", u)
                have(dve, "s", u)
                dve.tensor_scalar(nmx[:, u % 4:u % 4 + 1], rmx[:, u % 4:u % 4 + 1], -1.0, None, ALU.mult)\
                   .then_inc(mx_ok, 1)

            def normed(u):
                n = P * (1 + len(key_tiles(u // H)))
                c = slice(u % 4, u % 4 + 1)
                dve.wait_ge(p_ok, u + 1)
                link(dve.reciprocal(rinv[:, c], rsum[:, c]))
                dve.tensor_scalar(pr[:, u % 2, 0:n], pr[:, u % 2, 0:n], rinv[:, c], None, ALU.mult).then_inc(pn_ok, 1)

            def out_tile(b):
                bk = full(dve, "o", b)
                if b >= 2:
                    dve.wait_ge(osq_ok, b - 1)
                r = oraw[:, b % 2]
                drain(dve.tensor_copy(r.rearrange("p a n -> p (a n)"), bk[:, :]), "o", b)
                if b == 0:
                    dve.wait_ge(kv_out, 32)
                have(dve, "o", b)
                dve.tensor_tensor(attT[:, :, b * P:(b + 1) * P], r, chn[:, 2, :].unsqueeze(2).broadcast_to([P, CB, P]),
                                  ALU.mult).then_inc(att_ok, 1)

            def out_sums(b):
                dve.wait_ge(osq_ok, b + 1)
                if b >= 2:
                    full(dve, "ast", b - 2)
                link(dve.tensor_tensor(osq[:, 0:2, :], osq[:, 0:2, :], osq[:, 2:4, :], ALU.add))
                dve.tensor_tensor(osum[:, b % 2, :], osq[:, 0, :], osq[:, 1, :], ALU.add).then_inc(osum_ok, 1)

            def stat(b):
                bk = full(dve, "ast", b)
                drain(dve.tensor_copy(ss[:, 3, b:b + 1], bk[:, b:b + 1]), "ast", b)

            for u in range(-2, NT * H + 1):
                if u + 2 < NT * H:
                    scores(u + 2)
                if u >= -1 and u + 1 < NT * H:
                    normed(u + 1)
                if u >= 1 and (u - 1) % H == H - 1:
                    out_tile((u - 1) // H)
                if u - 1 >= H and (u - 1) % H == 2:
                    out_sums((u - 1) // H - 1)
                if u - 1 >= H and (u - 1) % H == 3:
                    stat((u - 1) // H - 1)
            out_sums(NT - 1)
            stat(NT - 1)
            dve.wait_ge(att_rt, 1)
            link(dve.reciprocal(rsh[:, 1, :], ss[:, 6, :]))
            dve.wait_ge(att_rt, 2)
            link(dve.reciprocal(rsh[:, 0, :], ss[:, 4, :]))

            def modulated(b):
                c = b // CT
                dve.wait_ge(n_rt, b + 1)
                link(dve.reciprocal(ss[:, 2, b:b + 1], ss[:, 1, b:b + 1]))
                if b >= 2:
                    full(dve, "h2T", b - 2, 1)
                    dve.wait_ge(h2_out[b % 2], 16 * (b // 2))
                link(dve.scalar_tensor_tensor(out=h2[:, b % 2, :], in0=x[:, b, :], scalar=ss[:, 2, b:b + 1],
                                              in1=G2[:, c, :], op0=ALU.mult, op1=ALU.mult))
                dve.tensor_tensor(h2[:, b % 2, :], h2[:, b % 2, :], SH2[c], ALU.add).then_inc(h2_ok, 1)
                bk = full(dve, "rt", b)
                drain(dve.tensor_tensor(lg[:, b, :], bk[:, 0:NG + NE], rb[:, :], ALU.add), "rt", b)

            dve.wait_ge(in_small, 80)
            dve.wait_ge(g2_in, 32)
            dve.wait_ge(sh2_in, 32)
            for b in range(NT):
                for n in range(2):
                    i = 2 * b + n
                    w = wtmp[:, i % 2, 0, :]
                    bk = full(dve, "wa", b, n)
                    if i >= 2:
                        dve.wait_ge(wt2_ok, i - 1)
                    drain(dve.tensor_scalar(w, bk[:, :], rsh[:, 0, b:b + 1], None, ALU.mult), "wa", b, n)
                    have(dve, "wa", b, n)
                    bk = full(dve, "wh", b, n)
                    drain(dve.scalar_tensor_tensor(out=w, in0=bk[:, :], scalar=rsh[:, 1, b:b + 1], in1=w,
                                                   op0=ALU.mult, op1=ALU.add), "wh", b, n)
                if b > 0:
                    modulated(b - 1)
            modulated(NT - 1)
            have(dve, "rt", NT - 1)

            def r4(i):
                return R[:, i, :, 0:NG]

            def r1(i):
                return R[:, i, :, 0:1]

            def over4(v):
                return v.broadcast_to([P, NT, NG])

            def first_max(val, mx, out, tmp, low):
                link(dve.tensor_reduce(mx, val, AX, ALU.max))
                link(dve.tensor_tensor(out, val, over4(mx), ALU.is_equal))
                link(dve.scalar_tensor_tensor(out=tmp, in0=out, scalar=-float(NG),
                                              in1=iota[:, 0:NG].unsqueeze(1).broadcast_to([P, NT, NG]),
                                              op0=ALU.mult, op1=ALU.add))
                link(dve.tensor_reduce(low, tmp, AX, ALU.min))
                link(dve.tensor_tensor(out, tmp, over4(low), ALU.is_equal))

            gl = lg[:, :, 0:NG]
            first_max(gl, r1(2), r4(3), r4(4), r1(5))
            dve.tensor_tensor(r4(0), gl, over4(r1(2)), ALU.subtract).then_inc(route_e, 1)
            el = lg[:, :, NG:].rearrange("p t (g j) -> p t g j", j=EPG)
            prod = R[:, 10].rearrange("p t (g j) -> p t g j", j=EPG)
            link(dve.tensor_tensor(prod, el, r4(3).unsqueeze(3).broadcast_to([P, NT, NG, EPG]), ALU.mult))
            link(dve.tensor_reduce(r4(6), prod.rearrange("p t g j -> p t j g"), AX, ALU.add))
            first_max(r4(6), r1(2), r4(7), r4(4), r1(5))
            link(dve.scalar_tensor_tensor(out=r4(6), in0=r4(7), scalar=-1.0e30, in1=r4(6), op0=ALU.mult, op1=ALU.add))
            first_max(r4(6), r1(12), r4(11), r4(4), r1(5))
            dve.tensor_tensor(r1(8), r1(12), r1(2), ALU.subtract).then_inc(route_e, 1)
            A1, A2, A = R[:, 13], R[:, 14], R[:, 15]
            for dst, j1 in ((A1, 7), (A2, 11)):
                link(dve.tensor_tensor(dst.rearrange("p t (g j) -> p t g j", j=EPG),
                                       r4(3).unsqueeze(3).broadcast_to([P, NT, NG, EPG]),
                                       r4(j1).unsqueeze(2).broadcast_to([P, NT, NG, EPG]), ALU.mult))
            dve.tensor_tensor(A, A1, A2, ALU.add).then_inc(assigned, 1)
            dve.wait_ge(route_a, 2)
            link(dve.tensor_reduce(r1(5), r4(1), AX, ALU.add))
            link(dve.reciprocal(r1(5), r1(5)))
            link(dve.tensor_scalar(r1(2), r1(9), 1.0, None, ALU.add))
            link(dve.reciprocal(r1(2), r1(2)))
            w1 = wts[:, 0, :].unsqueeze(2)
            link(dve.tensor_tensor(w1, r1(2), r1(5), ALU.mult))
            link(dve.tensor_tensor(wts[:, 1, :].unsqueeze(2), w1, r1(9), ALU.mult))
            bk = full(dve, "rank")
            rk = R[:, 10]
            drain(dve.tensor_copy(rk, bk[:, 0:NT * NE].rearrange("p (t e) -> p t e", e=NE)), "rank")
            have(dve, "rank")
            link(dve.scalar_tensor_tensor(out=rankm[:, :, :], in0=rk, scalar=1.0, in1=A, op0=ALU.add, op1=ALU.mult))
            link(dve.tensor_scalar(rankm[:, :, :], rankm[:, :, :], -1.0, None, ALU.add))
            row, more = R[:, 9], R[:, 11]
            link(dve.scalar_tensor_tensor(out=row, in0=iota[:, 0:NE].unsqueeze(1).broadcast_to([P, NT, NE]),
                                          scalar=float(P), in1=rk, op0=ALU.mult, op1=ALU.add))
            for p in range(1, NT):
                link(dve.tensor_scalar(more, rk, float(p * CAP), float(NE * P - CAP), ALU.is_ge, ALU.mult))
                link(dve.tensor_tensor(row, row, more, ALU.add))
            for k, Ak in enumerate((A1, A2)):
                link(dve.tensor_tensor(Ak, Ak, row, ALU.mult))
                link(dve.tensor_reduce(posf[:, k, :].unsqueeze(2), Ak, AX, ALU.add))
            link(dve.tensor_copy(posi[:, :, :], posf[:, :, :]))
            bk = full(dve, "total")
            drain(dve.tensor_reduce(R[:, 12, 0, 0:1], bk[:, 0:NE], AX, ALU.max), "total")
            have(dve, "total")
            dve.wait_ge(consts_ok, 2)
            dve.tensor_scalar(over[0:1, 0:1], R[0:1, 12, 0, 0:1], float(CAP), None, ALU.is_gt).then_inc(route_ok, 1)

            def slots_of(n, e, s):
                wait_past(dve, idx_full, n - 1)
                dve.tensor_tensor(sel[:, s], iota[:, :].unsqueeze(1).broadcast_to([P, NT, P]),
                                  rankm[:, :, bass.ds(e, 1)].broadcast_to([P, NT, P]), ALU.is_equal).then_inc(sel_ok, 1)

            def numbers(n, s):
                dve.wait_ge(idx_full, n + 1)
                wait_past(dve, xg_in[s], (n - s) * 8)
                dve.tensor_copy(idx[:, s:s + 1], bank[7][:, 0:1]).then_inc(idx_ok, 1)

            def rows_turned(n, s):
                for g in range(2):
                    dve.wait_ge(xgT_full, n * 2 + (g + 1))
                    dve.tensor_copy(xgT[:, s, 4 * g:4 * g + 4, :].rearrange("p a b -> p (a b)"), bank[g][:, :])\
                       .then_inc(xgT_ok, 1)

            def expert(p, i, s, ahead2, ahead1):
                n = (i + p * pairs) * 2 + s
                if ahead2:
                    slots_of(n + 2, i * 2 + (s + 2), s)
                dve.wait_ge(gu_full, n * 2 + 2)
                dve.wait_ge(sil_ok, n + 1)
                dve.tensor_tensor(hid[:, s, :], sil, bank[3][:, :], ALU.mult).then_inc(hid_ok, 1)
                if ahead2:
                    numbers(n + 2, s)
                if ahead1:
                    rows_turned(n + 1, 1 - s)
                dve.wait_ge(y_full, n * 2 + 2)
                wait_past(dve, y_out[s], (i + p * pairs) * 16)
                dve.tensor_copy(yout[:, s, 512:1024], bank[6][:, :]).then_inc(y_cpD, 1)

            def one_pass(p):
                for s in range(2):
                    slots_of(p * NE + s, s, s)
                    numbers(p * NE + s, s)
                rows_turned(p * NE, 0)
                for s in range(2):
                    expert(p, 0, s, True, True)
                with dve.Fori(1, pairs - 1) as i:
                    for s in range(2):
                        expert(p, i, s, True, True)
                for s in range(2):
                    expert(p, pairs - 1, s, False, s == 0)
            one_pass(0)
            v = dve.value_load(over[0:1, 0:1])
            with dve.If(v > 0):
                with dve.Fori(1, NT) as p:
                    dve.tensor_scalar(rankm[:, :, :], rankm[:, :, :], -float(CAP), None, ALU.add).then_inc(shifted, 1)
                    dve.wait_ge(shifted, p)
                    one_pass(p)
            dve.wait_ge(tail_in, 48)
            for t in range(NT + 2):
                if t < NT:
                    dve.wait_ge(f_a, t + 1)
                    dve.scalar_tensor_tensor(out=yb[:, t, :], in0=yb[:, t, :], scalar=wts[:, 1, t:t + 1], in1=ya[:, t, :],
                                             op0=ALU.mult, op1=ALU.add).then_inc(f_b, 1)
                if 0 < t <= NT:
                    dve.wait_ge(f_c, t)
                    dve.tensor_tensor(x[:, t - 1, :], x[:, t - 1, :], yb[:, t - 1, :], ALU.add).then_inc(f_cmb, 1)
                if t > 1:
                    q = t - 2
                    dve.wait_ge(f_rt, q + 1)
                    link(dve.reciprocal(ss[:, 2, q:q + 1], ss[:, 1, q:q + 1]))
                    dve.scalar_tensor_tensor(out=x[:, q, :], in0=x[:, q, :], scalar=ss[:, 2, q:q + 1], in1=fg,
                                             op0=ALU.mult, op1=ALU.mult).then_inc(f_ok, 1)

        @block.tensor
        def _(pe):
            def open_bank(*name):
                j = JOB[name]
                prev = [q for q in range(j) if JOBS[q][1] == JOBS[j][1]]
                if prev:
                    have(pe, *JOBS[prev[-1]][0])
                return bank[JOBS[j][1]]

            def close(ins):
                ins.then_inc(pe_full, 1)

            def group(out, terms, start=True):
                for i, (l, r) in enumerate(terms):
                    ins = pe.matmul(out, l, r, start=(i == 0), stop=(i == len(terms) - 1))
                return ins

            def chunk(c, again=0):
                i = FIRST_USE[c][again]
                pe.wait_ge(chunk_in[i % NRING], 16 * (i // NRING + 1))
                return slot[i % NRING]

            def turn(out, src):
                return pe.transpose(out, src, ident[:, :])

            pe.wait_ge(consts_ok, 2)

            def ada(j):
                W = chunk(("ada", j)).rearrange("p (k n) -> p k n", n=512)
                b = open_bank("ada", j)
                close(group(b[0:2, :], [(scond[:, k, :], W[:, k, :]) for k in range(KT)]))

            def col(j):
                if j == 0:
                    open_bank("mcol")
                have(pe, "ada", j)
                b = bank[JOBS[JOB[("mcol",)]][1]]
                for q in range(4):
                    o = (4 * j + q) * 2
                    ins = pe.matmul(b[:, o:o + 2], mrow[0][:, j % 2, q * P:(q + 1) * P], ident[0:2, 0:2],
                                    start=True, stop=True)
                if j < NA_FIRST - 1:
                    ins.then_inc(mrow_used, 1)
                else:
                    close(ins)

            pe.wait_ge(in_mlp, 80)
            for layer in range(2):
                src, k = (zf, EMB) if layer == 0 else (mh[0], FF)
                if layer:
                    pe.wait_ge(sin_ok, 1)
                for i, (lo, hi) in enumerate(((0, LAT), (LAT, TOK))):
                    b = open_bank(f"mlp{layer + 1}", i)
                    close(pe.matmul(b[0:FF, 0:hi - lo], w12[0:k, layer, :], src[0:k, lo:hi], start=True, stop=True))
                if layer == 0:
                    pe.wait_ge(in_ctx, 16)
                    b = open_bank("ckT")
                    for cb in range(CB):
                        ins = turn(b[:, cb * P:(cb + 1) * P], craw[:, cb * P:(cb + 1) * P])
                    close(ins)
                    pe.wait_ge(cond_ok, 1)
                ada(layer)
            pe.wait_ge(sin_ok, 2)
            for t in range(NT):
                for d in range(2):
                    b = open_bank("filt", t, d)
                    close(pe.matmul(b[:, :], mh[1][0:FF, t * P:(t + 1) * P], mw3[0:FF, d * CH:(d + 1) * CH],
                                    start=True, stop=True))
            for j in range(2):
                col(j)
            for j in range(2, NA_FIRST):
                ada(j)
                col(j)
            pe.wait_ge(filt_ok, 2 * NT)
            F = chunk(("dft",)).rearrange("p (a t k) -> p a t k", a=2, k=LAT)
            pe.wait_ge(in_dft, 16)
            for kt in range(NT):
                for ri, src in enumerate((s_flt, d_flt)):
                    b = open_bank("kf", kt, ri)
                    if kt < CT:
                        close(group(b[:, :], [(F[:, ri, t, kt * P:(kt + 1) * P], src[:, t, :]) for t in range(CT)]))
                    else:
                        close(pe.matmul(b[:, :], dftp[:, ri, :], src[:, CT, :], start=True, stop=True))
            pe.wait_ge(xn_ok, NT)
            for k in range(KT):
                b = open_bank("xT", k)
                for t in range(CT):
                    ins = turn(b[:, t * P:(t + 1) * P], xn[:, t, k * P:(k + 1) * P])
                close(ins)
            for g in range(2):
                b = open_bank("xTp", g)
                for j in range(4):
                    k = 4 * g + j
                    ins = turn(b[:, j * P:(j + 1) * P], xn[:, CT, k * P:(k + 1) * P])
                close(ins)

            def project(job, jobp, W):
                for cb in range(CB):
                    b = open_bank(*job, cb)
                    close(group(b[:, :], [(W[:, k, cb * P:(cb + 1) * P], hT[:, k, 0:LAT]) for k in range(KT)]))
                b = open_bank(*jobp)
                for cb in range(CB):
                    ins = group(b[:, cb * P:(cb + 1) * P],
                                [(W[:, k, cb * P:(cb + 1) * P], hT[:, k, LAT:TOK]) for k in range(KT)])
                close(ins)

            have(pe, "xTp", 1)
            for c in range(3):
                project(("hy", c), ("hyp", c), chunk(("win", HY[c])).rearrange("p (k n) -> p k n", n=512))
            pe.wait_ge(z_ok, CB)
            for t in range(NT):
                b = open_bank("zT", t)
                lo = t * P if t < CT else LAT + 1
                for cb in range(CB):
                    ins = turn(b[:, cb * P:(cb + 1) * P], z[:, cb, lo:lo + P])
                close(ins)
            have(pe, "zT", NT - 1)
            F = chunk(("dft",), 1).rearrange("p (a t k) -> p a t k", a=2, k=LAT)
            for kt in range(NT):
                for ri in range(2):
                    b = open_bank("uf", kt, ri)
                    if kt < CT:
                        close(group(b[:, :], [(F[:, ri, t, kt * P:(kt + 1) * P], zt[:, t, :]) for t in range(CT)]))
                    else:
                        close(pe.matmul(b[:, :], dftp[:, ri, :], zt[:, CT, :], start=True, stop=True))
            for j in range(NA_FIRST, N_ADA):
                ada(j)
            pe.wait_ge(y_ok, NT)
            F = chunk(("idft",)).rearrange("p (a t k) -> p a t k", a=2, k=LAT)
            for cb in range(CB):
                b = open_bank("inv", cb)
                close(group(b[:, :], [(Y[:, kt, cb * P:(cb + 1) * P], F[:, ri, kt, :])
                                      for ri, Y in enumerate((YR, YI)) for kt in range(CT)]))
            b = open_bank("invp")
            for cb in range(CB):
                ins = group(b[:, cb * P:(cb + 1) * P], [(Y[:, CT, cb * P:(cb + 1) * P], dftp[:, 2 + ri, :])
                                                        for ri, Y in enumerate((YR, YI))])
            close(ins)
            b = open_bank("hst")
            pe.wait_ge(hsum_ok, 1)
            for t in range(NT):
                ins = pe.matmul(b[:, t:t + 1], sq[:, 0, t * P:(t + 1) * P], ones[:, 0:1], start=True, stop=True)
            close(ins)
            for ch, w in (("q", WQ), ("k", WK)):
                project((ch,), (ch + "p",), chunk(("win", w)).rearrange("p (k n) -> p k n", n=512))
            W = chunk(("win", WV)).rearrange("p (k n) -> p k n", n=512)
            for t in range(NT):
                b = open_bank("V", t)
                close(group(b[:, :], [(hT[:, k, t * P:(t + 1) * P], W[:, k, :]) for k in range(KT)]))
            have(pe, "kp")
            b = open_bank("nk")
            for cb in range(CB):
                ins = turn(b[:, cb * P:(cb + 1) * P], KTt[:, cb, LAT:TOK])
            close(ins)
            have(pe, "V", NT - 1)
            pe.wait_ge(in_ctx, 32)

            def scores(u):
                b, h = u // H, u % H
                hp, pair = h % 2 * DH, h // 2
                bk = open_bank("s", u)
                q = QT[hp:hp + DH, pair, b * P:(b + 1) * P]
                kc = ckT[hp:hp + DH, pair, :] if b < CT else KTt[hp:hp + DH, pair, LAT:TOK]
                ins = pe.matmul(bk[:, 0:P], q, kc, start=True, stop=True)
                kts = key_tiles(b)
                if kts:
                    ins = pe.matmul(bk[:, P:P * (1 + len(kts))], q,
                                    KTt[hp:hp + DH, pair, kts[0] * P:(kts[-1] + 1) * P], start=True, stop=True)
                close(ins)

            def turn_probs(u):
                bk = open_bank("pt", u)
                pe.wait_ge(pn_ok, u + 1)
                for j in range(1 + len(key_tiles(u // H))):
                    ins = turn(bk[:, j * P:(j + 1) * P], pr[:, u % 2, j * P:(j + 1) * P])
                close(ins)

            def values(u):
                b, h = u // H, u % H
                cols = slice(h * DH, (h + 1) * DH)
                hp, pair = h % 2 * DH, h // 2
                if h == 0:
                    open_bank("o", b)
                have(pe, "pt", u)
                vs = [cv[:, cols]] if b < CT else [V[:, CT, cols]]
                vs += [V[:, t, cols] for t in key_tiles(b)]
                ins = group(bank[6][hp:hp + DH, pair * P:(pair + 1) * P], [(v, PT[:, u % 2, j, :]) for j, v in enumerate(vs)])
                if h == H - 1:
                    close(ins)
                else:
                    ins.then_inc(pv_ok, 1)

            def att_stat(b):
                bk = open_bank("ast", b)
                pe.wait_ge(osum_ok, b + 1)
                close(pe.matmul(bk[:, b:b + 1], osum[:, b % 2, :], ones[:, 0:1], start=True, stop=True))

            for u in range(-2, NT * H + 1):
                if u + 2 < NT * H:
                    scores(u + 2)
                if 0 <= u < NT * H:
                    turn_probs(u)
                if u >= 1:
                    values(u - 1)
                if u - 1 >= H and (u - 1) % H == 3:
                    att_stat((u - 1) // H - 1)
            att_stat(NT - 1)
            Ws = [chunk(("wout", n)).rearrange("p (k n) -> p k n", n=512) for n in range(2)]
            pe.wait_ge(hg_ok, CB)
            pe.wait_ge(att_ok, NT)

            def route(b):
                pe.wait_ge(h2_ok, b + 1)
                for g in range(2):
                    bk = open_bank("h2T", b, g)
                    for j in range(4):
                        ins = turn(bk[:, j * P:(j + 1) * P], h2[:, b % 2, (4 * g + j) * P:(4 * g + j + 1) * P])
                    close(ins)
                have(pe, "h2T", b, 1)
                bk = open_bank("rt", b)
                close(group(bk[:, 0:NG + NE], [(h2T[:, b % 2, k, :], rw[:, k, :]) for k in range(KT)]))

            pe.wait_ge(in_small, 80)
            for b in range(NT):
                for n in range(2):
                    for job, src, k0 in (("wa", attT, 0), ("wh", hyoT, CB)):
                        bk = open_bank(job, b, n)
                        close(group(bk[:, :], [(src[:, cb, b * P:(b + 1) * P], Ws[n][:, k0 + cb, :])
                                               for cb in range(CB)]))
                if b > 0:
                    route(b - 1)
            route(NT - 1)
            A = R[:, 15]
            pe.wait_ge(assigned, 1)
            bk = open_bank("rank")
            for t in range(NT):
                ins = group(bk[:, t * NE:(t + 1) * NE], [(ones[:, :], A[:, q, :]) for q in range(t)] + [(tri[:, :], A[:, t, :])])
            close(ins)
            bk = open_bank("total")
            close(group(bk[:, 0:NE], [(ones[:, :], A[:, t, :]) for t in range(NT)]))
            have(pe, "rank")
            have(pe, "total")

            def numbers(n, s):
                pe.wait_ge(sel_ok, n + 1)
                wait_past(pe, idx_ok, n)
                group(bank[7][:, 0:1], [(sel[:, s, t, :], tid[:, t:t + 1]) for t in range(NT)]).then_inc(idx_full, 1)

            def turn_rows(n, s):
                pe.wait_ge(xg_in[s], (n - s) * 8 + 16)
                wait_past(pe, xgT_ok, n * 2)
                for g in range(2):
                    for j in range(4):
                        ins = turn(bank[g][:, j * P:(j + 1) * P], xg[:, s, (4 * g + j) * P:(4 * g + j + 1) * P])
                    ins.then_inc(xgT_full, 1)

            def expert(p, i, s, ahead2, ahead1):
                n = (i + p * pairs) * 2 + s
                w = [slot[3 * s + j].rearrange("p (k n) -> p k n", n=512 if j < 2 else D) for j in range(3)]
                arrived = (n - s) * 8 + 16
                pe.wait_ge(xgT_ok, n * 2 + 2)
                for j, freed in ((0, sil_ok), (1, hid_ok)):
                    wait_past(pe, freed, n)
                    pe.wait_ge(ew_in[3 * s + j], arrived)
                    group(bank[2 + j][:, :], [(xgT[:, s, k, :], w[j][:, k, :]) for k in range(KT)]).then_inc(gu_full, 1)
                if ahead2:
                    numbers(n + 2, s)
                if ahead1:
                    turn_rows(n + 1, 1 - s)
                pe.wait_ge(hid_ok, n + 1)
                for f in range(FE // P):
                    ins = turn(bank[4][:, f * P:(f + 1) * P], hid[:, s, f * P:(f + 1) * P])
                ins.then_inc(hidT_full, 1)
                pe.wait_ge(hidT_ok, n + 1)
                pe.wait_ge(ew_in[3 * s + 2], arrived)
                for half, freed in ((0, y_cpA), (1, y_cpD)):
                    wait_past(pe, freed, n)
                    group(bank[5 + half][:, :], [(hidT[:, s, f, :], w[2][:, f, half * 512:(half + 1) * 512])
                                                 for f in range(FE // P)]).then_inc(y_full, 1)

            def one_pass(p):
                for s in range(2):
                    numbers(p * NE + s, s)
                turn_rows(p * NE, 0)
                for s in range(2):
                    expert(p, 0, s, True, True)
                with pe.Fori(1, pairs - 1) as i:
                    for s in range(2):
                        expert(p, i, s, True, True)
                for s in range(2):
                    expert(p, pairs - 1, s, False, s == 0)
            one_pass(0)
            pe.wait_ge(route_ok, 1)
            v = pe.value_load(over[0:1, 0:1])
            with pe.If(v > 0):
                with pe.Fori(1, NT) as p:
                    one_pass(p)


def constants():
    f = np.float32
    feats, decs = [], []
    lo, hi = math.log(1e-2) / 1.5, math.log(1e-2) / 0.3
    deltas = np.abs(np.linspace(lo, hi, CH))
    fb = np.linspace(1e-4, 15, 16)[:, None]
    for L in (LAT, CTX):
        t = np.linspace(0.0, 1.0, L)[None, :]
        w = 2.0 * np.pi * np.arange(L)[None, :] / L
        feats.append(np.concatenate([t, np.cos(fb * w), -np.sin(fb * w)], axis=0))
        decs.append(np.exp(-t.T * deltas[None, :]))
    bmask = np.ones((P, NT))
    bmask[0, 0] = bmask[0, CT] = 0.0

    def transforms(L):
        n, k = np.arange(L)[:, None], np.arange(L)[None, :]
        th = np.pi * ((2 * k + 1) * n % (4 * L)) / (2 * L) * 1.0
        th = 2 * np.pi * ((2 * k + 1) * n % (4 * L)) / (4 * L)
        return np.cos(th), -np.sin(th)

    def tiles(m):
        return m.reshape(-1, P, m.shape[1]).transpose(1, 0, 2)
    c, s = transforms(LAT)
    dft = np.stack([np.stack([tiles(c), tiles(s)], 1).reshape(P, -1),
                    np.stack([tiles(c.T / LAT), tiles(s.T / LAT)], 1).reshape(P, -1)])
    c, s = transforms(CTX)
    dftp = np.stack([c, s, c.T / CTX, s.T / CTX], 1)
    maskb = np.full((P, 3, 3 * NA_COLS), -1e30)
    for kind, b in enumerate((0, 1, LAT // P - 1)):
        for p in range(P):
            qc = b * NA_COLS + p % NA_COLS
            cs = min(max(qc - NA_COLS // 2, 0), GRID_W - NA_COLS)
            kc = (b - 1) * NA_COLS + np.arange(3 * NA_COLS)
            maskb[p, kind, (kc >= cs) & (kc < cs + NA_COLS)] = 0.0
    return {
        "zf": np.concatenate(feats, 1).astype(f), "dec": np.concatenate(decs, 0).astype(f),
        "bmask": bmask.astype(f), "dft": dft.astype(f), "dftp": dftp.astype(f), "maskb": maskb.astype(f),
        "iota": np.tile(np.arange(P, dtype=np.float16), (P, 1)),
        "tid": (np.arange(NT)[None, :] * P + np.arange(P)[:, None]).astype(np.float16),
    }


def kernel(**inp):
    import concourse.bacc as bacc
    from concourse.bass_utils import run_bass_kernel_spmd

    g = {k: np.asarray(v) for k, v in inp.items()}

    def cols(v):
        return v.reshape(-1, P).T
    latent = g["x_sample"][0].reshape(ROWS, CT, NA_COLS, D).transpose(1, 0, 2, 3).reshape(LAT, D)
    taps = np.stack([*g["conv_w"][0], g["conv_b"][0]], 0)
    padded = np.pad(g["rpb"][0], ((0, 0), (0, 0), (NA_COLS, NA_COLS)))
    shifted = np.stack([padded[:, :, NA_COLS - 1 - c:4 * NA_COLS - 1 - c] for c in range(NA_COLS)], 0)
    arrays = {
        "x": np.concatenate([latent, g["x_prompt"][0]], 0),
        "cond": np.stack([cols(g["c"][0]), cols(g["c_ctx"])], 2),
        "ck": g["cache_k"][0, 0].reshape(CTX, CH), "cv": g["cache_v"][0, 0].reshape(CTX, CH),
        "w_ada": g["w_ada"][0], "b2": np.broadcast_to(g["b_ada"], (2, 6 * D)), "w_in": g["w_in"][0],
        "w_out": g["w_out"][0], "w_gate": g["w_gate"][0], "w_up": g["w_up"][0], "w_down": g["w_down"][0],
        "g1c": cols(g["norm1_g"][0]), "g2r": np.broadcast_to(g["norm2_g"], (2, D)), "fg": g["final_g"],
        "cwb": np.stack([taps[:, (c - WX0) * CH:(c - WX0 + 1) * CH].reshape(4, CB, P).transpose(2, 1, 0) for c in HY], 1),
        "chn": np.stack([cols(g["hyena_skip"][0]), cols(g["gnorm_hyena"][0]), cols(g["gnorm_att"][0])], 1),
        "w1": g["filt_w1"][0], "w2": g["filt_w2"][0], "w3": g["filt_w3"][0],
        "mlp_c": np.stack([g["filt_b1"][0], g["filt_b2"][0], g["filt_freq"][0]], 1),
        "rw": np.concatenate([g["router_grp_w"][0], g["router_exp_w"][0]], 1),
        "rb": np.concatenate([g["router_grp_b"][0], g["router_exp_b"][0]], 0),
        "rpb": shifted.reshape(NA_COLS, H, -1),
        **constants(),
    }
    nc = bacc.Bacc("TRN2", target_bir_lowering=False, num_devices=1)
    a, sent = {}, {}
    for name, v in arrays.items():
        v = np.ascontiguousarray(v)
        sent["in_" + name] = v
        a[name] = nc.dram_tensor("in_" + name, v.shape, mybir.dt.from_np(v.dtype), kind="ExternalInput").ap()
    shapes = {"y": (TOK, D), "k": (CTX, CH), "v": (CTX, CH)}
    outs = {n: nc.dram_tensor("out_" + n, s, F32, kind="ExternalOutput").ap() for n, s in shapes.items()}
    program(nc, a, outs)
    r = run_bass_kernel_spmd(nc, [sent], core_ids=[0]).results[0]
    y = r["out_y"]
    ys = y[:LAT].reshape(CT, ROWS, NA_COLS, D).transpose(1, 0, 2, 3).reshape(1, LAT, D)
    kv = (1, 1, CTX, H, DH)
    return y[LAT:].reshape(1, CTX, D), ys, r["out_k"].reshape(kv), r["out_v"].reshape(kv)
```

```python
import math
from contextlib import ExitStack

import numpy as np

import concourse.bass as bass
from concourse import mybir

F32 = mybir.dt.float32
F16 = mybir.dt.float16
F32R = mybir.dt.float32r
I32 = mybir.dt.int32
U32 = mybir.dt.uint32
ALU = mybir.AluOpType
ACT = mybir.ActivationFunctionType
AX = mybir.AxisListType.X

P = 128
D = 1024
KT = D // P
LAT, CTX = 512, 128
TOK = LAT + CTX
NT = TOK // P
CT = NT - 1
H, DH = 8, 64
CH = 512
CB = CH // P
GRID_W, NA_ROWS, NA_COLS = 64, 8, 16
ROWS = LAT // GRID_W
FF, EMB = 64, 33
NG, EPG = 4, 4
NE = NG * EPG
FE = 512
EPS = 1e-6
TWO_PI = 2.0 * math.pi
ROUND = 1.5 * 2.0 ** 23
PI_A = float(np.float32(6.28125))
PI_B = float(np.float32(np.float32(1.9353071795e-3) * 1.0))
PI_B = float(np.floor(PI_B * 2 ** 22) / 2 ** 22)
PI_C = float(np.float32(TWO_PI - PI_A - PI_B))
CAP = 128
QW = 1024
HALVES = 2
WQ, WK, WV, WX0, WX1, WVH = range(6)
HY = [WVH, WX1, WX0]
NA_FIRST = 4
N_ADA = 12


def key_tiles(b):
    return [t for t in (b - 1, b, b + 1) if 0 <= t < CT] if b < CT else []


def psum_jobs():
    jobs = []
    turn = [0]

    def add(name, eng, bank=None):
        if bank is None:
            bank = turn[0] % 6
            turn[0] += 1
        jobs.append((name, bank, eng))

    for layer in range(2):
        for i in range(2):
            add((f"mlp{layer + 1}", i), "dve")
        if layer == 0:
            add(("ckT",), "act")
        add(("ada", layer), "dve")
    for t in range(NT):
        for d in range(2):
            add(("filt", t, d), "dve")
    for j in range(2, NA_FIRST):
        add(("ada", j), "dve")
    add(("mcol",), "dve", 6)
    for kt in range(NT):
        for ri in range(2):
            add(("kf", kt, ri), "act")
    for k in range(KT):
        add(("xT", k), "dve")
    for g in range(2):
        add(("xTp", g), "dve")
    for c in range(3):
        for cb in range(CB):
            add(("hy", c, cb), "act")
        add(("hyp", c), "act")
    for t in range(NT):
        add(("zT", t), "act")
    for kt in range(NT):
        for ri in range(2):
            add(("uf", kt, ri), "dve")
    for j in range(NA_FIRST, N_ADA):
        add(("ada", j), "dve")
    for cb in range(CB):
        add(("inv", cb), "dve")
    add(("invp",), "dve")
    for c in "qk":
        for cb in range(CB):
            add((c, cb), "act")
        add((c + "p",), "act")
        if c == "q":
            add(("hst",), "dve")
    for t in range(NT):
        add(("V", t), "act")
    add(("nk",), "act")
    units = [(b, h) for b in range(NT) for h in range(H)]
    for u in range(-2, len(units) + 1):
        if u + 2 < len(units):
            add(("s", u + 2), "dve", (u + 2) % 3)
        if 0 <= u < len(units):
            add(("pt", u), "act", 3 + u % 3)
        if u >= 1 and (u - 1) % H == H - 1:
            add(("o", (u - 1) // H), "dve", 6)
        if u - 1 >= H and (u - 1) % H == 3:
            add(("ast", (u - 1) // H - 1), "dve", 7)
    add(("ast", NT - 1), "dve", 7)
    turn[0] = 0
    for b in range(NT + 2):
        for n in range(2):
            if b < NT:
                add(("wa", b, n), "dve")
                add(("wh", b, n), "dve")
            if n == 0 and b > 1:
                for g in range(2):
                    add(("h2T", b - 2, g), "act")
                add(("rt", b - 2), "dve", 6)
    add(("rank",), "dve", 7)
    add(("total",), "dve", 6)
    return jobs


JOBS = psum_jobs()
JOB = {name: i for i, (name, _, _) in enumerate(JOBS)}
ORD = {}
for _name, _bank, _eng in JOBS:
    ORD[_name] = 1 + sum(1 for n in ORD if JOBS[JOB[n]][2] == _eng)

CHUNKS = ([("ada", j) for j in range(NA_FIRST)] + [("dft",)] + [("win", c) for c in HY] + [("dft",)]
          + [("ada", j) for j in range(NA_FIRST, N_ADA)] + [("idft",)]
          + [("win", c) for c in (WQ, WK, WV)] + [("wout", n) for n in range(2)])
NRING = 4
NCH = len(CHUNKS)
ESLOTS = 6
PROJ = [(w, next(i for i, c in enumerate(CHUNKS) if c == ("win", w))) for w in HY + [WQ, WK, WV]]
WIN_KB = [[167, 171, 140, 178], [182, 186, 190, 194], [167, 171, 140, 178],
          [147, 151, 155, 159], [163, 167, 188, 192], [171, 178, 182, 163]]
HYROW = range(3)


def last_jobs():
    seen, out = 0, []
    for c in CHUNKS:
        if c[0] == "dft":
            out.append(("kf", CT - 1, 1) if seen == 0 else ("uf", CT - 1, 1))
            seen += 1
        elif c[0] == "ada":
            out.append(c)
        elif c[0] == "idft":
            out.append(("inv", CB - 1))
        elif c[0] == "wout":
            out.append(("wh", NT - 1, c[1]))
        elif c[1] in HY:
            out.append(("hyp", HY.index(c[1])))
        else:
            out.append({WQ: ("qp",), WK: ("kp",), WV: ("V", NT - 1)}[c[1]])
    return out


LAST_JOB = last_jobs()
FIRST_USE = {}
for _i, _c in enumerate(CHUNKS):
    FIRST_USE.setdefault(_c, []).append(_i)


def program(nc, a, outs):
    ctx = ExitStack()
    with ctx:
        def sb(name, shape, dt=F32):
            return ctx.enter_context(nc.sbuf_tensor(name, shape, dt))

        def sem(name):
            return ctx.enter_context(nc.semaphore(name))

        bank = [ctx.enter_context(nc.psum_tensor(f"bank{i}", [P, 512], F32)) for i in range(8)]
        KB = 256

        def part(name, kb, shape, dt=F32R):
            if not kb:
                with nc.sbuf_tensor(name, shape, dt) as t:
                    return t
            with nc.sbuf_tensor(name + "_before", [P, int(kb * KB)], F32), nc.sbuf_tensor(name, shape, dt) as t:
                return t
        xgTh, xgTl = part("xgTh", 92, [P, KT, P]), part("xgTl", 96, [P, KT, P])
        hidTh, hidTl = part("hidTh", 100, [P, FE // P, P]), part("hidTl", 102, [P, FE // P, P])
        hT = part("hT", 84, [P, KT, TOK], F32)
        hTh, hTl = part("hTh", 64, [P, KT, TOK]), part("hTl", 84, [P, KT, TOK])
        WP = [[part(f"WP{c}{r}", kb, [P, QW]) for r, kb in enumerate(kbs)] for c, kbs in enumerate(WIN_KB)]
        WH = part("WH", 128, [P, HALVES, 4, QW])
        slot_kb = [0, 16, 32, 48, 164, 180]
        slot = [part(f"slot{i}", kb, [P, 4 * QW], F32)[:, :] for i, kb in enumerate(slot_kb)]
        WL = [part(f"WL{i}", kb, [P, 4, QW]) for i, kb in enumerate(slot_kb)]
        big = sb("big", [P, 198 * KB])

        def at(kb, *shape):
            n = int(np.prod(shape))
            v = big[:, int(kb * KB):int(kb * KB) + n]
            if len(shape) == 1:
                return v
            names = "abcd"[:len(shape)]
            return v.rearrange(f"p ({' '.join(names)}) -> p {' '.join(names)}",
                               **{x: s for x, s in zip(names[1:], shape[1:])})

        x = at(64, NT, D)
        s_flt, d_flt = at(104, NT, CH), at(114, NT, CH)
        dec = at(124, NT, CH)
        zf = at(134, TOK)
        mw3 = at(136.5, 2 * CH)
        mh = [at(140.5, TOK), at(143, TOK)]
        KR, KI = at(147, NT, CH), at(157, NT, CH)
        mtmp = [at(167, TOK), at(169.5, TOK)]
        fbuf = at(172, 2, CH)
        xn = at(178, NT, D)
        UW = 644
        ustrip = at(104, CB, UW)
        z = at(114.25, CB, UW)
        x0 = at(124.5, CB, UW)
        ctmp = at(134.75, 2, UW)
        zt = at(178, NT, CH)
        YR, YI = at(188, NT, CH), at(167, NT, CH)
        ytmp = at(140, 2, CH)
        hyoT = at(104, CB, TOK)
        sq = at(178, CB, TOK)
        t1 = at(140, 2, TOK)
        QT, KTt = at(114.25, CB, TOK), at(124.5, CB, TOK)
        V = at(134.75, NT, CH)
        nkb = at(188, CH)
        base = at(145, H, NA_ROWS, 3 * NA_COLS)
        Tm = at(157, 3, 512)
        pr = at(164, 2, 512)
        PT = at(168, 2, 4, P)
        sc = at(172, 2, 512)
        oraw = at(176, 2, CB, P)
        osq = at(184, CB, P)
        osum = at(163, 2, P)
        attT = at(186, CB, TOK)
        gt1 = at(84, 2, D)
        G2 = at(92, 2, D)
        SH2 = [at(180, D), at(100, D)]
        wtmp = at(122.25, 2, 2, 512)
        h2 = at(130.5, 2, D)
        h2T = at(138.5, 2, KT, P)
        xg = at(84, 2, D)
        hid = at(104, FE)
        sil = at(106, FE)
        yout = at(108, 2, D)
        gt2 = at(116, 2, D)
        fg = at(124, D)
        ya, yb = at(0, NT, D), at(20, NT, D)
        sqd = at(147, D)

        ident = sb("ident", [P, P])
        b_buf = [at(147, 2, 512)[0:2], at(104, 2, 512)[0:2]]
        mrow = [at(151, 2, 512)[0:2], at(108, 2, 512)[0:2]]
        g2row = at(112, 512)[0:2]
        ckT = sb("ckT", [P, CB, P])
        craw = at(176, CH)
        cv = at(196, CH)
        cond = sb("cond", [P, KT, 2])
        scond = sb("scond", [P, KT, 2])
        csig = sb("csig", [P, KT, 2])
        mcol = sb("mcol", [P, 2, KT, 2])
        g1c = sb("g1c", [P, KT])
        cwb = sb("cwb", [P, 3, CB, 4])
        chn = sb("chn", [P, 3, CB])
        mlp_c = sb("mlp_c", [FF, 3])
        mlp_f = sb("mlp_f", [FF, 2])
        w12 = sb("w12", [FF, 2, FF])
        bmask = sb("bmask", [P, NT])
        maskb = sb("maskb", [P, 3, 3 * NA_COLS])
        dftp = sb("dftp", [P, 4, P])
        ones = sb("ones", [P, P])
        tri = sb("tri", [P, P])
        iota = sb("iota", [P, P], F16)
        tid = sb("tid", [P, NT], F16)
        rw = sb("rw", [P, KT, NG + NE])
        rb = sb("rb", [P, NG + NE])
        ss = sb("ss", [P, 8, NT])
        rmx = sb("rmx", [P, 4])
        nmx = sb("nmx", [P, 4])
        rsum = sb("rsum", [P, 4])
        rinv = sb("rinv", [P, 4])
        lg = sb("lg", [P, NT, NG + NE])
        R = at(151, 16, NT, NE)
        rankm = sb("rankm", [P, NT, NE])
        posf = sb("posf", [P, 2, NT])
        posi = sb("posi", [P, 2, NT], I32)
        wts = sb("wts", [P, 2, NT])
        over = sb("over", [1, 1], I32)
        rsh = sb("rsh", [P, 2, NT])
        sel = at(160, 2, NT, P // 2).bitcast(F16)
        idx = sb("idx", [P, 2], I32)

        m_dram = nc.dram_tensor("m_scratch", [2, 6 * D], F32).ap()
        h2_dram = nc.dram_tensor("h2_scratch", [TOK, D], F32).ap()
        y_dram = nc.dram_tensor("y_scratch", [NT * NE * P, D], F32).ap()

        hTh_ok, hTl_ok = sem("hT_high_ok"), sem("hT_low_ok")
        wp_high, wp_low = sem("w_in_high_ok"), sem("w_in_low_ok")
        pe_full = sem("pe_bank_full")
        drained = {"act": sem("act_bank_drained"), "dve": sem("dve_bank_drained")}
        chunk_in = [sem(f"chunk_in{i}") for i in range(NRING)]
        in_mlp, in_dec, in_cond, in_small, in_x, in_base, in_ctx = (
            sem(n) for n in ("in_mlp", "in_dec", "in_cond", "in_small", "in_x", "in_base", "in_ctx"))
        in_dft = sem("in_dft")
        b_in = [sem("b_ada_in0"), sem("b_ada_in1")]
        m_out = [sem("m_row_out0"), sem("m_row_out1")]
        gt1_in, g2_in, sh2_in, tail_in = sem("gt1_in"), sem("g2_in"), sem("sh2_in"), sem("tail_in")
        act_chain, dve_chain, pool_chain = sem("act_chain"), sem("dve_chain"), sem("pool_chain")
        consts_ok = sem("consts_ok")
        cond_ok = sem("cond_ok")
        sin_arg, sin_ok = sem("sin_arg"), sem("sin_ok")
        filt_ok = sem("filt_ok")
        x_rt, x_rs, xn_ok = sem("x_rt"), sem("x_rs"), sem("xn_ok")
        conv_ok, z_ok = sem("conv_ok"), sem("z_ok")
        tap_ok = sem("conv_tap_ok")
        y_ok = sem("y_ok")
        hyo_ok, hsq_ok, hg_ok = sem("hyo_ok"), sem("hsq_ok"), sem("hyena_gained")
        hrt = sem("h_root")
        kv_out = sem("kv_out")
        tm_ok = sem("bias_ok")
        mx_ok, p_ok = sem("mx_ok"), sem("p_ok")
        att_rt = sem("att_root")
        pv_ok = sem("pv_ok")
        wt2_ok = sem("x1_ok")
        n_rt, h2_ok = sem("n_rt"), sem("h2_ok")
        h2_out = [sem("h2_out0"), sem("h2_out1")]
        route_e, route_a, route_ok = sem("route_exp_arg"), sem("route_exp_ok"), sem("route_ok")
        ew_in = [sem(f"expert_w_in{i}") for i in range(ESLOTS)]
        epsb = sb("epsb", [P, 1])
        mrow_used = sem("mod_row_turned")
        att_ok = sem("att_ok")
        assigned, shifted = sem("assigned"), sem("ranks_shifted")
        g2_done = sem("gain2_done")
        gather_go = sem("gather_go")
        sel_ok, idx_full, idx_ok = sem("sel_ok"), sem("idx_full"), sem("idx_ok")
        xg_in = [sem("xg_in0"), sem("xg_in1")]
        high_ok = [sem(f"weight_high_ok_{w}") for w in ("gate", "up", "down")]
        low_ok = [sem(f"weight_low_ok_{w}") for w in ("gate", "up", "down")]
        used = [sem(f"weight_used_{w}") for w in ("gate", "up", "down")]
        xgT_full, xh_ok, xl_ok = sem("xgT_full"), sem("xgT_high_ok"), sem("xgT_low_ok")
        sil_ok, hid_ok = sem("silu_ok"), sem("hid_ok")
        hidT_full, hh_ok, hl_ok = sem("hidT_full"), sem("hidT_high_ok"), sem("hidT_low_ok")
        y_out = [sem("y_out0"), sem("y_out1")]
        yab_in = [sem(f"results_in{t}") for t in range(NT)]
        f_a, f_b, f_c = sem("first_weighted"), sem("results_summed"), sem("gated")
        g2row_in, pn_ok = sem("g2row_in"), sem("probs_normed")
        osq_ok, osum_ok, hsum_ok = sem("osq_ok"), sem("osum_ok"), sem("hsum_ok")
        stores_ok = sem("stores_ok")
        strip_ok = sem("strip_ok")
        y_cpA, y_cpD = sem("y_copied_act"), sem("y_copied_dve")
        f_cmb, f_rt, f_ok, f_out = sem("f_cmb"), sem("f_rt"), sem("f_ok"), sem("f_out")

        def full(eng, *name):
            eng.wait_ge(pe_full, JOB[name] + 1)
            return bank[JOBS[JOB[name]][1]]

        def have(eng, *name):
            eng.wait_ge(drained[JOBS[JOB[name]][2]], ORD[name])

        def drain(ins, *name):
            return ins.then_inc(drained[JOBS[JOB[name]][2]], 1)

        def wait_past(eng, sema, count):
            if not isinstance(count, int) or count > 0:
                eng.wait_ge(sema, count)

        def win_high(act, c, r):
            i = PROJ[c][1]
            act.wait_ge(chunk_in[i % NRING], 16 * (i // NRING + 1))
            act.copy(WP[c][r][:, :], slot[i % NRING][:, r * QW:(r + 1) * QW]).then_inc(wp_high, 1)

        def win_low(dve, c, r):
            i = PROJ[c][1]
            dve.wait_ge(wp_high, 4 * c + r + 1)
            dve.tensor_tensor(WL[i % NRING][:, r, :], slot[i % NRING][:, r * QW:(r + 1) * QW],
                              WP[c][r][:, :].bitcast(F32), ALU.subtract).then_inc(wp_low, 1)

        def expert_steps(eng, p, step):
            for m in range(3):
                step(p, m // 2, m % 2, m)
            with eng.Fori(1, pairs - 2) as i:
                step(p, i, 1)
                step(p, i + 1, 0)
            for m in range(NE - 3, NE + 1):
                step(p, m // 2, m % 2, m)

        def quarter(s, w, r):
            return slot[3 * s + w][:, r * QW:(r + 1) * QW]

        def high_half(w, s):
            return s if w == 0 else 1 - s

        def wait_pv(eng, u):
            if u % H == H - 1:
                full(eng, "o", u // H)
            else:
                eng.wait_ge(pv_ok, u // H * (H - 1) + u % H + 1)

        def turned_h2(act, b):
            for g in range(2):
                bk = full(act, "h2T", b, g)
                if b >= 2:
                    full(act, "rt", b - 2)
                drain(act.copy(h2T[:, b % 2, 4 * g:4 * g + 4, :].rearrange("p a b -> p (a b)"), bk[:, :]), "h2T", b, g)

        def chunk_src(c):
            if c[0] == "dft":
                return a["dft"][0]
            if c[0] == "idft":
                return a["dft"][1]
            w = {"ada": a["w_ada"], "win": a["w_in"], "wout": a["w_out"]}[c[0]]
            return w[:, c[1] * 512:(c[1] + 1) * 512].rearrange("(k p) n -> p k n", p=P)

        def chunk_view(i):
            return slot[i % NRING].rearrange("p (k n) -> p k n", n=512)

        pairs = NE // 2

        block = ctx.enter_context(nc.Block())

        @block.sync
        def _(sp):
            sp.dma_start(zf[0:EMB, :], a["zf"]).then_inc(in_mlp, 16)
            sp.dma_start(w12[0:EMB, 0, :], a["w1"]).then_inc(in_mlp, 16)
            sp.dma_start(w12[:, 1, :], a["w2"]).then_inc(in_mlp, 16)
            sp.dma_start(mlp_c[:, :], a["mlp_c"]).then_inc(in_mlp, 16)
            sp.dma_start(mw3[0:FF, :], a["w3"]).then_inc(in_mlp, 16)

            def load_chunk(i):
                if i >= NRING:
                    full(sp, *LAST_JOB[i - NRING])
                src = chunk_src(CHUNKS[i])
                if len(src.shape) == 2:
                    src = src.rearrange("p (k n) -> p k n", n=512)
                sp.dma_start(chunk_view(i), src).then_inc(chunk_in[i % NRING], 16)

            load_chunk(0)
            sp.dma_start(dec, a["dec"].rearrange("(t p) n -> p t n", p=P)).then_inc(in_dec, 16)
            sp.dma_start(bmask[:, :], a["bmask"]).then_inc(in_dec, 16)
            load_chunk(1)
            sp.dma_start(x, a["x"].rearrange("(t p) n -> p t n", p=P)).then_inc(in_x, 16)
            load_chunk(2)
            sp.dma_start(dftp[:, :, :], a["dftp"]).then_inc(in_dft, 16)
            for i in range(3, NCH):
                load_chunk(i)
            full(sp, "V", NT - 1)
            sp.dma_start(x, a["x"].rearrange("(t p) n -> p t n", p=P)).then_inc(in_x, 16)
            wg, wu, wd = a["w_gate"], a["w_up"], a["w_down"]

            def load_expert(e, s, ended=None):
                for j, w in enumerate((wg, wu, wd)):
                    if ended is not None:
                        sp.wait_ge(used[j], ended * 4)
                    src = w[bass.ds(e, 1), :, :] if not isinstance(e, int) else w[e:e + 1, :, :]
                    n = 512 if j < 2 else 1024
                    src = src.rearrange("a (k p) n -> p (a k) n", p=P)
                    sp.dma_start(slot[3 * s + j].rearrange("p (k n) -> p k n", n=n), src)\
                      .then_inc(ew_in[3 * s + j], 16)
            full(sp, *LAST_JOB[-1])
            load_expert(0, 0)
            sp.wait_ge(h2_ok, NT)
            load_expert(1, 1)
            with sp.Fori(1, pairs) as i:
                for s in range(2):
                    load_expert(i * 2 + s, s, i * 2 + (s - 1))
            sp.wait_ge(route_ok, 1)
            v = sp.value_load(over[0:1, 0:1])
            with sp.If(v > 0):
                with sp.Fori(1, NT) as t:
                    with sp.Fori(0, pairs) as i:
                        for s in range(2):
                            load_expert(i * 2 + s, s, (t * pairs + i) * 2 + (s - 1))
            for t in range(NT):
                sp.wait_ge(f_ok, t + 1)
                sp.dma_start(outs["y"][t * P:(t + 1) * P, :], x[:, t, :]).then_inc(f_out, 16)
            sp.wait_ge(f_out, 16 * NT)
            sp.wait_ge(kv_out, 32)

        @block.gpsimd
        def _(pool):
            n_chain = [0]

            def link(ins):
                n_chain[0] += 1
                ins.then_inc(pool_chain, 1)
                pool.wait_ge(pool_chain, n_chain[0])

            link(pool.memset(ident[:, :], 0.0))
            link(pool.affine_select(out=ident[:, :], in_=ident[:, :], compare_op=ALU.not_equal, fill=1.0,
                                    base=0, pattern=[[-1, P]], channel_multiplier=1))
            link(pool.memset(ones[:, :], 1.0))
            link(pool.affine_select(out=tri[:, :], in_=ones[:, :], compare_op=ALU.is_gt, fill=0.0,
                                    base=0, pattern=[[1, P]], channel_multiplier=-1))
            pool.memset(over[:, :], 0).then_inc(consts_ok, 1)
            pool.dma_start(rw[:, :, :], a["rw"].rearrange("(k p) n -> p k n", p=P)).then_inc(in_small, 16)
            pool.dma_start(rb[:, :], a["rb"].partition_broadcast(P)).then_inc(in_small, 16)
            pool.dma_start(iota[:, :], a["iota"]).then_inc(in_small, 16)
            pool.dma_start(tid[:, :], a["tid"]).then_inc(in_small, 16)
            pool.dma_start(maskb[:, :, :], a["maskb"]).then_inc(in_small, 16)
            have(pool, "invp")
            have(pool, "hst")
            for r in range(ROWS):
                pool.dma_start(base[r * NA_COLS:(r + 1) * NA_COLS].rearrange("p h r c -> p h (r c)"),
                               a["rpb"][:, :, (NA_ROWS - 1 - r) * 3 * NA_COLS:(2 * NA_ROWS - 1 - r) * 3 * NA_COLS])\
                    .then_inc(in_base, 16)
            link(pool.memset(Tm, 0.0))
            pool.wait_ge(in_small, 5 * 16)
            pool.wait_ge(in_base, 16 * ROWS)

            def load_modulations():
                for q in m_out:
                    pool.wait_ge(q, 8 * (N_ADA - NA_FIRST))
                have(pool, "V", NT - 1)
                full(pool, "hst")
                for c in range(2):
                    for dst, v, s_in in ((gt1[:, c, :], 2, gt1_in), (G2[:, c, :], 4, g2_in), (SH2[c], 3, sh2_in)):
                        pool.dma_start(dst, m_dram[c:c + 1, v * D:(v + 1) * D].rearrange("a n -> (a n)")
                                       .partition_broadcast(P)).then_inc(s_in, 16)

            for u in range(CT * H):
                b, h = u // H, u % H
                if u >= 3:
                    have(pool, "s", u - 3)
                kts = key_tiles(b)
                kind = 0 if b == 0 else 2 if b == CT - 1 else 1
                for j, t in enumerate(kts):
                    dt = t - b + 1
                    out = Tm[:, u % 3, P * (1 + j):P * (2 + j)].rearrange("p (r c) -> p r c", c=NA_COLS)
                    in0 = base[:, h, :, dt * NA_COLS:(dt + 1) * NA_COLS]
                    in1 = maskb[:, kind, dt * NA_COLS:(dt + 1) * NA_COLS].unsqueeze(1)\
                        .broadcast_to([P, NA_ROWS, NA_COLS])
                    last = pool.tensor_tensor(out, in0, in1, ALU.add)
                last.then_inc(tm_ok, 1)
                if u == 3:
                    load_modulations()
            def store_h2(b):
                pool.wait_ge(h2_ok, b + 1)
                pool.dma_start(h2_dram[b * P:(b + 1) * P, :], h2[:, b % 2, :]).then_inc(h2_out[b % 2], 16)

            pool.wait_ge(gt1_in, 32)
            pool.wait_ge(in_x, 32)
            for b in range(NT):
                for n in range(2):
                    i = 2 * b + n
                    have(pool, "wh", b, n)
                    w = wtmp[:, i % 2, 0, :]
                    link(pool.tensor_tensor(w, w, gt1[:, b // CT, n * 512:(n + 1) * 512], ALU.mult))
                    pool.tensor_tensor(x[:, b, n * 512:(n + 1) * 512], x[:, b, n * 512:(n + 1) * 512], w,
                                       ALU.add).then_inc(wt2_ok, 1)
                if b > 0:
                    store_h2(b - 1)
            store_h2(NT - 1)
            pool.wait_ge(h2_out[0], 16 * 3)
            pool.wait_ge(h2_out[1], 16 * 2)

            def gather(n, s):
                pool.wait_ge(idx_ok, n + 1)
                wait_past(pool, xgT_full, n * 2 - 2)
                pool.sem_inc(gather_go, 1)
                pool.indirect_dma_start(out=xg[:, s, :], out_offset=None, in_=h2_dram,
                                        in_offset=bass.IndirectOffsetOnAxis(ap=idx[:, s:s + 1].bitcast(U32), axis=0))\
                    .then_inc(xg_in[s], 16)

            def load_tail():
                for c in range(2):
                    pool.dma_start(gt2[:, c, :], m_dram[c:c + 1, 5 * D:6 * D].rearrange("a n -> (a n)")
                                   .partition_broadcast(P)).then_inc(tail_in, 16)
                pool.dma_start(fg, a["fg"].partition_broadcast(P)).then_inc(tail_in, 16)

            def one_pass(p, then=None):
                for s in range(2):
                    gather(p * NE + s, s)
                if then is not None:
                    then()
                with pool.Fori(0, pairs - 1) as i:
                    for s in range(2):
                        gather((i + p * pairs) * 2 + (s + 2), s)
            one_pass(0, load_tail)
            pool.wait_ge(route_ok, 1)
            v = pool.value_load(over[0:1, 0:1])
            with pool.If(v > 0):
                with pool.Fori(1, NT) as p:
                    one_pass(p)
            pool.wait_ge(stores_ok, 1)

            def results(table):
                for t in range(NT):
                    for k, buf in enumerate((ya, yb)):
                        pool.indirect_dma_start(out=buf[:, t, :], out_offset=None, in_=table,
                                                in_offset=bass.IndirectOffsetOnAxis(ap=posi[:, k, t:t + 1].bitcast(U32), axis=0))\
                            .then_inc(yab_in[t], 16)
            with pool.If(v > 0):
                results(y_dram)
            with pool.Else():
                results(y_dram[0:NE * P, :])
            pool.wait_ge(tail_in, 48)
            for t in range(NT):
                pool.wait_ge(f_b, t + 1)
                pool.tensor_tensor(yb[:, t, :], yb[:, t, :], gt2[:, t // CT, :], ALU.mult).then_inc(f_c, 1)

        @block.scalar
        def _(act):
            n_chain = [0]

            def link(ins):
                n_chain[0] += 1
                ins.then_inc(act_chain, 1)
                act.wait_ge(act_chain, n_chain[0])

            act.dma_start(cond[:, :, :], a["cond"]).then_inc(in_cond, 16)
            act.dma_start(craw, a["ck"]).then_inc(in_ctx, 16)
            act.dma_start(g1c[:, :], a["g1c"]).then_inc(in_cond, 16)
            act.dma_start(cwb[:, :, :, :], a["cwb"]).then_inc(in_cond, 16)
            act.dma_start(chn[:, :, :], a["chn"]).then_inc(in_cond, 16)
            act.wait_ge(in_cond, 64)
            act.activation(scond[:, :, :], cond[:, :, :], ACT.Silu).then_inc(cond_ok, 1)

            def load_bias(j):
                r = 0 if j < NA_FIRST else 1
                act.dma_start(b_buf[r][:, j % 2, :], a["b2"][:, j * 512:(j + 1) * 512]).then_inc(b_in[j % 2], 16)
            load_bias(0)
            load_bias(1)
            for layer in range(2):
                act.wait_ge(sin_arg, layer + 1)
                act.activation(mh[layer][0:FF, :], mtmp[0][0:FF, :], ACT.Sin).then_inc(sin_ok, 1)
                if layer == 0:
                    b = full(act, "ckT")
                    drain(act.copy(ckT[:, :, :].rearrange("p a b -> p (a b)"), b[:, :]), "ckT")
                have(act, "ada", layer)
                load_bias(layer + 2)
            act.wait_ge(in_x, 16)
            for t in range(NT):
                link(act.activation(xn[:, t, :], x[:, t, :], ACT.Square, scale=1.0 / 32.0,
                                    accum_out=ss[:, 0, t:t + 1]))
            act.wait_ge(consts_ok, 2)
            act.activation(ss[:, 1, :], ss[:, 0, :], ACT.Sqrt, bias=epsb[:, :]).then_inc(x_rt, 1)
            for kt in range(NT):
                for ri, K in enumerate((KR, KI)):
                    b = full(act, "kf", kt, ri)
                    drain(act.copy(K[:, kt, :], b[:, :]), "kf", kt, ri)
                if kt == 0:
                    act.wait_ge(x_rs, 1)
                act.activation(xn[:, kt, :], x[:, kt, :], ACT.Copy, scale=ss[:, 2, kt:kt + 1]).then_inc(xn_ok, 1)
            win_high(act, 0, 0)
            win_high(act, 0, 1)
            win_high(act, 0, 2)
            for k in range(KT):
                have(act, "xT", k)
                act.copy(hTh[:, k, 0:LAT], hT[:, k, 0:LAT]).then_inc(hTh_ok, 1)
            full(act, "xTp", 1)
            win_high(act, 0, 3)
            have(act, "xTp", 1)
            act.copy(hTh[:, :, LAT:TOK], hT[:, :, LAT:TOK]).then_inc(hTh_ok, 1)
            for c in range(3):
                for cb in range(CB):
                    b = full(act, "hy", c, cb)
                    if c == 0 and cb == 0:
                        act.wait_ge(strip_ok, 3)
                    if c > 0:
                        act.wait_ge(conv_ok, (c - 1) * CB + cb + 1)
                    dst = ustrip[:, cb, 1:1 + LAT].rearrange("p (r b c) -> p b r c", r=ROWS, c=NA_COLS)
                    drain(act.copy(dst, b[:, :].rearrange("p (b r c) -> p b r c", r=ROWS, c=NA_COLS)), "hy", c, cb)
                    if c == 1:
                        full(act, "hyp", 0)
                    if c < 2:
                        win_high(act, c + 1, cb)
                b = full(act, "hyp", c)
                drain(act.copy(ustrip[:, :, LAT + 2:LAT + 2 + CTX],
                               b[:, :].rearrange("p (a n) -> p a n", n=CTX)), "hyp", c)
                have(act, "hyp", c)
                for cb in range(CB):
                    dst = (z[:, cb], ctmp[:, cb % 2], x0[:, cb])[c][:, 0:UW - 3]
                    if c == 1 and cb >= 2:
                        act.wait_ge(z_ok, cb - 1)
                    act.activation(dst, ustrip[:, cb, 1:UW - 2], ACT.Identity, scale=cwb[:, HYROW[c], cb, 1:2],
                                   bias=cwb[:, HYROW[c], cb, 3:4]).then_inc(tap_ok, 1)
            for t in range(NT):
                b = full(act, "zT", t)
                drain(act.copy(zt[:, t, :], b[:, :]), "zT", t)
            act.wait_ge(conv_ok, 3 * CB)
            load_bias(4)
            load_bias(5)
            act.dma_start(g2row, a["g2r"][:, 0:512]).then_inc(g2row_in, 16)
            for j in range(NA_FIRST, N_ADA):
                have(act, "ada", j)
                if j in (8, 9):
                    act.wait_ge(g2_done, j - 7)
                act.dma_start(m_dram[:, j * 512:(j + 1) * 512], mrow[1][:, j % 2, :]).then_inc(m_out[j % 2], 16)
                if j + 2 < N_ADA:
                    load_bias(j + 2)
                if j == 8:
                    act.dma_start(g2row, a["g2r"][:, 512:1024]).then_inc(g2row_in, 16)
            act.wait_ge(y_ok, NT)
            for r in range(4):
                win_high(act, 3, r)
            for cb in range(CB):
                act.wait_ge(hyo_ok, CB)
                act.activation(sq[:, cb, :], hyoT[:, cb, :], ACT.Square).then_inc(hsq_ok, 1)
            full(act, "invp")
            for r in range(4):
                win_high(act, 4, r)
            act.wait_ge(hsq_ok, CB)
            for cb in range(CB):
                act.activation(hyoT[:, cb, :], hyoT[:, cb, :], ACT.Copy, scale=chn[:, 1, cb:cb + 1]).then_inc(hg_ok, 1)
            have(act, "invp")
            act.dma_start(cv, a["cv"]).then_inc(in_ctx, 16)
            for ch, dst, scale in (("q", QT, DH ** -0.5), ("k", KTt, 1.0)):
                for cb in range(CB):
                    b = full(act, ch, cb)
                    drain(act.activation(dst[:, cb, 0:LAT], b[:, :], ACT.Copy, scale=scale), ch, cb)
                    if ch == "k" and cb < 3:
                        full(act, "hst")
                        win_high(act, 5, cb)
                b = full(act, ch + "p")
                if ch == "k":
                    win_high(act, 5, 3)
                drain(act.activation(dst[:, :, LAT:TOK], b[:, :].rearrange("p (a n) -> p a n", n=CTX), ACT.Copy,
                                     scale=scale), ch + "p")
            for t in range(NT):
                b = full(act, "V", t)
                drain(act.copy(V[:, t, :], b[:, :]), "V", t)
            b = full(act, "nk")
            drain(act.copy(nkb, b[:, :]), "nk")
            have(act, "nk")
            act.dma_start(outs["v"], V[:, CT, :]).then_inc(kv_out, 16)
            act.dma_start(outs["k"], nkb).then_inc(kv_out, 16)

            def exps(u):
                b, h = u // H, u % H
                n = P * (1 + len(key_tiles(b)))
                act.wait_ge(mx_ok, u + 1)
                if u >= 2:
                    full(act, "pt", u - 2)
                act.activation(pr[:, u % 2, 0:n], sc[:, u % 2, 0:n], ACT.Exp, bias=nmx[:, u % 4:u % 4 + 1],
                               accum_out=rsum[:, u % 4:u % 4 + 1]).then_inc(p_ok, 1)

            def probs_turned(u):
                nk = 1 + len(key_tiles(u // H))
                b = full(act, "pt", u)
                if u >= 2:
                    wait_pv(act, u - 2)
                drain(act.copy(PT[:, u % 2, 0:nk, :].rearrange("p a b -> p (a b)"), b[:, 0:nk * P]), "pt", u)

            def att_squares(b):
                have(act, "o", b)
                act.activation(osq, oraw[:, b % 2], ACT.Square).then_inc(osq_ok, 1)

            exps(0)
            for u in range(NT * H):
                if u + 1 < NT * H:
                    exps(u + 1)
                probs_turned(u)
                if u % H == 1 and u > H:
                    att_squares(u // H - 1)
            act.wait_ge(hrt, 1)
            act.activation(ss[:, 6, :], ss[:, 5, :], ACT.Sqrt, scale=1.0 / CH, bias=epsb[:, :]).then_inc(att_rt, 1)
            att_squares(NT - 1)
            have(act, "ast", NT - 1)
            act.activation(ss[:, 4, :], ss[:, 3, :], ACT.Sqrt, scale=1.0 / CH, bias=epsb[:, :]).then_inc(att_rt, 1)
            for b in range(NT + 2):
                if b > 1:
                    turned_h2(act, b - 2)
                if b < NT:
                    act.wait_ge(wt2_ok, 2 * b + 2)
                    link(act.activation(sqd, x[:, b, :], ACT.Square, scale=1.0 / 32.0, accum_out=ss[:, 0, b:b + 1]))
                    act.activation(ss[:, 1, b:b + 1], ss[:, 0, b:b + 1], ACT.Sqrt, bias=epsb[:, :]).then_inc(n_rt, 1)
            act.wait_ge(route_e, 1)
            act.activation(R[:, 1, :, 0:NG], R[:, 0, :, 0:NG], ACT.Exp).then_inc(route_a, 1)
            act.wait_ge(route_e, 2)
            act.activation(R[:, 9, :, 0:1], R[:, 8, :, 0:1], ACT.Exp).then_inc(route_a, 1)

            def high_parts(w, n, s, freed, count):
                act.wait_ge(ew_in[3 * s + w], (n - s) * 8 + 16)
                for r in range(4):
                    if freed is not None:
                        wait_past(act, freed, count + (r + 1))
                    act.copy(WH[:, high_half(w, s), r, :], quarter(s, w, r)).then_inc(high_ok[w], 1)

            def rows_high(n):
                for g in range(2):
                    act.wait_ge(xgT_full, n * 2 + (g + 1))
                    act.copy(xgTh[:, 4 * g:4 * g + 4, :].rearrange("p a b -> p (a b)"), bank[g][:, :]).then_inc(xh_ok, 1)

            def step(p, i, s, m=None):
                n = (i + p * pairs) * 2 + s
                if m == 0:
                    high_parts(1, n, s, None, 0)
                elif m == 1:
                    high_parts(1, n, s, used[0], (n - 1) * 4)
                elif m != NE:
                    high_parts(1, n, s, used[2], (n - 2) * 4)
                if m != NE:
                    act.wait_ge(used[0], n * 4 + 4)
                    wait_past(act, hid_ok, n)
                    act.activation(sil, bank[2][:, :], ACT.Silu).then_inc(sil_ok, 1)
                if m != 0:
                    act.wait_ge(hidT_full, n)
                    act.copy(hidTh[:, :, :].rearrange("p a b -> p (a b)"), bank[4][:, :]).then_inc(hh_ok, 1)
                    if m == NE:
                        high_parts(2, n - 1, 1 - s, used[1], (n - 1) * 4)
                    else:
                        high_parts(2, n - 1, 1 - s, used[0], n * 4)
                if m is None or m + 1 < NE:
                    rows_high(n + 1)
                    high_parts(0, n + 1, 1 - s, used[1], n * 4)
                if m != 0:
                    act.wait_ge(used[2], n * 4)
                    wait_past(act, y_out[1 - s], (n - 1 - (1 - s)) * 8)
                    act.copy(yout[:, 1 - s, 0:512], bank[5][:, :]).then_inc(y_cpA, 1)
                    act.wait_ge(y_cpA, n)
                    act.wait_ge(y_cpD, n)
                    act.dma_start(y_dram[bass.ds((n - 1) * P, P), :], yout[:, 1 - s, :]).then_inc(y_out[1 - s], 16)

            full(act, "rt", NT - 1)
            act.wait_ge(h2_out[0], 16 * 3)
            act.wait_ge(h2_out[1], 16 * 2)

            def one_pass(p):
                wait_past(act, used[2], p * (NE * 4))
                high_parts(0, p * NE, 0, None, 0)
                rows_high(p * NE)
                act.wait_ge(route_ok, 1)
                expert_steps(act, p, step)
                for s in range(2):
                    act.wait_ge(y_out[s], (p + 1) * (pairs * 16))
            one_pass(0)
            v = act.value_load(over[0:1, 0:1])
            with act.If(v > 0):
                with act.Fori(1, NT) as p:
                    one_pass(p)
            act.copy(ss[:, 7, :], ss[:, 6, :]).then_inc(stores_ok, 1)
            for t in range(NT + 1):
                if t < NT:
                    act.wait_ge(yab_in[t], 32)
                    act.activation(ya[:, t, :], ya[:, t, :], ACT.Copy, scale=wts[:, 0, t:t + 1]).then_inc(f_a, 1)
                if t > 0:
                    q = t - 1
                    act.wait_ge(f_cmb, t)
                    link(act.activation(sqd, x[:, q, :], ACT.Square, scale=1.0 / 32.0, accum_out=ss[:, 0, q:q + 1]))
                    act.activation(ss[:, 1, q:q + 1], ss[:, 0, q:q + 1], ACT.Sqrt, bias=epsb[:, :]).then_inc(f_rt, 1)

        @block.vector
        def _(dve):
            n_chain = [0]

            def link(ins):
                n_chain[0] += 1
                ins.then_inc(dve_chain, 1)
                dve.wait_ge(dve_chain, n_chain[0])

            dve.memset(epsb[:, :], EPS).then_inc(consts_ok, 1)
            dve.wait_ge(in_mlp, 80)
            def ada(j):
                r = 0 if j < NA_FIRST else 1
                dve.wait_ge(b_in[j % 2], 16 * (j // 2 + 1))
                if 2 <= j < NA_FIRST:
                    dve.wait_ge(mrow_used, j - 1)
                if j >= NA_FIRST + 2:
                    dve.wait_ge(m_out[j % 2], 16 * ((j - NA_FIRST) // 2))
                b = full(dve, "ada", j)
                m = mrow[r][:, j % 2, :]
                drain(dve.tensor_tensor(m, b[0:2, :], b_buf[r][:, j % 2, :], ALU.add), "ada", j)
                if j in (8, 9):
                    dve.wait_ge(g2row_in, 16 * (j - 7))
                    have(dve, "ada", j)
                    dve.scalar_tensor_tensor(out=m, in0=m, scalar=1.0, in1=g2row, op0=ALU.add, op1=ALU.mult)\
                       .then_inc(g2_done, 1)

            for layer in range(2):
                v, k = mtmp[0][0:FF, :], mtmp[1][0:FF, :]
                if layer:
                    dve.wait_ge(sin_ok, 1)
                for i, (lo, hi) in enumerate(((0, LAT), (LAT, TOK))):
                    b = full(dve, f"mlp{layer + 1}", i)
                    drain(dve.tensor_scalar(v[:, lo:hi], b[0:FF, 0:hi - lo], mlp_c[:, layer:layer + 1], mlp_c[:, 2:3],
                                            ALU.add, ALU.mult), f"mlp{layer + 1}", i)
                have(dve, f"mlp{layer + 1}", 1)
                link(dve.tensor_scalar(k, v, 1.0 / TWO_PI, ROUND, ALU.mult, ALU.add))
                link(dve.tensor_scalar(k, k, ROUND, None, ALU.subtract))
                for part in (PI_A, PI_B, PI_C):
                    link(dve.scalar_tensor_tensor(out=v, in0=k, scalar=-part, in1=v, op0=ALU.mult, op1=ALU.add))
                dve.tensor_scalar(v, v, 3.1415925, -3.1415925, ALU.min, ALU.max).then_inc(sin_arg, 1)
                ada(layer)
            dve.wait_ge(in_dec, 32)
            for t in range(NT):
                b = full(dve, "filt", t, 0)
                drain(dve.tensor_tensor(fbuf[:, 0, :], b[:, :], dec[:, t, :], ALU.mult), "filt", t, 0)
                b = full(dve, "filt", t, 1)
                drain(dve.scalar_tensor_tensor(out=fbuf[:, 1, :], in0=b[:, :], scalar=bmask[:, t:t + 1],
                                               in1=dec[:, t, :], op0=ALU.mult, op1=ALU.mult), "filt", t, 1)
                have(dve, "filt", t, 1)
                dve.tensor_tensor(s_flt[:, t, :], fbuf[:, 0, :], fbuf[:, 1, :], ALU.add).then_inc(filt_ok, 1)
                dve.tensor_tensor(d_flt[:, t, :], fbuf[:, 0, :], fbuf[:, 1, :], ALU.subtract).then_inc(filt_ok, 1)
                dve.wait_ge(filt_ok, 2 * t + 2)

            for j in range(2, NA_FIRST):
                ada(j)
            dve.wait_ge(in_cond, 64)
            b = full(dve, "mcol")
            mc = b[:, 0:4 * KT].rearrange("p (v k c) -> p v k c", v=2, c=2)
            link(dve.tensor_copy(mcol[:, 1], mc[:, 0]))
            drain(dve.scalar_tensor_tensor(out=mcol[:, 0], in0=mc[:, 1], scalar=1.0,
                                           in1=g1c[:, :].unsqueeze(2).broadcast_to([P, KT, 2]),
                                           op0=ALU.add, op1=ALU.mult), "mcol")
            have(dve, "mcol")
            dve.wait_ge(x_rt, 1)
            dve.reciprocal(ss[:, 2, :], ss[:, 1, :]).then_inc(x_rs, 1)
            have(dve, "kf", NT - 1, 1)

            for r in range(3):
                win_low(dve, 0, r)

            def input_low(k):
                dve.wait_ge(hTh_ok, k + 1)
                part = (slice(None), k, slice(0, LAT)) if k < KT else (slice(None), slice(None), slice(LAT, TOK))
                dve.tensor_tensor(hTl[part], hT[part], hTh[part].bitcast(F32), ALU.subtract).then_inc(hTl_ok, 1)

            for k in range(KT):
                b = full(dve, "xT", k)
                drain(dve.tensor_scalar(hT[:, k, 0:LAT], b[:, :], mcol[:, 0, k, 0:1], mcol[:, 1, k, 0:1],
                                        ALU.mult, ALU.add), "xT", k)
                if k > 1:
                    input_low(k - 2)
            for g in range(2):
                b = full(dve, "xTp", g)
                for j in range(4):
                    k = 4 * g + j
                    ins = dve.tensor_scalar(hT[:, k, LAT:TOK], b[:, j * P:(j + 1) * P], mcol[:, 0, k, 1:2],
                                            mcol[:, 1, k, 1:2], ALU.mult, ALU.add)
                drain(ins, "xTp", g)
            for k in range(KT - 2, KT + 1):
                input_low(k)
            win_low(dve, 0, 3)
            for lo, hi in ((0, 1), (LAT + 1, LAT + 2), (UW - 2, UW)):
                dve.memset(ustrip[:, :, lo:hi], 0.0).then_inc(strip_ok, 1)
            n = 0
            for c in range(3):
                if c < 2:
                    for r in range(4):
                        win_low(dve, c + 1, r)
                for cb in range(CB):
                    n += 1
                    dst = (z[:, cb], ctmp[:, cb % 2], x0[:, cb])[c][:, 0:UW - 3]
                    w = cwb[:, HYROW[c], cb, :]
                    dve.wait_ge(tap_ok, n)
                    link(dve.scalar_tensor_tensor(out=dst, in0=ustrip[:, cb, 0:UW - 3], scalar=w[:, 0:1], in1=dst,
                                                  op0=ALU.mult, op1=ALU.add))
                    dve.scalar_tensor_tensor(out=dst, in0=ustrip[:, cb, 2:UW - 1], scalar=w[:, 2:3], in1=dst,
                                             op0=ALU.mult, op1=ALU.add).then_inc(conv_ok, 1)
                    dve.wait_ge(conv_ok, n)
                    if c == 1:
                        dve.tensor_tensor(z[:, cb, 0:UW - 3], z[:, cb, 0:UW - 3], dst, ALU.mult).then_inc(z_ok, 1)
            for kt in range(NT):
                re, im = full(dve, "uf", kt, 0), None
                yr, yi = YR[:, kt, :], YI[:, kt, :]
                if kt == 0:
                    have(dve, "kf", NT - 1, 1)
                link(dve.tensor_tensor(yr, re[:, :], KR[:, kt, :], ALU.mult))
                drain(dve.tensor_tensor(yi, re[:, :], KI[:, kt, :], ALU.mult), "uf", kt, 0)
                im = full(dve, "uf", kt, 1)
                link(dve.tensor_tensor(ytmp[:, 0, :], im[:, :], KI[:, kt, :], ALU.mult))
                drain(dve.tensor_tensor(ytmp[:, 1, :], im[:, :], KR[:, kt, :], ALU.mult), "uf", kt, 1)
                have(dve, "uf", kt, 1)
                link(dve.tensor_tensor(yr, yr, ytmp[:, 0, :], ALU.subtract))
                dve.tensor_tensor(yi, yi, ytmp[:, 1, :], ALU.add).then_inc(y_ok, 1)
                dve.wait_ge(y_ok, kt + 1)
            for j in range(NA_FIRST, N_ADA):
                ada(j)
            for r in range(4):
                win_low(dve, 3, r)
            for q in m_out:
                dve.wait_ge(q, 8 * (N_ADA - NA_FIRST))
            perm = "p (b r c) -> p r b c"
            for cb in range(CB):
                b = full(dve, "inv", cb)
                drain(dve.scalar_tensor_tensor(out=t1[:, cb % 2, 0:LAT], in0=z[:, cb, 0:LAT], scalar=chn[:, 0, cb:cb + 1],
                                               in1=b[:, :], op0=ALU.mult, op1=ALU.add), "inv", cb)
                have(dve, "inv", cb)
                nat = "p (r b c) -> p r b c"
                link(dve.tensor_tensor(hyoT[:, cb, 0:LAT].rearrange(perm, r=ROWS, c=NA_COLS),
                                       t1[:, cb % 2, 0:LAT].rearrange(nat, r=ROWS, c=NA_COLS),
                                       x0[:, cb, 0:LAT].rearrange(nat, r=ROWS, c=NA_COLS), ALU.mult))
            b = full(dve, "invp")
            for cb in range(CB):
                ins = dve.scalar_tensor_tensor(out=t1[:, cb % 2, cb // 2 * P:cb // 2 * P + P], in0=z[:, cb, LAT + 1:LAT + 1 + CTX],
                                               scalar=chn[:, 0, cb:cb + 1], in1=b[:, cb * P:(cb + 1) * P],
                                               op0=ALU.mult, op1=ALU.add)
            drain(ins, "invp")
            have(dve, "invp")
            for cb in range(CB):
                dve.tensor_tensor(hyoT[:, cb, LAT:TOK], t1[:, cb % 2, cb // 2 * P:cb // 2 * P + P],
                                  x0[:, cb, LAT + 1:LAT + 1 + CTX], ALU.mult).then_inc(hyo_ok, 1)
            dve.wait_ge(hsq_ok, CB)
            link(dve.tensor_tensor(sq[:, 0:2, :], sq[:, 0:2, :], sq[:, 2:4, :], ALU.add))
            dve.tensor_tensor(sq[:, 0, :], sq[:, 0, :], sq[:, 1, :], ALU.add).then_inc(hsum_ok, 1)
            for r in range(4):
                win_low(dve, 4, r)
            b = full(dve, "hst")
            drain(dve.tensor_copy(ss[:, 5, :], b[:, 0:NT]), "hst")
            have(dve, "hst")
            dve.tensor_copy(rsh[:, 1, :], ss[:, 5, :]).then_inc(hrt, 1)
            for r in range(4):
                win_low(dve, 5, r)

            def scores(u):
                b = full(dve, "s", u)
                n = P * (1 + len(key_tiles(u // H)))
                if u >= 2:
                    dve.wait_ge(p_ok, u - 1)
                if u < CT * H:
                    dve.wait_ge(tm_ok, u + 1)
                else:
                    dve.wait_ge(tm_ok, CT * H)
                drain(dve.tensor_tensor_reduce(sc[:, u % 2, 0:n], b[:, 0:n], Tm[:, u % 3, 0:n], 1.0, -3.0e38,
                                               ALU.add, ALU.max, rmx[:, u % 4:u % 4 + 1]), "s", u)
                have(dve, "s", u)
                dve.tensor_scalar(nmx[:, u % 4:u % 4 + 1], rmx[:, u % 4:u % 4 + 1], -1.0, None, ALU.mult)\
                   .then_inc(mx_ok, 1)

            def normed(u):
                n = P * (1 + len(key_tiles(u // H)))
                c = slice(u % 4, u % 4 + 1)
                dve.wait_ge(p_ok, u + 1)
                link(dve.reciprocal(rinv[:, c], rsum[:, c]))
                dve.tensor_scalar(pr[:, u % 2, 0:n], pr[:, u % 2, 0:n], rinv[:, c], None, ALU.mult).then_inc(pn_ok, 1)

            def out_tile(b):
                bk = full(dve, "o", b)
                if b >= 2:
                    dve.wait_ge(osq_ok, b - 1)
                r = oraw[:, b % 2]
                drain(dve.tensor_copy(r.rearrange("p a n -> p (a n)"), bk[:, :]), "o", b)
                if b == 0:
                    dve.wait_ge(kv_out, 32)
                have(dve, "o", b)
                dve.tensor_tensor(attT[:, :, b * P:(b + 1) * P], r, chn[:, 2, :].unsqueeze(2).broadcast_to([P, CB, P]),
                                  ALU.mult).then_inc(att_ok, 1)

            def out_sums(b):
                dve.wait_ge(osq_ok, b + 1)
                if b >= 2:
                    full(dve, "ast", b - 2)
                link(dve.tensor_tensor(osq[:, 0:2, :], osq[:, 0:2, :], osq[:, 2:4, :], ALU.add))
                dve.tensor_tensor(osum[:, b % 2, :], osq[:, 0, :], osq[:, 1, :], ALU.add).then_inc(osum_ok, 1)

            def stat(b):
                bk = full(dve, "ast", b)
                drain(dve.tensor_copy(ss[:, 3, b:b + 1], bk[:, b:b + 1]), "ast", b)

            for u in range(-2, NT * H + 1):
                if u + 2 < NT * H:
                    scores(u + 2)
                if u >= -1 and u + 1 < NT * H:
                    normed(u + 1)
                if u >= 1 and (u - 1) % H == H - 1:
                    out_tile((u - 1) // H)
                if u - 1 >= H and (u - 1) % H == 2:
                    out_sums((u - 1) // H - 1)
                if u - 1 >= H and (u - 1) % H == 3:
                    stat((u - 1) // H - 1)
            out_sums(NT - 1)
            stat(NT - 1)
            dve.wait_ge(att_rt, 1)
            link(dve.reciprocal(rsh[:, 1, :], ss[:, 6, :]))
            dve.wait_ge(att_rt, 2)
            link(dve.reciprocal(rsh[:, 0, :], ss[:, 4, :]))

            def modulated(b):
                c = b // CT
                dve.wait_ge(n_rt, b + 1)
                link(dve.reciprocal(ss[:, 2, b:b + 1], ss[:, 1, b:b + 1]))
                if b >= 2:
                    full(dve, "h2T", b - 2, 1)
                    dve.wait_ge(h2_out[b % 2], 16 * (b // 2))
                link(dve.scalar_tensor_tensor(out=h2[:, b % 2, :], in0=x[:, b, :], scalar=ss[:, 2, b:b + 1],
                                              in1=G2[:, c, :], op0=ALU.mult, op1=ALU.mult))
                dve.tensor_tensor(h2[:, b % 2, :], h2[:, b % 2, :], SH2[c], ALU.add).then_inc(h2_ok, 1)

            def logits(b):
                bk = full(dve, "rt", b)
                drain(dve.tensor_tensor(lg[:, b, :], bk[:, 0:NG + NE], rb[:, :], ALU.add), "rt", b)

            dve.wait_ge(in_small, 80)
            dve.wait_ge(g2_in, 32)
            dve.wait_ge(sh2_in, 32)
            for b in range(NT):
                for n in range(2):
                    i = 2 * b + n
                    w = wtmp[:, i % 2, 0, :]
                    bk = full(dve, "wa", b, n)
                    if i >= 2:
                        dve.wait_ge(wt2_ok, i - 1)
                    drain(dve.tensor_scalar(w, bk[:, :], rsh[:, 0, b:b + 1], None, ALU.mult), "wa", b, n)
                    have(dve, "wa", b, n)
                    bk = full(dve, "wh", b, n)
                    drain(dve.scalar_tensor_tensor(out=w, in0=bk[:, :], scalar=rsh[:, 1, b:b + 1], in1=w,
                                                   op0=ALU.mult, op1=ALU.add), "wh", b, n)
                    if n == 0 and b > 1:
                        logits(b - 2)
                    if n == 0 and b > 0:
                        modulated(b - 1)
            modulated(NT - 1)
            logits(NT - 2)
            logits(NT - 1)
            have(dve, "rt", NT - 1)

            def r4(i):
                return R[:, i, :, 0:NG]

            def r1(i):
                return R[:, i, :, 0:1]

            def over4(v):
                return v.broadcast_to([P, NT, NG])

            def first_max(val, mx, out, tmp, low):
                link(dve.tensor_reduce(mx, val, AX, ALU.max))
                link(dve.tensor_tensor(out, val, over4(mx), ALU.is_equal))
                link(dve.scalar_tensor_tensor(out=tmp, in0=out, scalar=-float(NG),
                                              in1=iota[:, 0:NG].unsqueeze(1).broadcast_to([P, NT, NG]),
                                              op0=ALU.mult, op1=ALU.add))
                link(dve.tensor_reduce(low, tmp, AX, ALU.min))
                link(dve.tensor_tensor(out, tmp, over4(low), ALU.is_equal))

            gl = lg[:, :, 0:NG]
            first_max(gl, r1(2), r4(3), r4(4), r1(5))
            dve.tensor_tensor(r4(0), gl, over4(r1(2)), ALU.subtract).then_inc(route_e, 1)
            el = lg[:, :, NG:].rearrange("p t (g j) -> p t g j", j=EPG)
            prod = R[:, 10].rearrange("p t (g j) -> p t g j", j=EPG)
            link(dve.tensor_tensor(prod, el, r4(3).unsqueeze(3).broadcast_to([P, NT, NG, EPG]), ALU.mult))
            link(dve.tensor_reduce(r4(6), prod.rearrange("p t g j -> p t j g"), AX, ALU.add))
            first_max(r4(6), r1(2), r4(7), r4(4), r1(5))
            link(dve.scalar_tensor_tensor(out=r4(6), in0=r4(7), scalar=-1.0e30, in1=r4(6), op0=ALU.mult, op1=ALU.add))
            first_max(r4(6), r1(12), r4(11), r4(4), r1(5))
            dve.tensor_tensor(r1(8), r1(12), r1(2), ALU.subtract).then_inc(route_e, 1)
            A1, A2, A = R[:, 13], R[:, 14], R[:, 15]
            for dst, j1 in ((A1, 7), (A2, 11)):
                link(dve.tensor_tensor(dst.rearrange("p t (g j) -> p t g j", j=EPG),
                                       r4(3).unsqueeze(3).broadcast_to([P, NT, NG, EPG]),
                                       r4(j1).unsqueeze(2).broadcast_to([P, NT, NG, EPG]), ALU.mult))
            dve.tensor_tensor(A, A1, A2, ALU.add).then_inc(assigned, 1)
            bk = full(dve, "rank")
            rk = R[:, 10]
            drain(dve.tensor_copy(rk, bk[:, 0:NT * NE].rearrange("p (t e) -> p t e", e=NE)), "rank")
            have(dve, "rank")
            link(dve.scalar_tensor_tensor(out=rankm[:, :, :], in0=rk, scalar=1.0, in1=A, op0=ALU.add, op1=ALU.mult))
            link(dve.tensor_scalar(rankm[:, :, :], rankm[:, :, :], -1.0, None, ALU.add))
            def slots_of(n, e, s):
                wait_past(dve, idx_full, n - 1)
                dve.tensor_tensor(sel[:, s], iota[:, :].unsqueeze(1).broadcast_to([P, NT, P]),
                                  rankm[:, :, bass.ds(e, 1)].broadcast_to([P, NT, P]), ALU.is_equal).then_inc(sel_ok, 1)

            def numbers(n, s):
                dve.wait_ge(idx_full, n + 1)
                wait_past(dve, xg_in[s], (n - s) * 8)
                dve.tensor_copy(idx[:, s:s + 1], bank[7][:, 0:1]).then_inc(idx_ok, 1)

            def rows_low(n):
                for g in range(2):
                    dve.wait_ge(xh_ok, n * 2 + (g + 1))
                    part = slice(4 * g, 4 * g + 4)
                    dve.tensor_tensor(xgTl[:, part, :].rearrange("p a b -> p (a b)"), bank[g][:, :],
                                      xgTh[:, part, :].rearrange("p a b -> p (a b)").bitcast(F32), ALU.subtract)\
                       .then_inc(xl_ok, 1)

            def low_parts(w, n, s):
                for r in range(4):
                    dve.wait_ge(high_ok[w], n * 4 + (r + 1))
                    dve.tensor_tensor(WL[3 * s + w][:, r, :], quarter(s, w, r),
                                      WH[:, high_half(w, s), r, :].bitcast(F32), ALU.subtract).then_inc(low_ok[w], 1)

            def step(p, i, s, m=None):
                n = (i + p * pairs) * 2 + s
                more = m is None or m + 2 < NE
                if more:
                    slots_of(n + 2, i * 2 + (s + 2), s)
                if m != NE:
                    low_parts(1, n, s)
                if m != 0:
                    dve.wait_ge(hh_ok, n)
                    dve.tensor_tensor(hidTl[:, :, :].rearrange("p a b -> p (a b)"), bank[4][:, :],
                                      hidTh[:, :, :].rearrange("p a b -> p (a b)").bitcast(F32), ALU.subtract)\
                       .then_inc(hl_ok, 1)
                    low_parts(2, n - 1, 1 - s)
                if m != NE:
                    dve.wait_ge(used[1], n * 4 + 4)
                    dve.wait_ge(sil_ok, n + 1)
                    wait_past(dve, hidT_full, n)
                    dve.tensor_tensor(hid, sil, bank[3][:, :], ALU.mult).then_inc(hid_ok, 1)
                if more:
                    numbers(n + 2, s)
                if m is None or m + 1 < NE:
                    rows_low(n + 1)
                    low_parts(0, n + 1, 1 - s)
                if m != 0:
                    dve.wait_ge(used[2], n * 4)
                    wait_past(dve, y_out[1 - s], (n - 1 - (1 - s)) * 8)
                    dve.tensor_copy(yout[:, 1 - s, 512:1024], bank[6][:, :]).then_inc(y_cpD, 1)

            def rest_of_routing():
                dve.wait_ge(route_a, 2)
                link(dve.tensor_reduce(r1(5), r4(1), AX, ALU.add))
                link(dve.reciprocal(r1(5), r1(5)))
                link(dve.tensor_scalar(r1(2), r1(9), 1.0, None, ALU.add))
                link(dve.reciprocal(r1(2), r1(2)))
                w1 = wts[:, 0, :].unsqueeze(2)
                link(dve.tensor_tensor(w1, r1(2), r1(5), ALU.mult))
                link(dve.tensor_tensor(wts[:, 1, :].unsqueeze(2), w1, r1(9), ALU.mult))
                row, more = R[:, 9], R[:, 11]
                link(dve.scalar_tensor_tensor(out=row, in0=iota[:, 0:NE].unsqueeze(1).broadcast_to([P, NT, NE]),
                                              scalar=float(P), in1=rk, op0=ALU.mult, op1=ALU.add))
                for p in range(1, NT):
                    link(dve.tensor_scalar(more, rk, float(p * CAP), float(NE * P - CAP), ALU.is_ge, ALU.mult))
                    link(dve.tensor_tensor(row, row, more, ALU.add))
                for k, Ak in enumerate((A1, A2)):
                    link(dve.tensor_tensor(Ak, Ak, row, ALU.mult))
                    link(dve.tensor_reduce(posf[:, k, :].unsqueeze(2), Ak, AX, ALU.add))
                link(dve.tensor_copy(posi[:, :, :], posf[:, :, :]))
                bk = full(dve, "total")
                drain(dve.tensor_reduce(R[:, 12, 0, 0:1], bk[:, 0:NE], AX, ALU.max), "total")
                have(dve, "total")
                dve.wait_ge(consts_ok, 2)
                dve.tensor_scalar(over[0:1, 0:1], R[0:1, 12, 0, 0:1], float(CAP), None, ALU.is_gt).then_inc(route_ok, 1)

            def one_pass(p, then=None):
                for s in range(2):
                    slots_of(p * NE + s, s, s)
                for s in range(2):
                    numbers(p * NE + s, s)
                if then is not None:
                    then()
                low_parts(0, p * NE, 0)
                rows_low(p * NE)
                expert_steps(dve, p, step)
            one_pass(0, rest_of_routing)
            v = dve.value_load(over[0:1, 0:1])
            with dve.If(v > 0):
                with dve.Fori(1, NT) as p:
                    dve.tensor_scalar(rankm[:, :, :], rankm[:, :, :], -float(CAP), None, ALU.add).then_inc(shifted, 1)
                    dve.wait_ge(shifted, p)
                    one_pass(p)
            dve.wait_ge(tail_in, 48)
            for t in range(NT + 2):
                if t < NT:
                    dve.wait_ge(f_a, t + 1)
                    dve.scalar_tensor_tensor(out=yb[:, t, :], in0=yb[:, t, :], scalar=wts[:, 1, t:t + 1], in1=ya[:, t, :],
                                             op0=ALU.mult, op1=ALU.add).then_inc(f_b, 1)
                if 0 < t <= NT:
                    dve.wait_ge(f_c, t)
                    dve.tensor_tensor(x[:, t - 1, :], x[:, t - 1, :], yb[:, t - 1, :], ALU.add).then_inc(f_cmb, 1)
                if t > 1:
                    q = t - 2
                    dve.wait_ge(f_rt, q + 1)
                    link(dve.reciprocal(ss[:, 2, q:q + 1], ss[:, 1, q:q + 1]))
                    dve.scalar_tensor_tensor(out=x[:, q, :], in0=x[:, q, :], scalar=ss[:, 2, q:q + 1], in1=fg,
                                             op0=ALU.mult, op1=ALU.mult).then_inc(f_ok, 1)

        @block.tensor
        def _(pe):
            def open_bank(*name):
                j = JOB[name]
                prev = [q for q in range(j) if JOBS[q][1] == JOBS[j][1]]
                if prev:
                    have(pe, *JOBS[prev[-1]][0])
                return bank[JOBS[j][1]]

            def close(ins):
                ins.then_inc(pe_full, 1)

            def group(out, terms, start=True):
                for i, (l, r) in enumerate(terms):
                    ins = pe.matmul(out, l, r, start=(i == 0), stop=(i == len(terms) - 1))
                return ins

            def chunk(c, again=0):
                i = FIRST_USE[c][again]
                pe.wait_ge(chunk_in[i % NRING], 16 * (i // NRING + 1))
                return slot[i % NRING]

            def turn(out, src):
                return pe.transpose(out, src, ident[:, :])

            pe.wait_ge(consts_ok, 2)

            def ada(j):
                W = chunk(("ada", j)).rearrange("p (k n) -> p k n", n=512)
                b = open_bank("ada", j)
                close(group(b[0:2, :], [(scond[:, k, :], W[:, k, :]) for k in range(KT)]))

            def col(j):
                if j == 0:
                    open_bank("mcol")
                have(pe, "ada", j)
                b = bank[JOBS[JOB[("mcol",)]][1]]
                for q in range(4):
                    o = (4 * j + q) * 2
                    ins = pe.matmul(b[:, o:o + 2], mrow[0][:, j % 2, q * P:(q + 1) * P], ident[0:2, 0:2],
                                    start=True, stop=True)
                if j < NA_FIRST - 1:
                    ins.then_inc(mrow_used, 1)
                else:
                    close(ins)

            pe.wait_ge(in_mlp, 80)
            for layer in range(2):
                src, k = (zf, EMB) if layer == 0 else (mh[0], FF)
                if layer:
                    pe.wait_ge(sin_ok, 1)
                for i, (lo, hi) in enumerate(((0, LAT), (LAT, TOK))):
                    b = open_bank(f"mlp{layer + 1}", i)
                    close(pe.matmul(b[0:FF, 0:hi - lo], w12[0:k, layer, :], src[0:k, lo:hi], start=True, stop=True))
                if layer == 0:
                    pe.wait_ge(in_ctx, 16)
                    b = open_bank("ckT")
                    for cb in range(CB):
                        ins = turn(b[:, cb * P:(cb + 1) * P], craw[:, cb * P:(cb + 1) * P])
                    close(ins)
                    pe.wait_ge(cond_ok, 1)
                ada(layer)
            pe.wait_ge(sin_ok, 2)
            for t in range(NT):
                for d in range(2):
                    b = open_bank("filt", t, d)
                    close(pe.matmul(b[:, :], mh[1][0:FF, t * P:(t + 1) * P], mw3[0:FF, d * CH:(d + 1) * CH],
                                    start=True, stop=True))
            for j in range(2):
                col(j)
            for j in range(2, NA_FIRST):
                ada(j)
                col(j)
            pe.wait_ge(filt_ok, 2 * NT)
            F = chunk(("dft",)).rearrange("p (a t k) -> p a t k", a=2, k=LAT)
            pe.wait_ge(in_dft, 16)
            for kt in range(NT):
                for ri, src in enumerate((s_flt, d_flt)):
                    b = open_bank("kf", kt, ri)
                    if kt < CT:
                        close(group(b[:, :], [(F[:, ri, t, kt * P:(kt + 1) * P], src[:, t, :]) for t in range(CT)]))
                    else:
                        close(pe.matmul(b[:, :], dftp[:, ri, :], src[:, CT, :], start=True, stop=True))
            pe.wait_ge(xn_ok, NT)
            for k in range(KT):
                b = open_bank("xT", k)
                for t in range(CT):
                    ins = turn(b[:, t * P:(t + 1) * P], xn[:, t, k * P:(k + 1) * P])
                close(ins)
            for g in range(2):
                b = open_bank("xTp", g)
                for j in range(4):
                    k = 4 * g + j
                    ins = turn(b[:, j * P:(j + 1) * P], xn[:, CT, k * P:(k + 1) * P])
                close(ins)

            def products(out, l, r, first, last):
                for i, (u, v) in enumerate(((0, 0), (0, 1), (1, 0))):
                    ins = pe.matmul(out, l[u], r[v], start=first and i == 0, stop=last and i == 2)
                return ins

            def split_group(out, terms, c=None):
                for k, (l, r) in enumerate(terms):
                    if c is not None and k % 2 == 0:
                        pe.wait_ge(wp_low, 4 * c + k // 2 + 1)
                    if c == 0:
                        pe.wait_ge(hTl_ok, k + 1)
                    ins = products(out, l, r, k == 0, k == len(terms) - 1)
                return ins

            def win_parts(c, k, lo, hi):
                cols = slice(k % 2 * 512 + lo, k % 2 * 512 + hi)
                return WP[c][k // 2][:, cols], WL[PROJ[c][1] % NRING][:, k // 2, cols]

            def input_parts(k, lo, hi):
                return hTh[:, k, lo:hi], hTl[:, k, lo:hi]

            def project(job, jobp, c):
                for cb in range(CB):
                    b = open_bank(*job, cb)
                    close(split_group(b[:, :], [(win_parts(c, k, cb * P, (cb + 1) * P), input_parts(k, 0, LAT))
                                                for k in range(KT)], c if cb == 0 else None))
                b = open_bank(*jobp)
                pe.wait_ge(hTl_ok, KT + 1)
                for cb in range(CB):
                    ins = split_group(b[:, cb * P:(cb + 1) * P],
                                      [(win_parts(c, k, cb * P, (cb + 1) * P), input_parts(k, LAT, TOK))
                                       for k in range(KT)])
                close(ins)

            for c in range(3):
                project(("hy", c), ("hyp", c), c)
            pe.wait_ge(z_ok, CB)
            for t in range(NT):
                b = open_bank("zT", t)
                lo = t * P if t < CT else LAT + 1
                for cb in range(CB):
                    ins = turn(b[:, cb * P:(cb + 1) * P], z[:, cb, lo:lo + P])
                close(ins)
            have(pe, "zT", NT - 1)
            F = chunk(("dft",), 1).rearrange("p (a t k) -> p a t k", a=2, k=LAT)
            for kt in range(NT):
                for ri in range(2):
                    b = open_bank("uf", kt, ri)
                    if kt < CT:
                        close(group(b[:, :], [(F[:, ri, t, kt * P:(kt + 1) * P], zt[:, t, :]) for t in range(CT)]))
                    else:
                        close(pe.matmul(b[:, :], dftp[:, ri, :], zt[:, CT, :], start=True, stop=True))
            for j in range(NA_FIRST, N_ADA):
                ada(j)
            pe.wait_ge(y_ok, NT)
            F = chunk(("idft",)).rearrange("p (a t k) -> p a t k", a=2, k=LAT)
            for cb in range(CB):
                b = open_bank("inv", cb)
                close(group(b[:, :], [(Y[:, kt, cb * P:(cb + 1) * P], F[:, ri, kt, :])
                                      for ri, Y in enumerate((YR, YI)) for kt in range(CT)]))
            b = open_bank("invp")
            for cb in range(CB):
                ins = group(b[:, cb * P:(cb + 1) * P], [(Y[:, CT, cb * P:(cb + 1) * P], dftp[:, 2 + ri, :])
                                                        for ri, Y in enumerate((YR, YI))])
            close(ins)
            project(("q",), ("qp",), 3)
            b = open_bank("hst")
            pe.wait_ge(hsum_ok, 1)
            for t in range(NT):
                ins = pe.matmul(b[:, t:t + 1], sq[:, 0, t * P:(t + 1) * P], ones[:, 0:1], start=True, stop=True)
            close(ins)
            project(("k",), ("kp",), 4)
            for t in range(NT):
                b = open_bank("V", t)
                close(split_group(b[:, :], [(input_parts(k, t * P, (t + 1) * P), win_parts(5, k, 0, 512))
                                            for k in range(KT)], 5 if t == 0 else None))
            have(pe, "kp")
            b = open_bank("nk")
            for cb in range(CB):
                ins = turn(b[:, cb * P:(cb + 1) * P], KTt[:, cb, LAT:TOK])
            close(ins)
            have(pe, "V", NT - 1)
            pe.wait_ge(in_ctx, 32)

            def scores(u):
                b, h = u // H, u % H
                hp, pair = h % 2 * DH, h // 2
                bk = open_bank("s", u)
                q = QT[hp:hp + DH, pair, b * P:(b + 1) * P]
                kc = ckT[hp:hp + DH, pair, :] if b < CT else KTt[hp:hp + DH, pair, LAT:TOK]
                ins = pe.matmul(bk[:, 0:P], q, kc, start=True, stop=True)
                kts = key_tiles(b)
                if kts:
                    ins = pe.matmul(bk[:, P:P * (1 + len(kts))], q,
                                    KTt[hp:hp + DH, pair, kts[0] * P:(kts[-1] + 1) * P], start=True, stop=True)
                close(ins)

            def turn_probs(u):
                bk = open_bank("pt", u)
                pe.wait_ge(pn_ok, u + 1)
                for j in range(1 + len(key_tiles(u // H))):
                    ins = turn(bk[:, j * P:(j + 1) * P], pr[:, u % 2, j * P:(j + 1) * P])
                close(ins)

            def values(u):
                b, h = u // H, u % H
                cols = slice(h * DH, (h + 1) * DH)
                hp, pair = h % 2 * DH, h // 2
                if h == 0:
                    open_bank("o", b)
                have(pe, "pt", u)
                vs = [cv[:, cols]] if b < CT else [V[:, CT, cols]]
                vs += [V[:, t, cols] for t in key_tiles(b)]
                ins = group(bank[6][hp:hp + DH, pair * P:(pair + 1) * P], [(v, PT[:, u % 2, j, :]) for j, v in enumerate(vs)])
                if h == H - 1:
                    close(ins)
                else:
                    ins.then_inc(pv_ok, 1)

            def att_stat(b):
                bk = open_bank("ast", b)
                pe.wait_ge(osum_ok, b + 1)
                close(pe.matmul(bk[:, b:b + 1], osum[:, b % 2, :], ones[:, 0:1], start=True, stop=True))

            for u in range(-2, NT * H + 1):
                if u + 2 < NT * H:
                    scores(u + 2)
                if 0 <= u < NT * H:
                    turn_probs(u)
                if u >= 1:
                    values(u - 1)
                if u - 1 >= H and (u - 1) % H == 3:
                    att_stat((u - 1) // H - 1)
            att_stat(NT - 1)
            Ws = [chunk(("wout", n)).rearrange("p (k n) -> p k n", n=512) for n in range(2)]
            pe.wait_ge(hg_ok, CB)
            pe.wait_ge(att_ok, NT)

            def route(b):
                pe.wait_ge(h2_ok, b + 1)
                for g in range(2):
                    bk = open_bank("h2T", b, g)
                    for j in range(4):
                        ins = turn(bk[:, j * P:(j + 1) * P], h2[:, b % 2, (4 * g + j) * P:(4 * g + j + 1) * P])
                    close(ins)
                have(pe, "h2T", b, 1)
                bk = open_bank("rt", b)
                close(group(bk[:, 0:NG + NE], [(h2T[:, b % 2, k, :], rw[:, k, :]) for k in range(KT)]))

            pe.wait_ge(in_small, 80)
            for b in range(NT):
                for n in range(2):
                    for job, src, k0 in (("wa", attT, 0), ("wh", hyoT, CB)):
                        bk = open_bank(job, b, n)
                        close(group(bk[:, :], [(src[:, cb, b * P:(b + 1) * P], Ws[n][:, k0 + cb, :])
                                               for cb in range(CB)]))
                    if n == 0 and b > 1:
                        route(b - 2)
            route(NT - 2)
            route(NT - 1)
            A = R[:, 15]
            pe.wait_ge(assigned, 1)
            bk = open_bank("rank")
            pe.matmul(bk[:, 0:NT * NE], tri[:, :], A, start=True, stop=False)
            for q in range(NT - 1):
                ins = pe.matmul(bk[:, (q + 1) * NE:NT * NE], ones[:, :],
                                A[:, q, :].unsqueeze(1).broadcast_to([P, NT - 1 - q, NE]), start=False, stop=q == NT - 2)
            close(ins)
            bk = open_bank("total")
            close(group(bk[:, 0:NE], [(ones[:, :], A[:, t, :]) for t in range(NT)]))
            have(pe, "rank")

            def numbers(n, s):
                pe.wait_ge(sel_ok, n + 1)
                wait_past(pe, idx_ok, n)
                group(bank[7][:, 0:1], [(sel[:, s, t, :], tid[:, t:t + 1]) for t in range(NT)]).then_inc(idx_full, 1)

            def turn_rows(n, s):
                pe.wait_ge(xg_in[s], (n - s) * 8 + 16)
                wait_past(pe, xl_ok, n * 2)
                for g in range(2):
                    for j in range(4):
                        ins = turn(bank[g][:, j * P:(j + 1) * P], xg[:, s, (4 * g + j) * P:(4 * g + j + 1) * P])
                    ins.then_inc(xgT_full, 1)

            def step(p, i, s, m=None):
                n = (i + p * pairs) * 2 + s
                if m != NE:
                    pe.wait_ge(xl_ok, n * 2 + 2)
                for w, freed in ((0, sil_ok), (1, hid_ok)):
                    if m == NE:
                        break
                    wait_past(pe, freed, n)
                    for r in range(4):
                        pe.wait_ge(low_ok[w], n * 4 + (r + 1))
                        for k in range(2):
                            cols = slice(k * FE, (k + 1) * FE)
                            ins = products(bank[2 + w][:, :], (xgTh[:, 2 * r + k, :], xgTl[:, 2 * r + k, :]),
                                           (WH[:, high_half(w, s), r, cols], WL[3 * s + w][:, r, cols]),
                                           r == 0 and k == 0, r == 3 and k == 1)
                        ins.then_inc(used[w], 1)
                    if w == 0 and m != 0:
                        turn_hidden(n)
                if m == NE:
                    turn_hidden(n)
                if m is None or m + 2 < NE:
                    numbers(n + 2, s)
                if m is None or m + 1 < NE:
                    turn_rows(n + 1, 1 - s)
                if m != 0:
                    pe.wait_ge(hl_ok, n)
                    wait_past(pe, y_cpA, n - 1)
                    wait_past(pe, y_cpD, n - 1)
                    for f in range(FE // P):
                        pe.wait_ge(low_ok[2], (n - 1) * 4 + (f + 1))
                        for half in range(2):
                            cols = slice(half * 512, (half + 1) * 512)
                            ins = products(bank[5 + half][:, :], (hidTh[:, f, :], hidTl[:, f, :]),
                                           (WH[:, high_half(2, 1 - s), f, cols], WL[3 * (1 - s) + 2][:, f, cols]),
                                           f == 0, f == 3)
                        ins.then_inc(used[2], 1)

            def turn_hidden(n):
                pe.wait_ge(hid_ok, n)
                wait_past(pe, hl_ok, n - 1)
                for f in range(FE // P):
                    ins = turn(bank[4][:, f * P:(f + 1) * P], hid[:, f * P:(f + 1) * P])
                ins.then_inc(hidT_full, 1)

            def one_pass(p):
                for s in range(2):
                    numbers(p * NE + s, s)
                turn_rows(p * NE, 0)
                have(pe, "total")
                expert_steps(pe, p, step)
            one_pass(0)
            pe.wait_ge(route_ok, 1)
            v = pe.value_load(over[0:1, 0:1])
            with pe.If(v > 0):
                with pe.Fori(1, NT) as p:
                    one_pass(p)


def constants():
    f = np.float32
    feats, decs = [], []
    lo, hi = math.log(1e-2) / 1.5, math.log(1e-2) / 0.3
    deltas = np.abs(np.linspace(lo, hi, CH))
    fb = np.linspace(1e-4, 15, 16)[:, None]
    for L in (LAT, CTX):
        t = np.linspace(0.0, 1.0, L)[None, :]
        w = 2.0 * np.pi * np.arange(L)[None, :] / L
        feats.append(np.concatenate([t, np.cos(fb * w), -np.sin(fb * w)], axis=0))
        decs.append(np.exp(-t.T * deltas[None, :]))
    bmask = np.ones((P, NT))
    bmask[0, 0] = bmask[0, CT] = 0.0

    def transforms(L):
        n, k = np.arange(L)[:, None], np.arange(L)[None, :]
        th = np.pi * ((2 * k + 1) * n % (4 * L)) / (2 * L) * 1.0
        th = 2 * np.pi * ((2 * k + 1) * n % (4 * L)) / (4 * L)
        return np.cos(th), -np.sin(th)

    def tiles(m):
        return m.reshape(-1, P, m.shape[1]).transpose(1, 0, 2)
    c, s = transforms(LAT)
    dft = np.stack([np.stack([tiles(c), tiles(s)], 1).reshape(P, -1),
                    np.stack([tiles(c.T / LAT), tiles(s.T / LAT)], 1).reshape(P, -1)])
    c, s = transforms(CTX)
    dftp = np.stack([c, s, c.T / CTX, s.T / CTX], 1)
    maskb = np.full((P, 3, 3 * NA_COLS), -1e30)
    for kind, b in enumerate((0, 1, LAT // P - 1)):
        for p in range(P):
            qc = b * NA_COLS + p % NA_COLS
            cs = min(max(qc - NA_COLS // 2, 0), GRID_W - NA_COLS)
            kc = (b - 1) * NA_COLS + np.arange(3 * NA_COLS)
            maskb[p, kind, (kc >= cs) & (kc < cs + NA_COLS)] = 0.0
    return {
        "zf": np.concatenate(feats, 1).astype(f), "dec": np.concatenate(decs, 0).astype(f),
        "bmask": bmask.astype(f), "dft": dft.astype(f), "dftp": dftp.astype(f), "maskb": maskb.astype(f),
        "iota": np.tile(np.arange(P, dtype=np.float16), (P, 1)),
        "tid": (np.arange(NT)[None, :] * P + np.arange(P)[:, None]).astype(np.float16),
    }


def kernel(**inp):
    import concourse.bacc as bacc
    from concourse.bass_utils import run_bass_kernel_spmd

    g = {k: np.asarray(v) for k, v in inp.items()}

    def cols(v):
        return v.reshape(-1, P).T
    latent = g["x_sample"][0].reshape(ROWS, CT, NA_COLS, D).transpose(1, 0, 2, 3).reshape(LAT, D)
    taps = np.stack([*g["conv_w"][0], g["conv_b"][0]], 0)
    padded = np.pad(g["rpb"][0], ((0, 0), (0, 0), (NA_COLS, NA_COLS)))
    shifted = np.stack([padded[:, :, NA_COLS - 1 - c:4 * NA_COLS - 1 - c] for c in range(NA_COLS)], 0)
    arrays = {
        "x": np.concatenate([latent, g["x_prompt"][0]], 0),
        "cond": np.stack([cols(g["c"][0]), cols(g["c_ctx"])], 2),
        "ck": g["cache_k"][0, 0].reshape(CTX, CH), "cv": g["cache_v"][0, 0].reshape(CTX, CH),
        "w_ada": g["w_ada"][0], "b2": np.broadcast_to(g["b_ada"], (2, 6 * D)), "w_in": g["w_in"][0],
        "w_out": g["w_out"][0], "w_gate": g["w_gate"][0], "w_up": g["w_up"][0], "w_down": g["w_down"][0],
        "g1c": cols(g["norm1_g"][0]), "g2r": np.broadcast_to(g["norm2_g"], (2, D)), "fg": g["final_g"],
        "cwb": np.stack([taps[:, (c - WX0) * CH:(c - WX0 + 1) * CH].reshape(4, CB, P).transpose(2, 1, 0) for c in HY], 1),
        "chn": np.stack([cols(g["hyena_skip"][0]), cols(g["gnorm_hyena"][0]), cols(g["gnorm_att"][0])], 1),
        "w1": g["filt_w1"][0], "w2": g["filt_w2"][0], "w3": g["filt_w3"][0],
        "mlp_c": np.stack([g["filt_b1"][0], g["filt_b2"][0], g["filt_freq"][0]], 1),
        "rw": np.concatenate([g["router_grp_w"][0], g["router_exp_w"][0]], 1),
        "rb": np.concatenate([g["router_grp_b"][0], g["router_exp_b"][0]], 0),
        "rpb": shifted.reshape(NA_COLS, H, -1),
        **constants(),
    }
    nc = bacc.Bacc("TRN2", target_bir_lowering=False, num_devices=1)
    a, sent = {}, {}
    for name, v in arrays.items():
        v = np.ascontiguousarray(v)
        sent["in_" + name] = v
        a[name] = nc.dram_tensor("in_" + name, v.shape, mybir.dt.from_np(v.dtype), kind="ExternalInput").ap()
    shapes = {"y": (TOK, D), "k": (CTX, CH), "v": (CTX, CH)}
    outs = {n: nc.dram_tensor("out_" + n, s, F32, kind="ExternalOutput").ap() for n, s in shapes.items()}
    program(nc, a, outs)
    r = run_bass_kernel_spmd(nc, [sent], core_ids=[0]).results[0]
    y = r["out_y"]
    ys = y[:LAT].reshape(CT, ROWS, NA_COLS, D).transpose(1, 0, 2, 3).reshape(1, LAT, D)
    kv = (1, 1, CTX, H, DH)
    return y[LAT:].reshape(1, CTX, D), ys, r["out_k"].reshape(kv), r["out_v"].reshape(kv)
```
